# Optimizing a Trainium2 kernel written in Bass

```python
import math
import jax
import jax.numpy as jnp
from jax import lax
import numpy as np

D_MODEL = 2048
BATCH = 1
SEQ = 512
DEPTH = 1
DEC_BATCH = 8
DEC_SEQ = 1
PAST_LEN = 2048
PAGE_SIZE = 128

HEAD_DIM = 128
N_HEADS_A = 8
N_HEADS_B = 8
DK_B = 128
DV_B = 128
WIDTH_A = N_HEADS_A * HEAD_DIM
WIDTH_B = N_HEADS_B * DV_B
MIX_WIDTH = WIDTH_A + WIDTH_B
DILATIONS = ((128, 1), (512, 4), (2048, 16))
MAX_WINDOW = 2048
ROPE_THETA = 500000.0
ROPE_DIM = HEAD_DIM // 4
CONV_WIDTH = 4
CONV_CH = 2 * N_HEADS_B * DK_B + N_HEADS_B * DV_B
CHUNK = 64
EPS = 1e-6
IN_COLS = 4 * WIDTH_A + CONV_CH + WIDTH_B + 2 * N_HEADS_B

kernel_name = 'hybrid_dilated_swa_gated_deltanet_step'

def rmsnorm(x, g):
    xf = x.astype(jnp.float32)
    y = xf * lax.rsqrt(jnp.mean(xf * xf, axis=-1, keepdims=True) + EPS)
    return (y * g.astype(jnp.float32)).astype(x.dtype)

def l2norm(x):
    return x * lax.rsqrt(jnp.sum(x * x, axis=-1, keepdims=True) + EPS)

def partial_rope(x, pos):
    half = ROPE_DIM // 2
    inv = ROPE_THETA ** (-jnp.arange(half, dtype=jnp.float32) / half)
    ang = pos.astype(jnp.float32)[:, None] * inv[None, :]
    cos = jnp.cos(ang)[None, :, None, :]
    sin = jnp.sin(ang)[None, :, None, :]
    xf = x.astype(jnp.float32)
    x1, x2, rest = xf[..., :half], xf[..., half:ROPE_DIM], xf[..., ROPE_DIM:]
    out = jnp.concatenate([x1 * cos - x2 * sin, x2 * cos + x1 * sin, rest], axis=-1)
    return out.astype(x.dtype)

def split_projection(h, w_in):
    p = jnp.einsum('btd,de->bte', h, w_in)
    b, t, _ = p.shape
    cuts = [WIDTH_A, 2 * WIDTH_A, 3 * WIDTH_A, 4 * WIDTH_A, 4 * WIDTH_A + CONV_CH,
            4 * WIDTH_A + CONV_CH + WIDTH_B, 4 * WIDTH_A + CONV_CH + WIDTH_B + N_HEADS_B]
    q_a, k_a, v_a, z_a, qkv_b, z_b, beta_in, a_in = jnp.split(p, cuts, axis=-1)
    heads = lambda u: u.reshape(b, t, N_HEADS_A, HEAD_DIM)
    return heads(q_a), heads(k_a), heads(v_a), z_a, qkv_b, z_b, beta_in, a_in

def dilated_window_prefill(q, k, v, dilation, n_back):
    b, s, h, d = q.shape
    length = s // dilation
    blk = n_back
    nb = -(-length // blk)
    lp = nb * blk

    def split(x):
        x = jnp.swapaxes(x.reshape(b, length, dilation, h, d), 1, 2)
        x = jnp.pad(x, ((0, 0), (0, 0), (0, lp - length), (0, 0), (0, 0)))
        return x.reshape(b, dilation, nb, blk, h, d)

    def with_prev(x):
        prev = jnp.pad(x, ((0, 0), (0, 0), (1, 0), (0, 0), (0, 0), (0, 0)))[:, :, :-1]
        return jnp.concatenate([prev, x], axis=3)

    def merge(x):
        x = x.reshape((b, dilation, lp) + x.shape[4:])[:, :, :length]
        return jnp.swapaxes(x, 1, 2).reshape((b, s) + x.shape[3:])

    qb = split(q)
    kk = with_prev(split(k))
    vv = with_prev(split(v))
    scores = jnp.einsum('brnqhd,brnkhd->brnhqk', qb, kk) * (HEAD_DIM ** -0.5)
    qi = jnp.arange(blk)[:, None]
    kj = jnp.arange(2 * blk)[None, :]
    dist = blk + qi - kj
    band = (dist >= 0) & (dist <= n_back)
    has_prev = jnp.arange(nb)[:, None, None] > 0
    mask = band[None] & (has_prev | (kj[None] >= blk))
    scores = jnp.where(mask[None, None, :, None], scores, -jnp.inf)
    m = jnp.max(scores, axis=-1)
    p = jnp.exp(scores - m[..., None])
    den = jnp.sum(p, axis=-1)
    o = jnp.einsum('brnhqk,brnkhd->brnqhd', p, vv) / jnp.swapaxes(den, -1, -2)[..., None]
    lse = jnp.swapaxes(m + jnp.log(den), -1, -2)
    return merge(o), merge(lse)

def dilated_window_decode(q, k_all, v_all, n_past, dilation, n_back):
    t = q.shape[1]
    idx = n_past + jnp.arange(t)[:, None] - dilation * jnp.arange(n_back + 1)[None, :]
    valid = idx >= 0
    idx = jnp.maximum(idx, 0)
    kg = k_all[:, idx]
    vg = v_all[:, idx]
    scores = jnp.einsum('bthd,btmhd->bthm', q, kg) * (HEAD_DIM ** -0.5)
    scores = jnp.where(valid[None, :, None, :], scores, -jnp.inf)
    m = jnp.max(scores, axis=-1)
    p = jnp.exp(scores - m[..., None])
    den = jnp.sum(p, axis=-1)
    o = jnp.einsum('bthm,btmhd->bthd', p, vg) / den[..., None]
    return o, m + jnp.log(den)

def merge_by_denominator(outs, lses):
    wts = jax.nn.softmax(jnp.stack(lses), axis=0)
    return jnp.sum(wts[..., None] * jnp.stack(outs), axis=0)

def dilated_attention_prompt(q, k, v):
    qf, kf, vf = q.astype(jnp.float32), k.astype(jnp.float32), v.astype(jnp.float32)
    res = [dilated_window_prefill(qf, kf, vf, dil, win // dil) for win, dil in DILATIONS]
    return merge_by_denominator([r[0] for r in res], [r[1] for r in res])

def dilated_attention_sample(q, k_all, v_all, n_past):
    qf, kf, vf = q.astype(jnp.float32), k_all.astype(jnp.float32), v_all.astype(jnp.float32)
    res = [dilated_window_decode(qf, kf, vf, n_past, dil, win // dil) for win, dil in DILATIONS]
    return merge_by_denominator([r[0] for r in res], [r[1] for r in res])

def gated_delta_rule(q, k, v, g, beta, s0):
    b, t, h, _ = q.shape
    n = -(-t // CHUNK)
    tp = n * CHUNK

    def chunks(x):
        x = jnp.pad(x.astype(jnp.float32), [(0, 0), (0, tp - t)] + [(0, 0)] * (x.ndim - 2))
        x = x.reshape((b, n, CHUNK) + x.shape[2:])
        return jnp.moveaxis(x, 3, 1)

    qc = chunks(q) * (DK_B ** -0.5)
    kc, vc, gc, bc = chunks(k), chunks(v), chunks(g), chunks(beta)
    gcum = jnp.cumsum(gc, axis=-1)
    ar = jnp.arange(CHUNK)
    incl = ar[:, None] >= ar[None, :]
    strict = ar[:, None] > ar[None, :]
    decay = jnp.exp(jnp.where(incl, gcum[..., :, None] - gcum[..., None, :], -jnp.inf))
    kbeta = kc * bc[..., None]
    a_mat = jnp.where(strict, jnp.einsum('bhnid,bhnjd->bhnij', kbeta, kc) * decay, 0.0)
    eye = jnp.eye(CHUNK, dtype=jnp.float32)
    t_mat = lax.linalg.triangular_solve(a_mat + eye, jnp.broadcast_to(eye, a_mat.shape),
                                        left_side=True, lower=True)
    u = jnp.einsum('bhnij,bhnje->bhnie', t_mat, vc * bc[..., None])
    w = jnp.einsum('bhnij,bhnjd->bhnid', t_mat, kbeta * jnp.exp(gcum)[..., None])
    qk = jnp.einsum('bhnid,bhnjd->bhnij', qc, kc) * decay
    q_dec = qc * jnp.exp(gcum)[..., None]
    k_dec = kc * jnp.exp(gcum[..., -1:] - gcum)[..., None]
    g_tot = jnp.exp(gcum[..., -1])
    xs = tuple(jnp.moveaxis(a, 2, 0) for a in (q_dec, k_dec, u, w, qk, g_tot))

    def step(state, inp):
        q_i, k_i, u_i, w_i, qk_i, gt_i = inp
        v_new = u_i - jnp.einsum('bhcd,bhde->bhce', w_i, state)
        o_i = jnp.einsum('bhcd,bhde->bhce', q_i, state) + jnp.einsum('bhcj,bhje->bhce', qk_i, v_new)
        state = state * gt_i[..., None, None] + jnp.einsum('bhcd,bhce->bhde', k_i, v_new)
        return state, o_i

    s_fin, o = lax.scan(step, s0.astype(jnp.float32), xs)
    o = jnp.moveaxis(jnp.moveaxis(o, 0, 2), 1, 3).reshape(b, tp, h, DV_B)[:, :t]
    return o, s_fin

def deltanet_branch(qkv_in, conv_buf, s0, beta_in, a_in, conv_w, a_log, dt_bias, onorm_w):
    b, t, _ = qkv_in.shape
    ext = jnp.concatenate([conv_buf.astype(qkv_in.dtype), qkv_in], axis=1)
    extf = ext.astype(jnp.float32)
    wf = conv_w.astype(jnp.float32)
    conv = extf[:, 0:t] * wf[0]
    for i in range(1, CONV_WIDTH):
        conv = conv + extf[:, i:i + t] * wf[i]
    c = jax.nn.silu(conv)
    q_b, k_b, v_b = jnp.split(c, [N_HEADS_B * DK_B, 2 * N_HEADS_B * DK_B], axis=-1)
    q_b = l2norm(q_b.reshape(b, t, N_HEADS_B, DK_B))
    k_b = l2norm(k_b.reshape(b, t, N_HEADS_B, DK_B))
    v_b = v_b.reshape(b, t, N_HEADS_B, DV_B)
    beta = jax.nn.sigmoid(beta_in.astype(jnp.float32))
    g = -jnp.exp(a_log.astype(jnp.float32)) * jax.nn.softplus(
        a_in.astype(jnp.float32) + dt_bias.astype(jnp.float32))
    o, s_new = gated_delta_rule(q_b, k_b, v_b, g, beta, s0)
    o = o * lax.rsqrt(jnp.mean(o * o, axis=-1, keepdims=True) + EPS) * onorm_w.astype(jnp.float32)
    return o, ext[:, -(CONV_WIDTH - 1):], s_new

def output_sublayer(x, o_a, z_a, o_b, z_b, w_out, g_post):
    b, t, _ = x.shape
    gated = jnp.concatenate([o_a.reshape(b, t, WIDTH_A) * jax.nn.silu(z_a.astype(jnp.float32)),
                             o_b.reshape(b, t, WIDTH_B) * jax.nn.silu(z_b.astype(jnp.float32))],
                            axis=-1).astype(x.dtype)
    y = jnp.einsum('bte,ed->btd', gated, w_out)
    return x + rmsnorm(y, g_post)

def setup_inputs(seed: int = 0) -> dict:
    key = jax.random.key(seed)
    ks = jax.random.split(key, 14)
    win_buf = min(MAX_WINDOW, PAST_LEN)
    f32 = jnp.float32
    dt = jnp.exp(jax.random.uniform(ks[10], (DEPTH, N_HEADS_B), f32, math.log(1e-3), math.log(1e-1)))
    return {
        'x_prompt': jax.random.normal(ks[0], (BATCH, SEQ, D_MODEL), f32),
        'x_sample': jax.random.normal(ks[1], (DEC_BATCH, DEC_SEQ, D_MODEL), f32),
        'cache_win_k': jax.random.normal(ks[2], (DEPTH, DEC_BATCH, win_buf, N_HEADS_A, HEAD_DIM), f32),
        'cache_win_v': jax.random.normal(ks[3], (DEPTH, DEC_BATCH, win_buf, N_HEADS_A, HEAD_DIM), f32),
        'state_conv': jax.random.normal(ks[4], (DEPTH, DEC_BATCH, CONV_WIDTH - 1, CONV_CH), f32),
        'state_delta': 0.1 * jax.random.normal(ks[5], (DEPTH, DEC_BATCH, N_HEADS_B, DK_B, DV_B), f32),
        'g_pre': 1.0 + 0.02 * jax.random.normal(ks[6], (DEPTH, D_MODEL), f32),
        'w_in': jax.random.normal(ks[7], (DEPTH, D_MODEL, IN_COLS), f32) * D_MODEL ** -0.5,
        'conv_w': jax.random.normal(ks[8], (DEPTH, CONV_WIDTH, CONV_CH), f32) * CONV_WIDTH ** -0.5,
        'a_log': jnp.log(jax.random.uniform(ks[9], (DEPTH, N_HEADS_B), f32, 1.0, 16.0)),
        'dt_bias': dt + jnp.log(-jnp.expm1(-dt)),
        'onorm_w': 1.0 + 0.02 * jax.random.normal(ks[11], (DEPTH, DV_B), f32),
        'w_out': jax.random.normal(ks[12], (DEPTH, MIX_WIDTH, D_MODEL), f32) * MIX_WIDTH ** -0.5,
        'g_post': 1.0 + 0.02 * jax.random.normal(ks[13], (DEPTH, D_MODEL), f32),
    }

def reference(x_prompt, x_sample, cache_win_k, cache_win_v, state_conv, state_delta,
              g_pre, w_in, conv_w, a_log, dt_bias, onorm_w, w_out, g_post):
    b, s, _ = x_prompt.shape
    db, t, _ = x_sample.shape
    keep = min(MAX_WINDOW, s)
    n_past = cache_win_k.shape[2]
    pos_p = jnp.arange(s, dtype=jnp.int32)
    pos_s = PAST_LEN + jnp.arange(t, dtype=jnp.int32)
    yp, ys = x_prompt, x_sample
    wk_p, wv_p, cv_p, st_p = [], [], [], []
    wk_s, wv_s, cv_s, st_s = [], [], [], []
    for l in range(DEPTH):
        q_a, k_a, v_a, z_a, qkv_b, z_b, beta_in, a_in = split_projection(rmsnorm(yp, g_pre[l]), w_in[l])
        q_a, k_a = partial_rope(q_a, pos_p), partial_rope(k_a, pos_p)
        o_a = dilated_attention_prompt(q_a, k_a, v_a)
        conv0 = jnp.zeros((b, CONV_WIDTH - 1, CONV_CH), qkv_b.dtype)
        s0 = jnp.zeros((b, N_HEADS_B, DK_B, DV_B), jnp.float32)
        o_b, conv_new, s_new = deltanet_branch(qkv_b, conv0, s0, beta_in, a_in, conv_w[l],
                                               a_log[l], dt_bias[l], onorm_w[l])
        yp = output_sublayer(yp, o_a, z_a, o_b, z_b, w_out[l], g_post[l])
        wk_p.append(k_a[:, s - keep:])
        wv_p.append(v_a[:, s - keep:])
        cv_p.append(conv_new)
        st_p.append(s_new)

        q_a, k_a, v_a, z_a, qkv_b, z_b, beta_in, a_in = split_projection(rmsnorm(ys, g_pre[l]), w_in[l])
        q_a, k_a = partial_rope(q_a, pos_s), partial_rope(k_a, pos_s)
        k_all = jnp.concatenate([cache_win_k[l].astype(k_a.dtype), k_a], axis=1)
        v_all = jnp.concatenate([cache_win_v[l].astype(v_a.dtype), v_a], axis=1)
        o_a = dilated_attention_sample(q_a, k_all, v_all, n_past)
        o_b, conv_new, s_new = deltanet_branch(qkv_b, state_conv[l], state_delta[l], beta_in, a_in,
                                               conv_w[l], a_log[l], dt_bias[l], onorm_w[l])
        ys = output_sublayer(ys, o_a, z_a, o_b, z_b, w_out[l], g_post[l])
        wk_s.append(k_a)
        wv_s.append(v_a)
        cv_s.append(conv_new)
        st_s.append(s_new)
    return (yp, ys, jnp.stack(wk_p), jnp.stack(wv_p), jnp.stack(cv_p), jnp.stack(st_p),
            jnp.stack(wk_s), jnp.stack(wv_s), jnp.stack(cv_s), jnp.stack(st_s))


_drawn_inputs = setup_inputs


def setup_inputs(seed=0):
    import zlib

    import numpy as np

    out = dict(_drawn_inputs(seed))
    spreads = {}
    factors = {}
    for name, (base, spread) in spreads.items():
        noise = np.random.default_rng([zlib.crc32(name.encode()), seed]).standard_normal(out[name].shape)
        drawn = base * np.exp(spread * noise) if base else spread * noise
        out[name] = jnp.asarray(drawn.astype(out[name].dtype))
    for name, factor in factors.items():
        out[name] = (out[name] * factor).astype(out[name].dtype)
    return out
```

```python
from contextlib import ExitStack
import numpy as np
import concourse.bass as bass
from concourse import mybir

F32 = mybir.dt.float32
F32R = mybir.dt.float32r
ALU = mybir.AluOpType
ACT = mybir.ActivationFunctionType
AX = mybir.AxisListType

P = 128
D = 2048
TP = 512
NB = 8
TT = TP + NB
HALF = TT // 2
KT = D // P
NQ = 4
NH = 8
HD = 128
NC = TP // P
WA = NH * HD
CONV_CH = 3 * WA
CW = 4
PAST = 2048
ROT = 32
EPS = 1e-6
SCALE = HD ** -0.5
LEVELS = 7
NEG = -1.0e30
SEGS = 8
T_A, T_B, T_O = 1, 1 + 4 * NH, 1 + 8 * NH


def tables():
    f = np.float32
    i = np.arange(P)
    t = {"c_ident": np.eye(P, dtype=f), "c_upper": (i[:, None] <= i[None, :]).astype(f)}
    lev = np.zeros((P, LEVELS, P), mybir.dt.np(mybir.dt.bfloat16))
    for n in range(LEVELS):
        s = 1 << n
        same = i[:, None] // (2 * s) == i[None, :] // (2 * s)
        lev[:, n] = same & ((i[:, None] // s) % 2 == 0) & ((i[None, :] // s) % 2 == 1)
    t["c_levels"] = lev
    kk = np.arange(TP)
    dist = P * (NC - 1 - kk // P)[None, :] + i[:, None] - (kk % P)[None, :]
    cnt = sum(((dist >= 0) & (dist <= w) & (dist % d == 0)).astype(int) for w, d in ((128, 1), (512, 4), (2048, 16)))
    t["c_lnmask"] = np.where(cnt > 0, np.log(np.maximum(cnt, 1)), NEG).astype(f)
    half = ROT // 2
    inv = f(500000.0) ** (-np.arange(half, dtype=f) / f(half))
    pos = np.concatenate([np.arange(TP), np.full(NB, PAST)]).astype(f)
    ang = (pos[:, None] * inv[None, :]).astype(f).T.astype(np.float64)
    t["c_rope"] = np.stack([np.tile(np.cos(ang), (2, 1)), np.tile(np.sin(ang), (2, 1))], 1).astype(f)
    rot = np.zeros((ROT, 2 * ROT), f)
    for m in range(half):
        rot[m + half, m] = -1.0
        rot[m, m + half] = 1.0
    t["c_rot"] = rot
    return t


class Chain:

    def __init__(self, eng, sem):
        self.eng, self.sem, self.base, self.off, self.n, self.per = eng, sem, 0, 0, 0, 0

    def at(self, h, first, per):
        self.off, self.n, self.per = (h - first) * per, 0, per

    def end(self, iterations):
        assert iterations == 1 or self.n == self.per, (self.n, self.per)
        self.base, self.off, self.n = self.base + iterations * self.n, 0, 0

    def link(self, ins):
        self.n += 1
        ins.then_inc(self.sem, 1)
        self.eng.wait_ge(self.sem, self.off + (self.base + self.n))


def idle(n):
    for _ in range(n):
        yield


def build(nc, x_prompt, x_sample, cache_k, cache_v, state_conv, state_delta, g_pre, w_in, conv_w, a_log, dt_bias,
          onorm_w, w_out, g_post, c_ident, c_upper, c_levels, c_lnmask, c_rope, c_rot,
          y_p, y_s, wk_p, wv_p, cv_p, st_p, wk_s, wv_s, cv_s, st_s):
    w_in_v = w_in[0].rearrange("(kt p) c -> p kt c", p=P)
    w_out_v = w_out[0].rearrange("(kt p) c -> p kt c", p=P)
    kp_v = wk_p[0, 0].rearrange("(c p) h d -> p c h d", p=P)
    vp_v = wv_p[0, 0].rearrange("(c p) h d -> p c h d", p=P)
    scratch_q = nc.dram_tensor("scratch_q", (NB, WA), F32, kind="Internal").ap()

    with ExitStack() as ctx:
        def sb(name, shape, dt=F32):
            return ctx.enter_context(nc.sbuf_tensor(name, shape, dt))

        def sem(name):
            return ctx.enter_context(nc.semaphore(name))

        h_hi = sb("h_hi", [P, KT, TT], F32R)
        h_lo = sb("h_lo", [P, KT, TT], F32R)
        w_raw = sb("w_raw", [P, NQ, 4, P])
        w_hi = sb("w_hi", [P, 2, KT, P], F32R)
        w_lo = sb("w_lo", [P, 2, KT, P], F32R)
        gated = sb("gated", [P, KT, TT])
        xin = gated[:].rearrange("p a b -> p (a b)")[:, 0:NC * D].rearrange("p (c d) -> p c d", d=D)
        ident = sb("ident", [P, P])
        upper = sb("upper", [P, P])
        ones = sb("ones", [P, P])
        levels = sb("levels", [P, LEVELS, P], mybir.dt.bfloat16)
        arena = sb("arena", [P, 4096 + 2 * TT])
        lnmask = arena[:, 0:TP]
        probs = arena[:, TP:TP + 10 * P]
        probT = arena[:, TP + 10 * P:TP + 20 * P]
        ktok = arena[:, TP + 20 * P:TP + 24 * P].rearrange("p (c d) -> p c d", c=NC)
        vtok = arena[:, TP + 24 * P:TP + 28 * P].rearrange("p (c d) -> p c d", c=NC)
        rope = arena[0:ROT, 4096:4096 + 2 * TT].rearrange("p (a t) -> p a t", a=2)
        b_kb, b_kbT, b_kdec, b_vb, b_D, b_QK, b_U, b_T, b_Y, b_B0 = [
            arena[:, n * TP:(n + 1) * TP].rearrange("p (c d) -> p c d", c=NC) for n in range(10)]
        b_A = b_kb
        b_B = (b_B0, b_D)
        b_o = b_T
        xq = sb("xq", [P, 3 + TT])
        xk = sb("xk", [P, TT])
        xv = sb("xv", [P, TT])
        xz = sb("xz", [P, TT])
        cq = sb("cq", [P, TT])
        acc = sb("acc", [P, TT])
        ez = sb("ez", [P, TT])
        sz = sb("sz", [P, TT])
        small = sb("small", [P, 4 * P])
        S = small[:, 0:P]
        rr = small[:, P:2 * P]
        vn = small[:, 2 * P:3 * P]
        o1 = small[:, 3 * P:4 * P]
        gw = small[:, 0:160].rearrange("p (a c h) -> p a c h", a=4, c=NC + 1)
        gt = small[:, 160:240].rearrange("p (c a h) -> p c a h", a=2, c=NC + 1)
        kv = sb("kv", [P, 2, WA])
        S0 = sb("S0", [P, NB, P])
        rb = sb("rb", [11, 10 * P])
        rows = rb[:, 0:P]
        vexp = rb[0:NB, P:5 * P].rearrange("p (b e) -> p b e", e=P)
        pd = rb[0:NH, 5 * P:8 * P].rearrange("p (n t) -> p n t", n=3)
        kvr = rb[0:NB, 8 * P:10 * P].rearrange("p (n t) -> p n t", n=2)
        qkrow = rb[0:NB, 5 * P:7 * P].rearrange("p (n t) -> p n t", n=2)
        vrow = rb[0:NB, 7 * P:8 * P]
        dgs = rb[0:NB, 8 * P:9 * P].rearrange("p (a h b) -> p a h b", a=2, h=NH)
        stT = sb("stT", [P, 3 * NH, 28])
        cw = sb("cw", [P, 3, 28])
        vecT = sb("vecT", [P, 33])
        ssum = sb("ssum", [P, 8])
        rstd = sb("rstd", [P, 8])
        adt = sb("adt", [P, 2, NH])
        G6 = sb("G6", [P, 6, NC, NH])
        hg = sb("hg", [P, 6, NC])
        gneg = sb("gneg", [P, NH])
        bgs = sb("bgs", [P, 2, NH, NB])
        sk = sb("sk", [P, 4, NC])
        oq = sb("oq", [P, NC])
        on = sb("on", [P, 2, NC])
        stat = sb("stat", [P, 3, NC])
        qS = sb("qS", [P, NH, NB])
        kS = sb("kS", [P, NH, NB])
        vS = sb("vS", [P, NH, NB])
        zS = sb("zS", [P, NH, NB])
        qks = sb("qks", [P, NH, NB])
        snew = sb("snew", [NH, NB])
        sc = sb("sc", [P, 3, NH])
        ds = sb("ds", [NH, 8])
        dg = sb("dg", [NH, NH])
        pT = sb("pT", [P, 4, NH])
        da = sb("da", [P, NH])
        dd = sb("dd", [P, 13, NB])
        fin = sb("fin", [P, 8])
        rotm = sb("rotm", [ROT, 2 * ROT])
        s_in = xz[:, 0:P]
        xba = cq[0:16, :]
        scin = arena[0:28, 0:CONV_CH]
        xs_in = kv[0:NB].rearrange("p a b -> p (a b)")
        junk = arena[:, CONV_CH:CONV_CH + D]
        xres = [arena[:, 0:D], arena[:, D:2 * D]]
        qb = sb("qb", [P, WA])
        K_TILE, V_TILE = (kv[:, 0], kv[:, 1], kv[:, 0]), (kv[:, 1], kv[:, 0], qb[:])

        PJ = ctx.enter_context(nc.psum_tensor("PJ", [P, 2, TP], F32))
        MX = ctx.enter_context(nc.psum_tensor("MX", [P, 4, TP], F32))
        MD = ctx.enter_context(nc.psum_tensor("MD", [P, 2, TP], F32))

        def mx(n):
            return MX[:, n].rearrange("p (c d) -> p c d", c=NC)

        NAMES = """c_in x_in s_loaded adt_in x_sq x_scaled hT_ps hT_hi hT_lo vec_ps vec_sb st_ps st_sb consts w_hi_ok w_lo_dve
        w_lo_pool w_used proj_ps proj_sb        
           q_rot q_ok k_rot k_ok k_T ktok_ok k_out v_T vtok_ok v_out row_out qrow_out
        scores negmax expd probs_ok probT_ps probT_ok attn_ps z_exp z_ok gated_a stash_q stash_k stash_v stash_z
        act_chain dve_chain cw_ok crow_ps crow_ok crow_out conv_ok conv_exp kv_silu q_silu sq_ok mix_T1 mix_ss
        mix_scal mix_gb mix_gr mix_tok mix_kbT_ps mix_kbT mix_arg mix_D mix_W mix_kk mix_qk mix_A mix_QK mix_B
        mix_U0 mix_T_ps mix_T mix_Y_ps mix_Y mix_Z mix_UT ch_kS ch_r ch_v_ps ch_v ch_S_ps ch_o_ps ch_S ch_o1 ch_o
        o_sq o_n o_T gated_b z_exp_b z_ok_b S_out hg_ok snew_ps snew_ok qkp qb_in kb0_in kb1_in kb2_in prod red sc_T
        sc_max p_exp p_norm p_T pT_ok vb0_in vb1_in vb2_in pv_ps gated_ad dkq d_sum d_vec d_rows d_rows_ok d_vexp
        d_outer d_add S0_in S0_scaled S0_out gated_bd g_hi g_lo sq_y ss_y y_T xr_in0 xr_in1 y_out_ok y_out memset_ok
        ssum_set zero_cols gates_pe gates_act gates_dve rstd_ok mix_rs on_rs d_rs d_rs2 fin_rs"""
        s = {n: sem(n) for n in NAMES.split()}
        raw_in = [sem(f"w_raw_in{q}") for q in range(NQ)]

        def lo_sem(q):
            return s["w_lo_dve"] if q % 2 == 0 else s["w_lo_pool"]

        block = ctx.enter_context(nc.Block())

        @block.sync
        def _(sp):
            def wait_lo(T, q):
                sp.wait_ge(lo_sem(q), 2 * T + q // 2 + 1)

            def load_w(view, c0, T, q, n=P):
                sp.dma_start(w_raw[:, q, :, 0:n], view[:, 4 * q:4 * q + 4, bass.ds(c0, n)]).then_inc(raw_in[q], 16)

            for c in range(NC):
                sp.dma_start(xin[:, c, :], x_prompt[0, c * P:(c + 1) * P, :]).then_inc(s["x_in"], 16)
            sp.dma_start(xs_in, x_sample.rearrange("b t d -> (b t) d")).then_inc(s["x_in"], 16)
            sp.dma_start(ident[:], c_ident).then_inc(s["c_in"], 16)
            sp.dma_start(s_in[0:16], g_pre.rearrange("o (a p) -> (o a) p", p=P)).then_inc(s["c_in"], 16)
            sp.dma_start(s_in[16:32], g_post.rearrange("o (a p) -> (o a) p", p=P)).then_inc(s["c_in"], 16)
            sp.dma_start(s_in[32:33], onorm_w).then_inc(s["c_in"], 16)
            sp.dma_start(scin[0:24], state_conv[0].rearrange("b i c -> (b i) c")).then_inc(s["c_in"], 16)
            sp.dma_start(scin[24:28], conv_w[0]).then_inc(s["c_in"], 16)
            for q in range(NQ):
                load_w(w_in_v, 8 * WA, 0, q, 16)
            sp.dma_start(upper[:], c_upper).then_inc(s["consts"], 16)
            sp.dma_start(levels[:], c_levels).then_inc(s["consts"], 16)
            sp.dma_start(rotm[:], c_rot).then_inc(s["consts"], 16)
            sp.dma_start(adt[:, 0], a_log[0].partition_broadcast(P)).then_inc(s["adt_in"], 16)
            sp.dma_start(adt[:, 1], dt_bias[0].partition_broadcast(P)).then_inc(s["adt_in"], 16)
            sp.dma_start(cv_s[0, :, 0:2, :], state_conv[0, :, 1:3, :]).then_inc(s["S_out"], 16)
            for q in range(NQ):
                wait_lo(0, q)
                load_w(w_in_v, 0, 1, q)
            sp.wait_ge(s["st_ps"], 24)
            sp.dma_start(lnmask, c_lnmask).then_inc(s["s_loaded"], 16)
            sp.dma_start(rope, c_rope).then_inc(s["s_loaded"], 16)

            def head_loads(h, T, nxt, work):
                for j in range(4):
                    for seg in range(SEGS):
                        if seg % 2 == 0 and nxt[j] is not None:
                            q = seg // 2
                            view, c0 = nxt[j]
                            wait_lo(T + j + 1, q)
                            load_w(view, c0, T + j + 2, q)
                        for g in work:
                            next(g, None)

            def cache_block(view, n):
                return (view[PAST - 128:PAST], view[PAST - 512:PAST:4], view[0:PAST:16])[n].rearrange(
                    "t h d -> t (h d)")

            def decode(b):
                vc = cache_v[0, b]
                yield from idle(8)
                sp.wait_ge(s["red"], 3 * b + 1)
                sp.dma_start(K_TILE[2], cache_block(cache_k[0, b], 2)).then_inc(s["kb2_in"], 16)
                yield from idle(2)
                sp.wait_ge(s["red"], 3 * b + 2)
                sp.dma_start(V_TILE[0], cache_block(vc, 0)).then_inc(s["vb0_in"], 16)
                yield
                sp.wait_ge(s["d_add"], 2 * b + 2)
                sp.dma_start(st_s[0, :, b].rearrange("b d e -> d b e"), S0[:]).then_inc(s["S0_out"], 16)
                yield from idle(2)
                sp.wait_ge(s["red"], 3 * b + 3)
                for n in (1, 2):
                    sp.dma_start(V_TILE[n], cache_block(vc, n)).then_inc(s[f"vb{n}_in"], 16)

            def prefetch(b):
                yield from idle(23)
                sp.wait_ge(s["qrow_out"], 16 * NH)
                if not isinstance(b, int) or b > 0:
                    sp.wait_ge(s["pv_ps"], b)
                    sp.wait_ge(s["S0_out"], 16 * b)
                kc = cache_k[0, b]
                sp.dma_start(qb[:], scratch_q[b].partition_broadcast(P)).then_inc(s["qb_in"], 16)
                for n in range(2):
                    sp.dma_start(K_TILE[n], cache_block(kc, n)).then_inc(s[f"kb{n}_in"], 16)
                sp.dma_start(S0[:], state_delta[0, :, b].rearrange("b d e -> d b e")).then_inc(s["S0_in"], 16)

            def mix_b(h):
                yield from idle(31)
                sp.wait_ge(s["ch_S"], 4 * h + 4)
                sp.dma_start(st_p[0, 0, h], S).then_inc(s["S_out"], 16)

            def loads_a(h, last=False):
                a = [(w_in_v, 2 * WA + h * HD), (w_in_v, 3 * WA + h * HD)]
                b = [(w_in_v, 5 * WA), (w_in_v, 6 * WA)] if last else \
                    [(w_in_v, (h + 1) * HD), (w_in_v, WA + (h + 1) * HD)]
                return a + b

            def loads_b(h, last=False):
                a = [(w_in_v, 4 * WA + h * HD), (w_in_v, 7 * WA + h * HD)]
                b = [(w_out_v, 0), (w_out_v, P)] if last else \
                    [(w_in_v, 5 * WA + (h + 1) * HD), (w_in_v, 6 * WA + (h + 1) * HD)]
                return a + b

            for q in range(NQ):
                wait_lo(1, q)
                load_w(w_in_v, WA, 2, q)
            with sp.Fori(0, NH - 1) as h:
                head_loads(h, 4 * h + T_A, loads_a(h), [])
            head_loads(NH - 1, T_A + 4 * (NH - 1), loads_a(NH - 1, True), [])
            head_loads(0, T_B, loads_b(0), [prefetch(0)])
            with sp.Fori(1, NH - 1) as h:
                head_loads(h, 4 * h + T_B, loads_b(h), [mix_b(h - 1), decode(h - 1), prefetch(h)])
            h = NH - 1
            head_loads(h, 4 * h + T_B, loads_b(h, True), [mix_b(h - 1), decode(h - 1), prefetch(h)])
            gens = [mix_b(h), decode(h)]
            for _ in range(40):
                for g in gens:
                    next(g, None)
            with sp.Fori(0, KT - 2) as j:
                for q in range(NQ):
                    wait_lo(j + (T_O + 1), q)
                    load_w(w_out_v, (j + 2) * P, j, q)
            sp.wait_ge(s["gated_b"], NH)
            for c in range(NC + 1):
                if c >= 2:
                    sp.wait_ge(s["y_out"], 16 * (c - 1))
                if c < NC:
                    sp.dma_start(xres[c % 2], x_prompt[0, c * P:(c + 1) * P, :]).then_inc(s[f"xr_in{c % 2}"], 16)
                else:
                    sp.dma_start(xres[c % 2][0:NB], x_sample.rearrange("b t d -> (b t) d")).then_inc(s[f"xr_in{c % 2}"], 16)
                if c >= 1:
                    sp.wait_ge(s["y_out_ok"], 4 * c)
                    sp.dma_start(y_p[0, (c - 1) * P:c * P, :], xres[(c - 1) % 2]).then_inc(s["y_out"], 16)
            sp.wait_ge(s["y_out_ok"], 4 * (NC + 1))
            sp.dma_start(y_s.rearrange("b t d -> (b t) d"), xres[NC % 2][0:NB]).then_inc(s["y_out"], 16)
            sp.wait_ge(s["y_out"], 16 * (NC + 1))
            sp.wait_ge(s["k_out"], 16 * NH)
            sp.wait_ge(s["row_out"], 16 * NH)
            sp.wait_ge(s["v_out"], 32 * NH)
            sp.wait_ge(s["crow_out"], 32 * 3 * NH)
            sp.wait_ge(s["S_out"], 16 * (NH + 1))
            sp.wait_ge(s["S0_out"], 16 * NH)

        @block.tensor
        def _(pe):
            def segment(T, par, half, q, first=False):
                if half == 0:
                    pe.wait_ge(lo_sem(q), 2 * T + q // 2 + 1)
                if q == 0 and not first:
                    pe.wait_ge(s["proj_sb"], 2 * T - 1 + half)
                tok = slice(half * HALF, (half + 1) * HALF)
                out = PJ[:, half, 0:HALF]
                for k in range(4 * q, 4 * q + 4):
                    wh, wl = w_hi[:, par, k, :], w_lo[:, par, k, :]
                    pe.matmul(out, wh, h_hi[:, k, tok], start=k == 0, stop=False)
                    pe.matmul(out, wh, h_lo[:, k, tok], start=False, stop=False)
                    last = pe.matmul(out, wl, h_hi[:, k, tok], start=False, stop=k == KT - 1)
                if q == NQ - 1:
                    last.then_inc(s["proj_ps"], 1)
                elif half == 1:
                    last.then_inc(s["w_used"], 1)

            def project(T, par, work, first=False):
                for half in range(2):
                    for q in range(NQ):
                        segment(T, par, half, q, first)
                        for g in work:
                            next(g, None)

            pe.wait_ge(s["c_in"], 96)
            pe.transpose(MD[:, 0, 0:33], s_in[0:33], ident[0:33, 0:33]).then_inc(s["vec_ps"], 1)
            for m in range(3 * NH):
                bank, o = m // 12, (m % 12) * 28
                pe.transpose(MX[:, 2 + bank, o:o + 28], scin[:, m * P:(m + 1) * P], ident[0:28, 0:28]).then_inc(
                    s["st_ps"], 1)
            pe.wait_ge(s["x_scaled"], NC + 1)
            for k in range(KT):
                pe.transpose(MD[:, 1, k * NB:(k + 1) * NB], xs_in[:, k * P:(k + 1) * P], ident[0:NB, 0:NB]).then_inc(
                    s["hT_ps"], 1)
            for k in range(KT):
                if k == 2:
                    pe.wait_ge(s["st_sb"], 2)
                if k >= 4:
                    pe.wait_ge(s["hT_lo"], k - 4 + 2)
                for c in range(NC):
                    last = pe.transpose(MX[:, k % 4, c * P:(c + 1) * P], xin[:, c, k * P:(k + 1) * P], ident[:])
                last.then_inc(s["hT_ps"], 1)
            pe.wait_ge(s["hT_lo"], KT + 1)

            def gates():
                yield from idle(8)
                pe.wait_ge(s["proj_sb"], 2)
                for c in range(NC):
                    pe.transpose(MD[:, 0, c * 16:(c + 1) * 16], xba[:, c * P:(c + 1) * P], ident[0:16, 0:16])
                pe.transpose(MD[0:NB, 0, 64:80], xba[:, TP:TT], ident[0:16, 0:16]).then_inc(s["gates_pe"], 1)
                yield from idle(5)
                pe.wait_ge(s["gates_dve"], 2)
                g = gw[:, 3, 0:NC, :].rearrange("p c h -> p (c h)")
                pe.matmul(MD[:, 1, 0:32], upper[:], g, start=True, stop=True)
                pe.matmul(MD[:, 1, 32:64], ones[:], g, start=True, stop=True).then_inc(s["gates_pe"], 1)
                yield from idle(3)
                pe.wait_ge(s["gates_dve"], 5)
                pe.matmul(MD[:, 0, 0:P], ones[0:NB, :], dgs.rearrange("p a h b -> p (a h b)"), start=True,
                          stop=True).then_inc(s["gates_pe"], 1)

            def own_a(h):
                yield from idle(9)
                pe.wait_ge(s["proj_sb"], 8 * h + 4)
                if not isinstance(h, int) or h > 0:
                    pe.wait_ge(s["gated_a"], h)
                for half in range(2):
                    last = pe.matmul(MX[0:2 * ROT, half, 0:HALF], rotm[:], xq[0:ROT, half * HALF:(half + 1) * HALF],
                                     start=True, stop=True)
                last.then_inc(s["q_rot"], 1)
                yield from idle(8)
                pe.wait_ge(s["proj_sb"], 8 * h + 6)
                pe.wait_ge(s["q_ok"], h + 1)
                for half in range(2):
                    last = pe.matmul(MX[0:2 * ROT, half, 0:HALF], rotm[:], xk[0:ROT, half * HALF:(half + 1) * HALF],
                                     start=True, stop=True)
                last.then_inc(s["k_rot"], 1)
                yield from idle(2)
                pe.wait_ge(s["k_ok"], h + 1)
                for c in range(NC):
                    pe.transpose(MX[:, 2, c * P:(c + 1) * P], xk[:, c * P:(c + 1) * P], ident[:])
                pe.transpose(MX[0:NB, 3, 0:P], xq[:, TP:TT], ident[:])
                pe.transpose(MX[0:NB, 3, P:2 * P], xk[:, TP:TT], ident[:]).then_inc(s["k_T"], 1)
                yield from idle(6)
                pe.wait_ge(s["proj_sb"], 8 * h + 8)
                pe.wait_ge(s["ktok_ok"], 2 * h + 2)
                for c in range(NC):
                    pe.transpose(MX[:, 2, c * P:(c + 1) * P], xv[:, c * P:(c + 1) * P], ident[:])
                pe.transpose(MX[0:NB, 3, 0:P], xv[:, TP:TT], ident[:]).then_inc(s["v_T"], 1)
                for i in range(NC):
                    if i != 1:
                        yield
                    if i == 2:
                        pe.wait_ge(s["vtok_ok"], 2 * h + 2)
                    pe.matmul(MX[:, i, 0:(i + 1) * P], xq[:, i * P:(i + 1) * P], xk[:, 0:(i + 1) * P], start=True,
                              stop=True).then_inc(s["scores"], 1)

            OFF = [0, 1, 3, 6]

            def tail_a(h):
                yield
                pe.wait_ge(s["probs_ok"], 4 * h + 4)
                for kt in range(NC):
                    bank, col = (kt, 0) if kt < 3 else (2, 2 * P)
                    for i in range(kt, NC):
                        o = (i * (i + 1) // 2 + kt) * P
                        last = pe.transpose(MX[:, bank, col + (i - kt) * P:col + (i - kt + 1) * P], probs[:, o:o + P],
                                            ident[:])
                    if kt != 2:
                        last.then_inc(s["probT_ps"], 1)
                        yield
                for kt in range(NC):
                    if kt < 3:
                        pe.wait_ge(s["probT_ok"], 3 * h + kt + 1)
                    o = sum(NC - n for n in range(kt)) * P
                    last = pe.matmul(MX[:, 3, kt * P:TP], vtok[:, kt, :], probT[:, o:o + (NC - kt) * P],
                                     start=kt == 0, stop=kt == NC - 1)
                    if kt == 1:
                        yield
                last.then_inc(s["attn_ps"], 1)

            def own_b(h):
                for j in range(3):
                    yield from idle(10 if j == 0 else 8)
                    pe.wait_ge(s["proj_sb"], 8 * h + (2 * T_B + 2 * (j + 1)))
                    if j == 0 and (not isinstance(h, int) or h > 0):
                        pe.wait_ge(s["d_add"], 2 * h)
                        pe.wait_ge(s["crow_ok"], 3 * h)
                    elif j > 0:
                        pe.wait_ge(s["crow_ok"], 3 * h + j)
                    pe.transpose(MD[0:11, 1, 0:P], xq[:, 3 + TP - 3:3 + TT], ident[:]).then_inc(s["crow_ps"], 1)

            def mix_b(h):
                chunks = range(NC)
                yield
                pe.wait_ge(s["q_silu"], h + 1)
                pe.wait_ge(s["kv_silu"], 2 * h + 2)
                for c in chunks:
                    pe.transpose(mx(0)[:, c, :], xk[:, c * P:(c + 1) * P], ident[:])
                for c in chunks:
                    last = pe.transpose(mx(1)[:, c, :], xv[:, c * P:(c + 1) * P], ident[:])
                last.then_inc(s["mix_T1"], 1)
                yield
                pe.wait_ge(s["sq_ok"], 2 * h + 2)
                for n, sq in enumerate((b_o, b_Y)):
                    for c in chunks:
                        last = pe.matmul(MX[:, 2, n * NC + c:n * NC + c + 1], sq[:, c, :], ones[:, 0:1], start=True,
                                         stop=True)
                last.then_inc(s["mix_ss"], 1)
                pe.wait_ge(s["mix_gr"], h + 1)
                pe.matmul(MX[:, 3, :], ones[:], b_B0.rearrange("p c d -> p (c d)"), start=True, stop=True).then_inc(
                    s["mix_gb"], 1)
                yield from idle(2)
                pe.wait_ge(s["mix_tok"], 3 * h + 3)
                for c in chunks:
                    last = pe.transpose(mx(0)[:, c, :], b_kb[:, c, :], ident[:])
                last.then_inc(s["mix_kbT_ps"], 1)
                yield
                pe.wait_ge(s["mix_kbT"], h + 1)
                for c in chunks:
                    last = pe.matmul(mx(1)[:, c, :], xk[:, c * P:(c + 1) * P], b_kbT[:, c, :], start=True, stop=True)
                last.then_inc(s["mix_kk"], 1)
                for c in chunks:
                    last = pe.matmul(mx(2)[:, c, :], xk[:, c * P:(c + 1) * P], cq[:, c * P:(c + 1) * P], start=True,
                                     stop=True)
                last.then_inc(s["mix_qk"], 1)
                yield from idle(2)
                pe.wait_ge(s["mix_U0"], h + 1)
                for c in chunks:
                    last = pe.transpose(mx(0)[:, c, :], b_U[:, c, :], ident[:])
                last.then_inc(s["mix_T_ps"], 1)
                for n in range(1, LEVELS):
                    yield
                    pe.wait_ge(s["mix_B"], LEVELS * h + n + 1)
                    if n == 1:
                        pe.wait_ge(s["mix_T"], h + 1)
                        pe.wait_ge(s["mix_A"], h + 1)
                    else:
                        pe.wait_ge(s["mix_UT"], (2 * LEVELS - 3) * h + 2 * (n - 1))
                    for c in chunks:
                        last = pe.matmul(mx(1)[:, c, :], b_B[n % 2][:, c, :], b_T[:, c, :], start=True, stop=True)
                    last.then_inc(s["mix_Y_ps"], 1)
                    yield
                    pe.wait_ge(s["mix_Y"], (LEVELS - 1) * h + n)
                    if n == 1:
                        pe.wait_ge(s["mix_QK"], h + 1)
                    for c in chunks:
                        last = pe.matmul(mx(2)[:, c, :], b_Y[:, c, :], b_U[:, c, :], start=True, stop=True)
                    last.then_inc(s["mix_Z"], 1)
                    if n < LEVELS - 1:
                        for c in chunks:
                            last = pe.matmul(mx(3)[:, c, :], b_U[:, c, :], b_Y[:, c, :], start=True, stop=True)
                        last.then_inc(s["mix_Z"], 1)
                for c in chunks:
                    if c > 0:
                        yield
                        pe.wait_ge(s["ch_S"], NC * h + c)
                        pe.matmul(MX[:, 0, 0:P], b_kbT[:, c, :], S, start=True, stop=True).then_inc(s["ch_kS"], 1)
                        if c > 1:
                            pe.wait_ge(s["ch_o1"], (NC - 1) * h + c - 1)
                        pe.matmul(MX[:, 1, 0:P], cq[:, c * P:(c + 1) * P], S, start=True, stop=True).then_inc(
                            s["ch_o_ps"], 1)
                    yield
                    if c == 0:
                        pe.wait_ge(s["mix_UT"], (2 * LEVELS - 3) * h + 2 * LEVELS - 3)
                    pe.wait_ge(s["ch_r"], NC * h + c + 1)
                    pe.matmul(MX[:, 2, 0:P], b_U[:, c, :], rr, start=True, stop=True).then_inc(s["ch_v_ps"], 1)
                    yield
                    pe.wait_ge(s["ch_v"], NC * h + c + 1)
                    pe.matmul(MX[:, 0, 0:P], b_kdec[:, c, :], vn, start=True, stop=True).then_inc(s["ch_S_ps"], 1)
                    if c > 0:
                        pe.wait_ge(s["ch_o"], NC * h + c)
                    pe.matmul(MX[:, 3, 0:P], b_QK[:, c, :], vn, start=True, stop=True).then_inc(s["ch_o_ps"], 1)
                yield
                pe.wait_ge(s["o_n"], h + 1)
                for c in chunks:
                    last = pe.transpose(mx(0)[:, c, :], b_o[:, c, :], ident[:])
                last.then_inc(s["o_T"], 1)

            def new_scores():
                pe.wait_ge(s["qkp"], 1)
                pe.wait_ge(s["gates_act"], 5)
                for b in range(NB):
                    last = pe.matmul(MD[0:NH, 0, b:b + 1], qks[:, :, b], ones[:, 0:1], start=True, stop=True)
                last.then_inc(s["snew_ps"], 1)
                yield

            def delta_decode(h):
                yield from idle(2)
                pe.wait_ge(s["dkq"], h + 1)
                pe.wait_ge(s["S0_in"], 16 * h + 16)
                pe.wait_ge(s["crow_ok"], 3 * h + 3)
                pe.matmul(MD[:, 1, 0:24], ones[:], dd[:, 2:5, :].rearrange("p a b -> p (a b)"), start=True, stop=True)
                for b in range(NB):
                    last = pe.matmul(MD[:, 1, 32 + 2 * b:34 + 2 * b], S0[:, b, :], dd[:, 0:2, b], start=True,
                                     stop=True)
                last.then_inc(s["d_sum"], 1)
                yield from idle(3)
                pe.wait_ge(s["d_vec"], h + 1)
                pe.transpose(MD[0:NB, 1, 0:P], dd[:, 5, :], ident[:])
                pe.transpose(MD[0:NB, 1, P:2 * P], dd[:, 6, :], ident[:])
                pe.matmul(MD[:, 1, 2 * P:2 * P + NB], ones[:], dd[:, 8, :], start=True, stop=True).then_inc(
                    s["d_rows"], 1)
                yield from idle(2)
                for n in range(2):
                    yield
                    pe.wait_ge(s["d_vexp"], 2 * h + n + 1)
                    if n == 0:
                        pe.wait_ge(s["d_rows_ok"], h + 1)
                        pe.wait_ge(s["gated_bd"], h + 1)
                    else:
                        pe.wait_ge(s["d_add"], 2 * h + 1)
                    pe.matmul(MD[:, 1, :], kvr[:, 0, :], vexp.rearrange("p b e -> p (b e)"), start=True,
                              stop=True).then_inc(s["d_outer"], 1)

            def attn_decode(b):
                yield from idle(15)
                pe.wait_ge(s["red"], 3 * b + 3)
                for n in range(3):
                    last = pe.transpose(MD[0:NH, 0, n * P:(n + 1) * P], sc[:, n, :], ident[:])
                last.then_inc(s["sc_T"], 1)
                yield from idle(3)
                pe.wait_ge(s["p_norm"], b + 1)
                pe.matmul(MD[:, 0, 3 * NH:4 * NH], ones[0:NH, :], dg[:], start=True, stop=True)
                for n in range(3):
                    last = pe.transpose(MD[:, 0, n * NH:(n + 1) * NH], pd[:, n, :], ident[0:NH, 0:NH])
                last.then_inc(s["p_T"], 1)
                yield
                pe.wait_ge(s["pT_ok"], b + 1)
                for n in range(3):
                    pe.wait_ge(s[f"vb{n}_in"], 16 * b + 16)
                for hh in range(NH):
                    if hh == 4:
                        yield
                    for n in range(3):
                        v = V_TILE[n]
                        last = pe.matmul(MD[:, 0, 64 + hh:65 + hh], v[:, hh * HD:(hh + 1) * HD], pT[:, n, hh:hh + 1],
                                         start=n == 0, stop=n == 2)
                last.then_inc(s["pv_ps"], 1)

            pe.wait_ge(s["consts"], 48)
            pe.wait_ge(s["memset_ok"], 1)
            project(0, 0, [], first=True)
            ga = gates()
            first_a = own_a(0)
            for j in range(4):
                project(T_A + j, (1 + j) % 2, [ga, first_a])
            with pe.Fori(1, NH) as h:
                work = [tail_a(h - 1), own_a(h)]
                for j in range(4):
                    project(4 * h + (T_A + j), (1 + j) % 2, work)
            work = [tail_a(NH - 1), own_b(0), new_scores()]
            for j in range(4):
                project(T_B + j, (1 + j) % 2, work)
            pe.wait_ge(s["gated_a"], NH)
            pe.wait_ge(s["snew_ok"], 1)
            with pe.Fori(1, NH) as h:
                work = [mix_b(h - 1), own_b(h), delta_decode(h - 1), attn_decode(h - 1)]
                for j in range(4):
                    project(4 * h + (T_B + j), (1 + j) % 2, work)
            work = [mix_b(NH - 1), delta_decode(NH - 1), attn_decode(NH - 1)]
            for _ in range(40):
                for g in work:
                    next(g, None)
            pe.wait_ge(s["g_lo"], KT)
            with pe.Fori(0, KT // 2) as i:
                for n in range(2):
                    project(2 * i + (T_O + n), (1 + n) % 2, [])
            pe.wait_ge(s["sq_y"], 2 * KT)
            for c in range(NC + 1):
                n = P if c < NC else NB
                last = pe.matmul(MD[0:n, 0, c:c + 1], acc[:, c * P:c * P + n], ones[:, 0:1], start=True, stop=True)
            last.then_inc(s["ss_y"], 1)
            pe.wait_ge(s["proj_sb"], 2 * (T_O + KT))
            for c in range(NC + 1):
                n = P if c < NC else NB
                for b in range(4):
                    if c > 0:
                        pe.wait_ge(s["y_out_ok"], 4 * (c - 1) + b + 1)
                    for k in range(4):
                        last = pe.transpose(MX[0:n, b, k * P:(k + 1) * P], gated[:, 4 * b + k, c * P:c * P + n],
                                            ident[:])
                    last.then_inc(s["y_T"], 1)

        @block.scalar
        def _(act):
            ch = Chain(act, s["act_chain"])

            def hi(T, par, q, n=P, first=False):
                act.wait_ge(raw_in[q], 16 * T + 16)
                if not first:
                    if q < NQ - 1:
                        act.wait_ge(s["w_used"], 3 * T - 6 + q + 1)
                    else:
                        act.wait_ge(s["proj_ps"], 2 * T - 2)
                act.activation(w_hi[:, par, 4 * q:4 * q + 4, 0:n], w_raw[:, q, :, 0:n], ACT.Copy).then_inc(
                    s["w_hi_ok"], 1)

            def rsqrt(out, in_, scale, ok):
                ch.link(act.activation(out, in_, ACT.Ln, scale=scale, bias=EPS))
                act.activation(out, out, ACT.Exp, scale=-0.5).then_inc(ok, 1)

            def copy_out(T, half, dst, off=0):
                act.wait_ge(s["proj_ps"], 2 * T + half + 1)
                o = off + half * HALF
                n = dst.shape[0]
                act.activation(dst[:, o:o + HALF], PJ[0:n, half, 0:HALF], ACT.Copy).then_inc(s["proj_sb"], 1)

            def head(T, dsts, before, work, guards, first_split=False):
                for j in range(4):
                    for seg in range(SEGS):
                        if seg % 2 == 0:
                            hi(T + (j + 1), j % 2, seg // 2, first=first_split and j == 0)
                        if seg == 0:
                            dst, off = before if j == 0 else dsts[j - 1]
                            if dst is not None:
                                copy_out(T + (j - 1), 1, dst, off)
                        if seg == 4:
                            guards(j)
                            copy_out(T + j, 0, dsts[j][0][:], dsts[j][1])
                        for g in work:
                            next(g, None)

            A_DST = [(xq[:], 0), (xk[:], 0), (xv[:], 0), (xz[:], 0)]
            B_DST = [(xq[:], 3), (xq[:], 3), (xq[:], 3), (xz[:], 0)]

            def guards_a(h):
                def guard(j):
                    if isinstance(h, int) and h == 0:
                        return
                    if j == 0:
                        act.wait_ge(s["scores"], 4 * h)
                        act.wait_ge(s["stash_q"], h)
                        act.wait_ge(s["stash_k"], h)
                    if j == 2:
                        act.wait_ge(s["stash_v"], h)
                    if j == 3:
                        act.wait_ge(s["z_ok"], h)
                return guard

            def guards_b(h):
                def guard(j):
                    if isinstance(h, int) and h == 0 and j == 0:
                        act.wait_ge(s["scores"], 4 * NH)
                        act.wait_ge(s["stash_q"], NH)
                        act.wait_ge(s["zero_cols"], 1)
                    elif j == 0:
                        act.wait_ge(s["conv_ok"], 3 * h)
                        act.wait_ge(s["crow_ps"], 3 * h)
                    if j in (1, 2):
                        act.wait_ge(s["conv_ok"], 3 * h + j)
                        act.wait_ge(s["crow_ps"], 3 * h + j)
                    if j == 3:
                        if isinstance(h, int) and h == 0:
                            act.wait_ge(s["z_ok"], NH)
                        else:
                            act.wait_ge(s["z_ok_b"], h)
                return guard

            for c in range(NC + 1):
                n = P if c < NC else NB
                src = xin[:, c, :] if c < NC else xs_in
                if c == 0:
                    act.wait_ge(s["x_in"], 16 * (NC + 1))
                    act.wait_ge(s["ssum_set"], 1)
                if c > 0:
                    act.wait_ge(s["x_sq"], c)
                act.activation(junk[0:n], src, ACT.Square, accum_out=ssum[0:n, c:c + 1]).then_inc(s["x_sq"], 1)
            act.wait_ge(s["x_sq"], NC + 1)
            rsqrt(rstd[:], ssum[:], 1.0 / D, s["rstd_ok"])
            act.wait_ge(s["vec_ps"], 1)
            act.activation(vecT[:], MD[:, 0, 0:33], ACT.Copy).then_inc(s["vec_sb"], 1)
            for m in range(2):
                act.wait_ge(s["st_ps"], 12 * m + 12)
                act.activation(stT[:, 12 * m:12 * m + 12, :].rearrange("p m w -> p (m w)"), MX[:, 2 + m, 0:336],
                               ACT.Copy).then_inc(s["st_sb"], 1)
            act.wait_ge(s["vec_sb"], 1)
            act.wait_ge(s["x_sq"], NC + 1)
            for k in range(KT):
                act.wait_ge(s["hT_ps"], KT + k + 1)
                act.activation(h_hi[:, k, 0:TP], MX[:, k % 4, :], ACT.Copy, scale=vecT[:, k:k + 1]).then_inc(
                    s["hT_hi"], 1)
            act.wait_ge(s["memset_ok"], 1)
            for q in range(NQ):
                hi(0, 0, q, 16, first=True)

            def gates():
                yield from idle(8)
                act.wait_ge(s["gates_pe"], 1)
                act.activation(gt[:, 0:NC].rearrange("p c a h -> p (c a h)"), MD[:, 0, 0:64], ACT.Copy)
                act.activation(gt[0:NB, NC].rearrange("p a h -> p (a h)"), MD[0:NB, 0, 64:80], ACT.Copy).then_inc(
                    s["gates_act"], 1)
                yield from idle(1)
                act.wait_ge(s["gates_dve"], 1)
                ch.link(act.activation(gw[:, 0], gt[:, :, 0, :], ACT.Exp, scale=-1.0))
                ch.link(act.activation(gw[:, 2], gw[:, 1], ACT.Exp, scale=-1.0))
                act.activation(gw[:, 2], gw[:, 2], ACT.Ln, bias=1.0)
                act.wait_ge(s["adt_in"], 32)
                act.activation(gneg[:], adt[:, 0], ACT.Exp).then_inc(s["gates_act"], 1)
                yield from idle(3)
                act.wait_ge(s["gates_pe"], 2)
                cum = MD[:, 1, 0:32].rearrange("p (c h) -> p c h", c=NC)
                act.activation(G6[:, 1], cum, ACT.Copy)
                act.activation(G6[:, 3], cum, ACT.Exp)
                act.activation(G6[:, 5], MD[:, 1, 32:64].rearrange("p (c h) -> p c h", c=NC), ACT.Exp)
                act.activation(gw[0:NB, 0, NC, :], gw[0:NB, 3, NC, :], ACT.Exp).then_inc(s["gates_act"], 1)
                yield
                act.wait_ge(s["gates_dve"], 3)
                act.activation(G6[:, 4], G6[:, 4], ACT.Exp).then_inc(s["gates_act"], 1)
                yield from idle(2)
                act.wait_ge(s["gates_pe"], 3)
                act.activation(bgs[:].rearrange("p a h b -> p (a h b)"), MD[:, 0, 0:P], ACT.Copy).then_inc(
                    s["gates_act"], 1)

            def own_a(h):
                first = isinstance(h, int) and h == 0
                yield from idle(19)
                act.wait_ge(s["k_T"], h + 1)
                if not first:
                    act.wait_ge(s["k_out"], 16 * h)
                    act.wait_ge(s["row_out"], 16 * h)
                    act.wait_ge(s["qrow_out"], 16 * h)
                act.activation(ktok, mx(2), ACT.Copy).then_inc(s["ktok_ok"], 1)
                act.activation(qkrow.rearrange("p a d -> p (a d)"), MX[0:NB, 3, 0:2 * P], ACT.Copy).then_inc(
                    s["ktok_ok"], 1)
                yield
                act.wait_ge(s["ktok_ok"], 2 * h + 2)
                act.dma_start(kp_v[:, :, h, :], ktok).then_inc(s["k_out"], 16)
                act.dma_start(scratch_q[:, bass.ds(h * HD, HD)], qkrow[:, 0]).then_inc(s["qrow_out"], 16)
                act.dma_start(wk_s[0, :, 0, h, :], qkrow[:, 1]).then_inc(s["row_out"], 16)
                yield from idle(5)
                act.wait_ge(s["v_T"], h + 1)
                if not first:
                    act.wait_ge(s["v_out"], 32 * h)
                    act.wait_ge(s["attn_ps"], h)
                act.activation(vtok, mx(2), ACT.Copy).then_inc(s["vtok_ok"], 1)
                act.activation(vrow, MX[0:NB, 3, 0:P], ACT.Copy).then_inc(s["vtok_ok"], 1)
                yield
                act.wait_ge(s["vtok_ok"], 2 * h + 2)
                act.dma_start(vp_v[:, :, h, :], vtok).then_inc(s["v_out"], 16)
                act.dma_start(wv_s[0, :, 0, h, :], vrow).then_inc(s["v_out"], 16)
                yield from idle(3)
                act.wait_ge(s["negmax"], h + 1)
                for i in range(NC):
                    p = probs[:, i * (i + 1) // 2 * P:(i + 1) * (i + 2) // 2 * P]
                    act.activation(p, p, ACT.Exp, bias=stat[:, 0, i:i + 1], accum_out=stat[:, 1, i:i + 1]).then_inc(
                        s["expd"], 1)

            def tail_a(h):
                yield
                act.wait_ge(s["proj_sb"], 8 * h + 2 * T_A + 8)
                act.wait_ge(s["k_ok"], h + 1)
                act.activation(ez[:], xz[:], ACT.Exp, scale=-1.0).then_inc(s["z_exp"], 1)
                for n, (o, w) in enumerate(((0, 4), (4, 3), (7, 3))):
                    act.wait_ge(s["probT_ps"], 3 * h + n + 1)
                    act.activation(probT[:, o * P:(o + w) * P], MX[:, n, 0:w * P], ACT.Copy).then_inc(
                        s["probT_ok"], 1)
                    yield

            def own_b(h):
                for j, m in enumerate((1, 2, 0)):
                    yield from idle(10 if j == 0 else 7)
                    act.wait_ge(s["crow_ps"], 3 * h + j + 1)
                    if j > 0 or not isinstance(h, int) or h > 0:
                        act.wait_ge(s["crow_out"], 32 * (3 * h + j))
                    act.activation(rows, MD[0:11, 1, 0:P], ACT.Copy).then_inc(s["crow_ok"], 1)
                    yield
                    act.wait_ge(s["conv_ok"], 3 * h + j + 1)
                    if j == 0:
                        act.wait_ge(s["z_ok"], NH)
                        if not isinstance(h, int) or h > 0:
                            act.wait_ge(s["z_ok_b"], h)
                    else:
                        act.wait_ge(s["kv_silu"], 2 * h + j)
                    act.activation(ez[:], acc[:], ACT.Exp, scale=-1.0).then_inc(s["conv_exp"], 1)
                    act.wait_ge(s["crow_ok"], 3 * h + j + 1)
                    act.dma_start(cv_p[0, 0, :, bass.ds((h + m * NH) * P, P)], rows[0:3]).then_inc(s["crow_out"], 16)
                    act.dma_start(cv_s[0, :, 2, bass.ds((h + m * NH) * P, P)], rows[3:11]).then_inc(
                        s["crow_out"], 16)

            def mix_b(h):
                yield
                act.wait_ge(s["q_silu"], h + 1)
                act.wait_ge(s["proj_sb"], 8 * h + 2 * T_B + 8)
                act.activation(ez[:], xz[:], ACT.Exp, scale=-1.0).then_inc(s["z_exp_b"], 1)
                yield
                act.wait_ge(s["mix_ss"], h + 1)
                rsqrt(sk[:, 0:2, :], MX[:, 2, 0:2 * NC].rearrange("p (a c) -> p a c", a=2), 1.0, s["mix_rs"])
                yield
                act.wait_ge(s["mix_arg"], h + 1)
                act.activation(b_D, b_D, ACT.Exp).then_inc(s["mix_D"], 1)
                yield
                act.wait_ge(s["mix_kbT_ps"], h + 1)
                act.activation(b_kbT, mx(0), ACT.Copy).then_inc(s["mix_kbT"], 1)
                yield from idle(3)
                act.wait_ge(s["mix_T_ps"], h + 1)
                act.activation(b_T, mx(0), ACT.Copy).then_inc(s["mix_T"], 1)
                for n in range(1, LEVELS):
                    yield
                    act.wait_ge(s["mix_Y_ps"], (LEVELS - 1) * h + n)
                    act.activation(b_Y, mx(1), ACT.Copy).then_inc(s["mix_Y"], 1)
                    yield
                for c in range(NC):
                    if c > 0:
                        yield
                        act.wait_ge(s["ch_o_ps"], (2 * NC - 1) * h + 2 * c)
                        act.wait_ge(s["o_sq"], NC * h + c)
                        act.activation(o1, MX[:, 1, 0:P], ACT.Copy, scale=oq[:, c:c + 1]).then_inc(s["ch_o1"], 1)
                    yield
                    act.wait_ge(s["ch_v_ps"], NC * h + c + 1)
                    act.activation(vn, MX[:, 2, 0:P], ACT.Copy).then_inc(s["ch_v"], 1)
                    yield
                    act.wait_ge(s["ch_o"], NC * h + c + 1)
                    act.activation(o1, b_o[:, c, :], ACT.Square, accum_out=on[:, 0, c:c + 1]).then_inc(
                        s["o_sq"], 1)
                act.wait_ge(s["o_sq"], NC * h + NC)
                rsqrt(on[:, 1, :], on[:, 0, :], 1.0 / HD, s["on_rs"])

            def delta_decode(h):
                yield from idle(2)
                act.wait_ge(s["d_sum"], h + 1)
                rsqrt(dd[:, 9:11, :], MD[:, 1, 0:2 * NB].rearrange("p (a b) -> p a b", a=2), 1.0, s["d_rs"])
                yield from idle(3)
                act.wait_ge(s["d_rows"], h + 1)
                rsqrt(dd[:, 10, :], MD[:, 1, 2 * P:2 * P + NB], 1.0 / HD, s["d_rs2"])
                act.activation(kvr.rearrange("p a d -> p (a d)"), MD[0:NB, 1, 0:2 * P], ACT.Copy).then_inc(
                    s["d_rows_ok"], 1)

            def attn_decode(b):
                yield from idle(16)
                act.wait_ge(s["sc_max"], b + 1)
                act.activation(pd.rearrange("p a t -> p (a t)"), MD[0:NH, 0, 0:3 * P], ACT.Exp, bias=ds[:, 1:2],
                               scale=SCALE, accum_out=ds[:, 3:4])
                act.activation(ds[:, 4:5], ds[:, 2:3], ACT.Exp).then_inc(s["p_exp"], 1)
                yield from idle(2)
                act.wait_ge(s["p_T"], b + 1)
                act.activation(pT[:].rearrange("p a h -> p (a h)"), MD[:, 0, 0:4 * NH], ACT.Copy).then_inc(
                    s["pT_ok"], 1)

            for seg in range(SEGS):
                if seg % 2 == 0:
                    hi(1, 1, seg // 2, first=True)
                if seg == 4:
                    copy_out(0, 0, xba)
            ga, first_a = gates(), own_a(0)
            head(T_A, A_DST, (xba, 0), [ga, first_a], guards_a(0))
            with act.Fori(1, NH) as h:
                head(4 * h + T_A, A_DST, A_DST[3], [tail_a(h - 1), own_a(h)], guards_a(h))
            head(T_B, B_DST, A_DST[3], [tail_a(NH - 1), own_b(0)], guards_b(0))
            ch.end(1)
            with act.Fori(1, NH) as h:
                ch.at(h, 1, 4)
                head(4 * h + T_B, B_DST, B_DST[3],
                     [mix_b(h - 1), own_b(h), delta_decode(h - 1), attn_decode(h - 1)], guards_b(h))
            ch.end(NH - 1)
            copy_out(T_O - 1, 1, xz[:])
            work = [mix_b(NH - 1), delta_decode(NH - 1), attn_decode(NH - 1)]
            for n in range(40):
                for g in work:
                    next(g, None)
            act.wait_ge(s["gated_a"], NH)
            act.wait_ge(s["gated_ad"], NB)
            act.wait_ge(s["gated_b"], NH)
            act.wait_ge(s["gated_bd"], NH)
            for k in range(KT):
                act.activation(h_hi[:, k, :], gated[:, k, :], ACT.Copy).then_inc(s["g_hi"], 1)
            act.wait_ge(s["g_lo"], KT)
            with act.Fori(0, KT // 2 - 1) as i:
                for n in range(2):
                    T = 2 * i + (T_O + n)
                    for seg in range(SEGS):
                        if seg % 2 == 0:
                            hi(T + 1, n, seg // 2)
            T = T_O + KT - 2
            for q in range(NQ):
                hi(T + 1, 0, q)
            ch.end(1)
            act.wait_ge(s["fin_rs"], 1)
            rsqrt(fin[:], fin[:], 1.0 / D, s["fin_rs"])

        @block.vector
        def _(dve):
            ch = Chain(dve, s["dve_chain"])
            link = ch.link

            def lo(T, par, q, n=P):
                dve.wait_ge(s["w_hi_ok"], 4 * T + q + 1)
                dve.tensor_tensor(w_lo[:, par, 4 * q:4 * q + 4, 0:n], w_raw[:, q, :, 0:n],
                                  w_hi[:, par, 4 * q:4 * q + 4, 0:n].bitcast(F32), ALU.subtract).then_inc(
                    s["w_lo_dve"], 1)

            def head(T, work):
                for j in range(4):
                    for seg in range(SEGS):
                        if seg % 4 == 0:
                            lo(T + (j + 1), j % 2, seg // 2)
                        for g in work:
                            next(g, None)

            dve.memset(ssum[:], 1.0).then_inc(s["ssum_set"], 1)
            dve.memset(gt, 0.0)
            dve.memset(ones[:], 1.0)
            dve.memset(w_hi[:, 0, :, :].bitcast(F32), 0.0)
            dve.memset(w_lo[:, 0, :, :].bitcast(F32), 0.0).then_inc(s["memset_ok"], 1)
            dve.wait_ge(s["x_sq"], NC + 1)
            dve.wait_ge(s["rstd_ok"], 1)
            for c in range(NC):
                dve.tensor_scalar(xin[:, c, :], xin[:, c, :], rstd[:, c:c + 1], None, ALU.mult).then_inc(
                    s["x_scaled"], 1)
            dve.tensor_scalar(xs_in, xs_in, rstd[0:NB, NC:NC + 1], None, ALU.mult).then_inc(s["x_scaled"], 1)
            dve.wait_ge(s["vec_sb"], 1)
            dve.wait_ge(s["hT_ps"], KT)
            g_bc = vecT[:, 0:KT].unsqueeze(2).to_broadcast((P, KT, NB))
            hs = acc[:, 0:P].rearrange("p (k b) -> p k b", k=KT)
            link(dve.tensor_tensor(hs, MD[:, 1, 0:P].rearrange("p (k b) -> p k b", k=KT), g_bc, ALU.mult))
            link(dve.tensor_copy(h_hi[:, :, TP:TT], hs))
            dve.wait_ge(s["x_sq"], NC + 1)
            dve.tensor_tensor(h_lo[:, :, TP:TT], hs, h_hi[:, :, TP:TT].bitcast(F32), ALU.subtract).then_inc(
                s["hT_lo"], 1)
            for k in range(KT):
                dve.wait_ge(s["hT_hi"], k + 1)
                dve.scalar_tensor_tensor(h_lo[:, k, 0:TP], MX[:, k % 4, :], vecT[:, k:k + 1],
                                         h_hi[:, k, 0:TP].bitcast(F32), ALU.mult, ALU.subtract).then_inc(
                    s["hT_lo"], 1)
            for q in (0, 2):
                lo(0, 0, q, 16)

            def gates():
                yield from idle(8)
                dve.wait_ge(s["gates_act"], 1)
                dve.wait_ge(s["adt_in"], 32)
                a = gt[:, :, 1, :]
                dtb = adt[:, 1].unsqueeze(1).to_broadcast((P, NC + 1, NH))
                link(dve.tensor_tensor(a, a, dtb, ALU.add))
                link(dve.tensor_scalar(gw[:, 1], a, -1.0, None, ALU.mult))
                dve.tensor_tensor(gw[:, 1], gw[:, 1], a, ALU.max).then_inc(s["gates_dve"], 1)
                yield
                yield
                dve.wait_ge(s["gates_act"], 2)
                link(dve.tensor_scalar(gw[:, 0], gw[:, 0], 1.0, None, ALU.add))
                link(dve.reciprocal(gw[:, 0], gw[:, 0]))
                link(dve.tensor_scalar(a, a, 0.0, None, ALU.max))
                link(dve.tensor_tensor(a, a, gw[:, 2], ALU.add))
                link(dve.tensor_scalar(gneg[:], gneg[:], -1.0, None, ALU.mult))
                dve.tensor_copy(G6[:, 0], gw[:, 0, 0:NC, :])
                ident8 = ident[0:NB, 0:NB].unsqueeze(1).to_broadcast((NB, NH, NB))
                link(dve.tensor_tensor(dgs[:, 0], gw[0:NB, 0, NC, :].unsqueeze(2).to_broadcast((NB, NH, NB)), ident8,
                                       ALU.mult))
                dve.tensor_tensor(gw[:, 3], a, gneg[:].unsqueeze(1).to_broadcast((P, NC + 1, NH)),
                                  ALU.mult).then_inc(s["gates_dve"], 1)
                yield from idle(3)
                dve.wait_ge(s["gates_act"], 3)
                tot = MD[:, 1, 32:64].rearrange("p (c h) -> p c h", c=NC)
                dve.tensor_tensor(G6[:, 4], tot, G6[:, 1], ALU.subtract).then_inc(s["gates_dve"], 1)
                dve.tensor_scalar(G6[:, 2], G6[:, 3], -1.0, None, ALU.mult).then_inc(s["gates_dve"], 1)
                dve.tensor_tensor(dgs[:, 1], gw[0:NB, 0, NC, :].unsqueeze(2).to_broadcast((NB, NH, NB)), ident8,
                                  ALU.mult).then_inc(s["gates_dve"], 1)

            def rope_on(x, ps_ready, n, ok):
                t1, t2 = acc[0:ROT, :], ez[0:ROT, :]
                dve.wait_ge(ps_ready, n)
                link(dve.tensor_tensor(t1, x[0:ROT, 0:TT], rope[:, 0, :], ALU.mult))
                link(dve.tensor_tensor(t2.rearrange("p (a t) -> p a t", a=2), MX[0:ROT, 0:2, 0:HALF],
                                       rope[:, 1, :].rearrange("p (a t) -> p a t", a=2), ALU.mult))
                dve.tensor_tensor(x[0:ROT, 0:TT], t1, t2, ALU.add).then_inc(ok, 1)

            def own_a(h):
                first = isinstance(h, int) and h == 0
                yield from idle(9)
                rope_on(xq, s["q_rot"], h + 1, s["q_ok"])
                yield from idle(8)
                rope_on(xk, s["k_rot"], h + 1, s["k_ok"])
                yield from idle(9)
                for i in range(NC):
                    if i >= 2:
                        yield
                    p = probs[:, i * (i + 1) // 2 * P:(i + 1) * (i + 2) // 2 * P]
                    dve.wait_ge(s["scores"], NC * h + i + 1)
                    if i == 0 and not first:
                        dve.wait_ge(s["probT_ps"], 3 * h)
                    link(dve.scalar_tensor_tensor(p, MX[:, i, 0:(i + 1) * P], SCALE, lnmask[:, (NC - 1 - i) * P:TP],
                                                  ALU.mult, ALU.add))
                    link(dve.tensor_reduce(stat[:, 0, i:i + 1], p, AX.X, ALU.max))
                dve.tensor_scalar(stat[:, 0, :], stat[:, 0, :], -1.0, None, ALU.mult).then_inc(s["negmax"], 1)
                yield
                yield
                dve.wait_ge(s["expd"], NC * h + NC)
                link(dve.reciprocal(stat[:, 2, :], stat[:, 1, :]))
                for i in range(NC):
                    p = probs[:, i * (i + 1) // 2 * P:(i + 1) * (i + 2) // 2 * P]
                    dve.tensor_scalar(p, p, stat[:, 2, i:i + 1], None, ALU.mult).then_inc(s["probs_ok"], 1)

            def tail_a(h):
                yield from idle(2)
                dve.wait_ge(s["z_exp"], h + 1)
                link(dve.tensor_scalar(ez[:], ez[:], 1.0, None, ALU.add))
                link(dve.reciprocal(ez[:], ez[:]))
                dve.wait_ge(s["stash_v"], h + 1)
                dve.tensor_tensor(sz[:], xz[:], ez[:], ALU.mult).then_inc(s["z_ok"], 1)
                yield from idle(3)
                dve.wait_ge(s["z_ok"], h + 1)
                dve.wait_ge(s["attn_ps"], h + 1)
                dve.tensor_tensor(gated[:, h, 0:TP], MX[:, 3, :], sz[:, 0:TP], ALU.mult).then_inc(s["gated_a"], 1)

            def own_b(h):
                first = isinstance(h, int) and h == 0
                for j, m in enumerate((1, 2, 0)):
                    yield from idle(9 if j == 0 else 6)
                    dve.wait_ge(s["proj_sb"], 8 * h + (2 * T_B + 2 * (j + 1)))
                    if j == 0:
                        dve.wait_ge(s["cw_ok"], h + 1)
                        if not first:
                            dve.wait_ge(s["q_silu"], h)
                    else:
                        dve.wait_ge(s["kv_silu"], 2 * h + j)
                    w = cw[:, m, :]
                    link(dve.tensor_scalar(acc[:, 0:TP], xq[:, 0:TP], w[:, 24:25], None, ALU.mult))
                    for i in range(1, CW):
                        link(dve.scalar_tensor_tensor(acc[:, 0:TP], xq[:, i:i + TP], w[:, 24 + i:25 + i],
                                                      acc[:, 0:TP], ALU.mult, ALU.add))
                    st = w[:, 0:24].rearrange("p (b i) -> p b i", i=3)
                    link(dve.tensor_scalar(acc[:, TP:TT], st[:, :, 0], w[:, 24:25], None, ALU.mult))
                    for i in range(1, CW):
                        src = st[:, :, i] if i < 3 else xq[:, 3 + TP:3 + TT]
                        ins = dve.scalar_tensor_tensor(acc[:, TP:TT], src, w[:, 24 + i:25 + i], acc[:, TP:TT],
                                                       ALU.mult, ALU.add)
                        if i < 3:
                            link(ins)
                    ins.then_inc(s["conv_ok"], 1)
                    yield from idle(2)
                    dve.wait_ge(s["conv_exp"], 3 * h + j + 1)
                    link(dve.tensor_scalar(ez[:], ez[:], 1.0, None, ALU.add))
                    ins = dve.reciprocal(ez[:], ez[:])
                    if j < 2:
                        link(ins)
                        if j == 0 and not first:
                            dve.wait_ge(s["mix_qk"], h)
                        if j == 0 and first:
                            dve.wait_ge(s["scores"], NC * NH)
                            dve.wait_ge(s["stash_k"], NH)
                        if j == 1 and not first:
                            dve.wait_ge(s["mix_T1"], h)
                        if j == 1 and first:
                            dve.wait_ge(s["v_T"], NH)
                            dve.wait_ge(s["stash_v"], NH)
                        dve.tensor_tensor((xk, xv)[j][:], acc[:], ez[:], ALU.mult).then_inc(s["kv_silu"], 1)
                    else:
                        link(ins)

            def bc(col):
                return col.unsqueeze(2).to_broadcast((P, NC, P))

            def mix_b(h):
                dve.tensor_tensor(cq[:], acc[:], ez[:], ALU.mult).then_inc(s["q_silu"], 1)
                yield
                yield
                dve.wait_ge(s["z_exp_b"], h + 1)
                link(dve.tensor_scalar(ez[:], ez[:], 1.0, None, ALU.add))
                link(dve.reciprocal(ez[:], ez[:]))
                dve.tensor_tensor(sz[:], xz[:], ez[:], ALU.mult).then_inc(s["z_ok_b"], 1)
                dve.wait_ge(s["mix_ss"], h + 1)
                dve.wait_ge(s["hg_ok"], h + 1)
                dve.wait_ge(s["mix_rs"], h + 1)
                link(dve.tensor_scalar(sk[:, 1, :], sk[:, 1, :], SCALE, None, ALU.mult))
                dve.tensor_tensor(sk[:, 3, :], sk[:, 0, :], hg[:, 4, :], ALU.mult).then_inc(s["mix_scal"], 1)
                dve.tensor_tensor(sk[:, 2, :], sk[:, 0, :], hg[:, 0, :], ALU.mult).then_inc(s["mix_scal"], 1)
                dve.tensor_tensor(oq[:], sk[:, 1, :], hg[:, 3, :], ALU.mult).then_inc(s["mix_scal"], 1)
                dve.wait_ge(s["mix_scal"], 3 * h + 3)
                yield
                dve.wait_ge(s["mix_T1"], h + 1)
                dve.tensor_tensor(b_kb, mx(0), bc(sk[:, 2, :]), ALU.mult).then_inc(s["mix_tok"], 1)
                dve.tensor_tensor(b_kdec, mx(0), bc(sk[:, 3, :]), ALU.mult).then_inc(s["mix_tok"], 1)
                dve.tensor_tensor(b_vb, mx(1), bc(hg[:, 0, :]), ALU.mult).then_inc(s["mix_tok"], 1)
                dve.wait_ge(s["mix_gb"], h + 1)
                link(dve.tensor_tensor(b_D, mx(3), bc(hg[:, 1, :]), ALU.subtract))
                dve.tensor_scalar(b_D, b_D, 0.0, None, ALU.min).then_inc(s["mix_arg"], 1)
                yield
                dve.wait_ge(s["mix_D"], h + 1)
                dve.wait_ge(s["mix_W"], h + 1)
                link(dve.tensor_tensor(b_D, b_D, b_QK, ALU.mult))
                yield
                dve.wait_ge(s["mix_kk"], h + 1)
                dve.tensor_tensor(b_A, mx(1), b_D, ALU.mult).then_inc(s["mix_A"], 1)
                dve.wait_ge(s["mix_qk"], h + 1)
                dve.tensor_tensor(b_QK, mx(2), b_D, ALU.mult).then_inc(s["mix_QK"], 1)
                yield from idle(2)
                for n in range(1, LEVELS):
                    yield
                    yield
                    z = (2 * LEVELS - 3) * h + 2 * (n - 1) + 1
                    dve.wait_ge(s["mix_Z"], z)
                    if n < LEVELS - 1:
                        dve.wait_ge(s["mix_Z"], z + 1)
                    dve.tensor_tensor(b_U, b_U, mx(2), ALU.subtract).then_inc(s["mix_UT"], 1)
                    if n < LEVELS - 1:
                        dve.tensor_tensor(b_T, b_T, mx(3), ALU.subtract).then_inc(s["mix_UT"], 1)
                for c in range(NC):
                    if c == 0:
                        dve.tensor_copy(rr, b_vb[:, 0, :]).then_inc(s["ch_r"], 1)
                    else:
                        yield
                        dve.wait_ge(s["ch_kS"], (NC - 1) * h + c)
                        dve.scalar_tensor_tensor(rr, MX[:, 0, 0:P], hg[:, 2, c:c + 1], b_vb[:, c, :], ALU.mult,
                                                 ALU.add).then_inc(s["ch_r"], 1)
                    yield
                    yield
                    dve.wait_ge(s["ch_S_ps"], NC * h + c + 1)
                    if c == 0:
                        dve.wait_ge(s["S_out"], 16 * h + 16)
                        dve.tensor_copy(S, MX[:, 0, 0:P]).then_inc(s["ch_S"], 1)
                    else:
                        dve.scalar_tensor_tensor(S, S, hg[:, 5, c:c + 1], MX[:, 0, 0:P], ALU.mult,
                                                 ALU.add).then_inc(s["ch_S"], 1)
                    dve.wait_ge(s["ch_o_ps"], (2 * NC - 1) * h + 2 * c + 1)
                    if c == 0:
                        dve.tensor_scalar(b_o[:, c, :], MX[:, 3, 0:P], sk[:, 1, c:c + 1], None, ALU.mult).then_inc(
                            s["ch_o"], 1)
                    else:
                        dve.wait_ge(s["ch_o1"], (NC - 1) * h + c)
                        dve.scalar_tensor_tensor(b_o[:, c, :], MX[:, 3, 0:P], sk[:, 1, c:c + 1], o1, ALU.mult,
                                                 ALU.add).then_inc(s["ch_o"], 1)
                dve.wait_ge(s["on_rs"], h + 1)
                dve.tensor_tensor(b_o, b_o, bc(on[:, 1, :]), ALU.mult).then_inc(s["o_n"], 1)
                yield
                dve.wait_ge(s["o_T"], h + 1)
                dve.wait_ge(s["z_ok_b"], h + 1)
                dve.scalar_tensor_tensor(gated[:, NH + h, 0:TP], MX[:, 0, :], vecT[:, 32:33], sz[:, 0:TP], ALU.mult,
                                         ALU.mult).then_inc(s["gated_b"], 1)

            def new_scores():
                dve.wait_ge(s["stash_k"], NH)
                dve.wait_ge(s["stash_q"], NH)
                dve.tensor_tensor(qks[:], qS[:], kS[:], ALU.mult).then_inc(s["qkp"], 1)
                yield
                dve.wait_ge(s["snew_ps"], 1)
                dve.tensor_scalar(snew[:], MD[0:NH, 0, 0:NB], SCALE, None, ALU.mult).then_inc(s["snew_ok"], 1)

            def delta_decode(h):
                kd, qd = xk[:, TP:TT], cq[:, TP:TT]
                yield
                dve.wait_ge(s["q_silu"], h + 1)
                dve.wait_ge(s["kv_silu"], 2 * h + 2)
                dve.tensor_copy(dd[:, 0, :], kd)
                dve.tensor_copy(dd[:, 1, :], qd)
                dve.tensor_tensor(dd[:, 2, :], kd, kd, ALU.mult)
                dve.tensor_tensor(dd[:, 3, :], qd, qd, ALU.mult)
                dve.tensor_copy(bt_s(0), bgs[:, 0, h, :])
                dve.tensor_copy(bt_s(1), bgs[:, 1, h, :])
                dve.tensor_tensor(dd[:, 4, :], kd, qd, ALU.mult).then_inc(s["dkq"], 1)
                yield
                yield
                dve.wait_ge(s["dkq"], h + 1)
                dve.wait_ge(s["d_sum"], h + 1)
                rk, rq = dd[:, 9, :], dd[:, 10, :]
                ks = MD[:, 1, 32:32 + 2 * NB].rearrange("p (b a) -> p a b", a=2)
                dve.wait_ge(s["d_rs"], h + 1)
                link(dve.tensor_scalar(rq, rq, SCALE, None, ALU.mult))
                dve.tensor_tensor(dd[:, 5, :], dd[:, 0, :], rk, ALU.mult)
                link(dve.tensor_tensor(dd[:, 6, :], ks[:, 0], rk, ALU.mult))
                link(dve.tensor_tensor(dd[:, 6, :], dd[:, 6, :], bt_s(1), ALU.mult))
                link(dve.tensor_tensor(dd[:, 6, :], xv[:, TP:TT], dd[:, 6, :], ALU.subtract))
                link(dve.tensor_tensor(dd[:, 6, :], dd[:, 6, :], bt_s(0), ALU.mult))
                link(dve.tensor_tensor(dd[:, 7, :], MD[:, 1, 2 * NB:3 * NB], rk, ALU.mult))
                link(dve.tensor_tensor(dd[:, 7, :], dd[:, 7, :], dd[:, 6, :], ALU.mult))
                link(dve.tensor_tensor(dd[:, 8, :], ks[:, 1], bt_s(1), ALU.mult))
                link(dve.tensor_tensor(dd[:, 7, :], dd[:, 7, :], dd[:, 8, :], ALU.add))
                link(dve.tensor_tensor(dd[:, 7, :], dd[:, 7, :], rq, ALU.mult))
                dve.tensor_tensor(dd[:, 8, :], dd[:, 7, :], dd[:, 7, :], ALU.mult).then_inc(s["d_vec"], 1)
                yield
                yield
                dve.wait_ge(s["d_rows"], h + 1)
                dve.wait_ge(s["z_ok_b"], h + 1)
                dve.wait_ge(s["d_rs2"], h + 1)
                link(dve.tensor_tensor(dd[:, 7, :], dd[:, 7, :], dd[:, 10, :], ALU.mult))
                dve.scalar_tensor_tensor(gated[:, NH + h, TP:TT], dd[:, 7, :], vecT[:, 32:33], sz[:, TP:TT], ALU.mult,
                                         ALU.mult).then_inc(s["gated_bd"], 1)
                yield from idle(2)
                for n in range(2):
                    yield
                    dve.wait_ge(s["d_outer"], 2 * h + n + 1)
                    dve.wait_ge(s["S0_scaled"], h + 1)
                    st = S0[:, 4 * n:4 * n + 4, :]
                    dve.tensor_tensor(st, st, MD[:, 1, :].rearrange("p (b e) -> p b e", b=4), ALU.add).then_inc(
                        s["d_add"], 1)

            def bt_s(n):
                return dd[:, 12 - n, :]

            def attn_decode(b):
                yield from idle(8)
                for n in range(3):
                    dve.wait_ge(s["prod"], 3 * b + n + 1)
                    src = K_TILE[n]
                    dve.tensor_reduce(sc[:, n, :], src.rearrange("p (h d) -> p h d", h=NH), AX.X, ALU.add).then_inc(
                        s["red"], 1)
                    yield
                    yield
                    if n == 1:
                        yield
                dve.wait_ge(s["sc_T"], b + 1)
                link(dve.tensor_reduce(ds[:, 0:1], MD[0:NH, 0, 0:3 * P], AX.X, ALU.max))
                link(dve.tensor_copy(ds[:, 2:3], snew[:, bass.ds(b, 1)]))
                link(dve.scalar_tensor_tensor(ds[:, 0:1], ds[:, 0:1], SCALE, ds[:, 2:3], ALU.mult, ALU.max))
                link(dve.tensor_scalar(ds[:, 1:2], ds[:, 0:1], -1.0, None, ALU.mult))
                dve.tensor_tensor(ds[:, 2:3], ds[:, 2:3], ds[:, 0:1], ALU.subtract).then_inc(s["sc_max"], 1)
                yield
                yield
                dve.wait_ge(s["p_exp"], b + 1)
                link(dve.tensor_scalar(ds[:, 4:5], ds[:, 4:5], 3.0, None, ALU.mult))
                link(dve.tensor_tensor(ds[:, 5:6], ds[:, 3:4], ds[:, 4:5], ALU.add))
                link(dve.reciprocal(ds[:, 5:6], ds[:, 5:6]))
                link(dve.tensor_tensor(ds[:, 4:5], ds[:, 4:5], ds[:, 5:6], ALU.mult))
                dve.tensor_scalar(dg[:], ident[0:NH, 0:NH], ds[:, 4:5], None, ALU.mult)
                dve.tensor_scalar(pd, pd, ds[:, 5:6], None, ALU.mult).then_inc(s["p_norm"], 1)
                yield
                yield
                dve.wait_ge(s["pT_ok"], b + 1)
                link(dve.tensor_tensor(da[:], vS[:, :, b], pT[:, 3, :], ALU.mult))
                dve.wait_ge(s["pv_ps"], b + 1)
                link(dve.tensor_tensor(da[:], MD[:, 0, 64:64 + NH], da[:], ALU.add))
                dve.tensor_tensor(gated[:, 0:NH, TP + b], da[:], zS[:, :, b], ALU.mult).then_inc(s["gated_ad"], 1)

            for q in (0, 2):
                lo(1, 1, q)
            dve.wait_ge(s["s_loaded"], 32)
            ga, first_a = gates(), own_a(0)
            head(T_A, [ga, first_a])
            ch.end(1)
            with dve.Fori(1, NH) as h:
                ch.at(h, 1, 15)
                head(4 * h + T_A, [tail_a(h - 1), own_a(h)])
            ch.end(NH - 1)
            head(T_B, [tail_a(NH - 1), own_b(0), new_scores()])
            ch.end(1)
            dve.wait_ge(s["stash_z"], NH)
            with dve.Fori(1, NH) as h:
                ch.at(h, 1, 53)
                head(4 * h + T_B, [mix_b(h - 1), own_b(h), delta_decode(h - 1), attn_decode(h - 1)])
            ch.end(NH - 1)
            work = [mix_b(NH - 1), delta_decode(NH - 1), attn_decode(NH - 1)]
            for _ in range(40):
                for g in work:
                    next(g, None)
            for k in range(KT):
                dve.wait_ge(s["g_hi"], k + 1)
                dve.tensor_tensor(h_lo[:, k, :], gated[:, k, :], h_hi[:, k, :].bitcast(F32), ALU.subtract).then_inc(
                    s["g_lo"], 1)
            link(dve.memset(acc[:], 0.0))
            ch.end(1)

            def y_half(T, j, half):
                dve.wait_ge(s["proj_ps"], 2 * T + half + 1)
                tok = slice(half * HALF, (half + 1) * HALF)
                link(dve.tensor_copy(sz[:, tok], PJ[:, half, 0:HALF]))
                dve.tensor_scalar(gated[:, j, tok], sz[:, tok], fin[:, 0:1], None, ALU.mult).then_inc(s["proj_sb"], 1)
                link(dve.tensor_tensor(ez[:, tok], sz[:, tok], sz[:, tok], ALU.mult))
                dve.tensor_tensor(acc[:, tok], acc[:, tok], ez[:, tok], ALU.add).then_inc(s["sq_y"], 1)

            def y_tile(T, j, par, split=True):
                link(dve.tensor_copy(fin[:, 0:1], vecT[:, bass.ds(j + KT, 1)]))
                if split:
                    lo(T + 1, par, 0)
                    lo(T + 1, par, 2)
                y_half(T, j, 0)
                y_half(T, j, 1)

            dve.wait_ge(s["proj_sb"], 2 * T_O)
            with dve.Fori(0, KT // 2 - 1) as i:
                ch.at(i, 0, 10)
                for n in range(2):
                    y_tile(2 * i + (T_O + n), 2 * i + n, n)
            ch.end(KT // 2 - 1)
            y_tile(T_O + KT - 2, KT - 2, 0)
            y_tile(T_O + KT - 1, KT - 1, 1, split=False)
            dve.wait_ge(s["sq_y"], 2 * KT)
            link(dve.memset(fin[:], 1.0))
            dve.wait_ge(s["ss_y"], 1)
            link(dve.tensor_copy(fin[:, 0:NC], MD[:, 0, 0:NC]))
            link(dve.tensor_copy(fin[0:NB, NC:NC + 1], MD[0:NB, 0, NC:NC + 1]))
            dve.tensor_copy(fin[:, 7:8], fin[:, 7:8]).then_inc(s["fin_rs"], 1)
            dve.wait_ge(s["fin_rs"], 2)
            for c in range(NC + 1):
                n = P if c < NC else NB
                dve.wait_ge(s[f"xr_in{c % 2}"], 16 * (c // 2) + 16)
                for b in range(4):
                    x = xres[c % 2][0:n, b * TP:(b + 1) * TP]
                    dve.wait_ge(s["y_T"], 4 * c + b + 1)
                    dve.scalar_tensor_tensor(x, MX[0:n, b, :], fin[0:n, c:c + 1], x, ALU.mult, ALU.add).then_inc(
                        s["y_out_ok"], 1)

        @block.gpsimd
        def _(pool):
            def lo(T, par, q, n=P):
                pool.wait_ge(s["w_hi_ok"], 4 * T + q + 1)
                pool.tensor_tensor(w_lo[:, par, 4 * q:4 * q + 4, 0:n], w_raw[:, q, :, 0:n],
                                   w_hi[:, par, 4 * q:4 * q + 4, 0:n].bitcast(F32), ALU.subtract).then_inc(
                    s["w_lo_pool"], 1)

            def head(T, work):
                for j in range(4):
                    for seg in range(SEGS):
                        if seg % 4 == 2:
                            lo(T + (j + 1), j % 2, seg // 2)
                        for g in work:
                            next(g, None)

            def own_a(h):
                yield from idle(10)
                pool.wait_ge(s["q_ok"], h + 1)
                pool.tensor_copy(qS[:, h, :], xq[:, TP:TT]).then_inc(s["stash_q"], 1)
                yield from idle(8)
                pool.wait_ge(s["k_ok"], h + 1)
                pool.tensor_copy(kS[:, h, :], xk[:, TP:TT]).then_inc(s["stash_k"], 1)
                yield from idle(8)
                pool.wait_ge(s["proj_sb"], 8 * h + 2 * T_A + 6)
                pool.tensor_copy(vS[:, h, :], xv[:, TP:TT]).then_inc(s["stash_v"], 1)

            def tail_a(h):
                yield from idle(3)
                pool.wait_ge(s["z_ok"], h + 1)
                pool.tensor_copy(zS[:, h, :], sz[:, TP:TT]).then_inc(s["stash_z"], 1)

            def own_b(h):
                if isinstance(h, int) and h == 0:
                    pool.wait_ge(s["st_sb"], 2)
                else:
                    pool.wait_ge(s["conv_ok"], 3 * h)
                pool.tensor_copy(cw[:], stT[:].rearrange("p (m h) w -> p m h w", m=3)[:, :, h, :]).then_inc(
                    s["cw_ok"], 1)
                yield

            def mix_b(h):
                pool.wait_ge(s["q_silu"], h + 1)
                pool.tensor_copy(hg[:], G6[:, :, :, h]).then_inc(s["hg_ok"], 1)
                pool.wait_ge(s["hg_ok"], h + 1)
                pool.tensor_tensor(b_B0, ident[:].unsqueeze(1).to_broadcast((P, NC, P)),
                                   hg[:, 1, :].unsqueeze(2).to_broadcast((P, NC, P)), ALU.mult).then_inc(
                    s["mix_gr"], 1)
                kk, qq = xk[:, 0:TP].rearrange("p (c d) -> p c d", c=NC), cq[:, 0:TP].rearrange("p (c d) -> p c d", c=NC)
                pool.wait_ge(s["kv_silu"], 2 * h + 2)
                pool.tensor_tensor(b_o, kk, kk, ALU.mult).then_inc(s["sq_ok"], 1)
                yield
                pool.wait_ge(s["q_silu"], h + 1)
                pool.tensor_tensor(b_Y, qq, qq, ALU.mult).then_inc(s["sq_ok"], 1)
                yield
                yield
                pool.wait_ge(s["mix_scal"], 3 * h + 1)
                pool.tensor_tensor(b_QK, upper[:].unsqueeze(1).to_broadcast((P, NC, P)),
                                   sk[:, 0, :].unsqueeze(2).to_broadcast((P, NC, P)), ALU.mult).then_inc(
                    s["mix_W"], 1)
                yield from idle(3)
                pool.wait_ge(s["mix_A"], h + 1)
                pool.wait_ge(s["mix_gb"], h + 1)
                for n in range(LEVELS):
                    if n == 1:
                        pool.wait_ge(s["mix_QK"], h + 1)
                    if n == 2:
                        pool.wait_ge(s["mix_U0"], h + 1)
                    if n >= 3:
                        pool.wait_ge(s["mix_Y_ps"], (LEVELS - 1) * h + n - 2)
                    ins = pool.tensor_tensor(b_B[n % 2], b_A, levels[:, n, :].unsqueeze(1).to_broadcast((P, NC, P)),
                                             ALU.mult)
                    ins.then_inc(s["mix_B"], 1)
                    if n == 0:
                        pool.wait_ge(s["mix_B"], LEVELS * h + 1)
                        pool.tensor_tensor(b_U, ident[:].unsqueeze(1).to_broadcast((P, NC, P)), b_B[0],
                                           ALU.subtract).then_inc(s["mix_U0"], 1)
                        yield
                    if n >= 1:
                        yield
                        yield

            def delta_decode(h):
                yield from idle(3)
                pool.wait_ge(s["d_sum"], h + 1)
                pool.tensor_tensor(S0[:], S0[:], dd[:, 11, :].unsqueeze(2).to_broadcast((P, NB, P)),
                                   ALU.mult).then_inc(s["S0_scaled"], 1)
                yield from idle(3)
                for n in range(2):
                    pool.wait_ge(s["d_rows_ok"], h + 1)
                    if n == 1:
                        pool.wait_ge(s["d_outer"], 2 * h + 1)
                    pool.tensor_tensor(vexp, kvr[:, 1, :].unsqueeze(1).to_broadcast((NB, 4, P)),
                                       ident[0:NB, 4 * n:4 * n + 4].unsqueeze(2).to_broadcast((NB, 4, P)),
                                       ALU.mult).then_inc(s["d_vexp"], 1)
                    yield
                    yield
                    yield

            def attn_decode(b):
                yield from idle(5)
                pool.wait_ge(s["qb_in"], 16 * b + 16)
                for n in range(3):
                    yield
                    pool.wait_ge(s[f"kb{n}_in"], 16 * b + 16)
                    t = K_TILE[n]
                    pool.tensor_tensor(t, t, qb[:], ALU.mult).then_inc(s["prod"], 1)
                    yield
                    if n == 1:
                        yield

            for q in (1, 3):
                pool.wait_ge(s["memset_ok"], 1)
                lo(0, 0, q, 16)
            for q in (1, 3):
                lo(1, 1, q)
            head(T_A, [own_a(0)])
            with pool.Fori(1, NH) as h:
                head(4 * h + T_A, [tail_a(h - 1), own_a(h)])
            pool.wait_ge(s["scores"], 4 * NH)
            pool.memset(xq[:, 0:3], 0.0).then_inc(s["zero_cols"], 1)
            head(T_B, [tail_a(NH - 1), own_b(0)])
            pool.wait_ge(s["gates_dve"], 5)
            pool.wait_ge(s["gates_act"], 4)
            pool.wait_ge(s["gated_a"], NH)
            pool.wait_ge(s["k_out"], 16 * NH)
            pool.wait_ge(s["v_out"], 32 * NH)
            with pool.Fori(1, NH) as h:
                head(4 * h + T_B, [mix_b(h - 1), own_b(h), delta_decode(h - 1), attn_decode(h - 1)])
            work = [mix_b(NH - 1), delta_decode(NH - 1), attn_decode(NH - 1)]
            for _ in range(40):
                for g in work:
                    next(g, None)
            with pool.Fori(0, KT // 2 - 1) as i:
                for n in range(2):
                    for q in (1, 3):
                        lo(2 * i + (T_O + n + 1), n, q)
            for q in (1, 3):
                lo(T_O + KT - 1, 0, q)


_INS = ["x_prompt", "x_sample", "cache_win_k", "cache_win_v", "state_conv", "state_delta", "g_pre", "w_in", "conv_w",
        "a_log", "dt_bias", "onorm_w", "w_out", "g_post"]
_CONST = ["c_ident", "c_upper", "c_levels", "c_lnmask", "c_rope", "c_rot"]
_OUTS = [(1, TP, D), (NB, 1, D), (1, 1, TP, NH, HD), (1, 1, TP, NH, HD), (1, 1, CW - 1, CONV_CH), (1, 1, NH, HD, HD),
         (1, NB, 1, NH, HD), (1, NB, 1, NH, HD), (1, NB, CW - 1, CONV_CH), (1, NB, NH, HD, HD)]


def kernel(**inputs):
    import concourse.bacc as bacc
    from concourse.bass_utils import run_bass_kernel_spmd

    nc = bacc.Bacc("TRN2", target_bir_lowering=False, num_devices=1)
    arrays, args = {}, []
    consts = tables()
    for name in _INS + _CONST:
        a = np.ascontiguousarray(inputs[name] if name in inputs else consts[name])
        arrays[f"in_{name}"] = a
        args.append(nc.dram_tensor(f"in_{name}", a.shape, mybir.dt.from_np(a.dtype), kind="ExternalInput").ap())
    for i, shape in enumerate(_OUTS):
        args.append(nc.dram_tensor(f"out_{i}", shape, F32, kind="ExternalOutput").ap())
    build(nc, *args)
    r = run_bass_kernel_spmd(nc, [arrays], core_ids=[0])
    return tuple(r.results[0][f"out_{i}"] for i in range(len(_OUTS)))
```

```python
from contextlib import ExitStack
import numpy as np
import concourse.bass as bass
from concourse import mybir

F32 = mybir.dt.float32
F32R = mybir.dt.float32r
ALU = mybir.AluOpType
ACT = mybir.ActivationFunctionType
AX = mybir.AxisListType

P = 128
D = 2048
TP = 512
NB = 8
TT = TP + NB
HALF = TT // 2
KT = D // P
NQ = 4
NH = 8
HD = 128
NC = TP // P
WA = NH * HD
CONV_CH = 3 * WA
CW = 4
PAST = 2048
ROT = 32
EPS = 1e-6
SCALE = HD ** -0.5
LEVELS = 7
NEG = -1.0e30
SEGS = 8
T_A, T_B, T_O = 1, 1 + 4 * NH, 1 + 8 * NH


def tables():
    f = np.float32
    i = np.arange(P)
    t = {"c_ident": np.eye(P, dtype=f), "c_upper": (i[:, None] <= i[None, :]).astype(f)}
    t["c_causal"] = np.where(i[:, None] <= i[None, :], 0.0, NEG).astype(f)
    lev = np.zeros((P, LEVELS, P), mybir.dt.np(mybir.dt.bfloat16))
    for n in range(LEVELS):
        s = 1 << n
        same = i[:, None] // (2 * s) == i[None, :] // (2 * s)
        lev[:, n] = same & ((i[:, None] // s) % 2 == 0) & ((i[None, :] // s) % 2 == 1)
    t["c_levels"] = lev
    kk = np.arange(TP)
    dist = P * (NC - 1 - kk // P)[None, :] + i[:, None] - (kk % P)[None, :]
    cnt = sum(((dist >= 0) & (dist <= w) & (dist % d == 0)).astype(int) for w, d in ((128, 1), (512, 4), (2048, 16)))
    t["c_lnmask"] = np.where(cnt > 0, np.log(np.maximum(cnt, 1)), NEG).astype(f)
    half = ROT // 2
    inv = f(500000.0) ** (-np.arange(half, dtype=f) / f(half))
    pos = np.concatenate([np.arange(TP), np.full(NB, PAST)]).astype(f)
    ang = (pos[:, None] * inv[None, :]).astype(f).T.astype(np.float64)
    t["c_rope"] = np.stack([np.tile(np.cos(ang), (2, 1)), np.tile(np.sin(ang), (2, 1))], 1).astype(f)
    rot = np.zeros((ROT, 2 * ROT), f)
    for m in range(half):
        rot[m + half, m] = -1.0
        rot[m, m + half] = 1.0
    t["c_rot"] = rot
    return t


class Chain:

    def __init__(self, eng, sem):
        self.eng, self.sem, self.base, self.off, self.n, self.per = eng, sem, 0, 0, 0, 0

    def at(self, h, first, per):
        self.off, self.n, self.per = (h - first) * per, 0, per

    def end(self, iterations):
        assert iterations == 1 or self.n == self.per, (self.n, self.per)
        self.base, self.off, self.n = self.base + iterations * self.n, 0, 0

    def link(self, ins):
        self.n += 1
        ins.then_inc(self.sem, 1)
        self.eng.wait_ge(self.sem, self.off + (self.base + self.n))


def idle(n):
    for _ in range(n):
        yield


def build(nc, x_prompt, x_sample, cache_k, cache_v, state_conv, state_delta, g_pre, w_in, conv_w, a_log, dt_bias,
          onorm_w, w_out, g_post, c_ident, c_upper, c_causal, c_levels, c_lnmask, c_rope, c_rot,
          y_p, y_s, wk_p, wv_p, cv_p, st_p, wk_s, wv_s, cv_s, st_s):
    w_in_v = w_in[0].rearrange("(kt p) c -> p kt c", p=P)
    w_out_v = w_out[0].rearrange("(kt p) c -> p kt c", p=P)
    kp_v = wk_p[0, 0].rearrange("(c p) h d -> p c h d", p=P)
    vp_v = wv_p[0, 0].rearrange("(c p) h d -> p c h d", p=P)
    scratch_q = nc.dram_tensor("scratch_q", (NB, WA), F32, kind="Internal").ap()

    with ExitStack() as ctx:
        def sb(name, shape, dt=F32):
            return ctx.enter_context(nc.sbuf_tensor(name, shape, dt))

        def sem(name):
            return ctx.enter_context(nc.semaphore(name))

        h_hi = sb("h_hi", [P, KT, TT], F32R)
        h_lo = sb("h_lo", [P, KT, TT], F32R)
        w_raw = sb("w_raw", [P, NQ, 4, P])
        w_hi = sb("w_hi", [P, 2, KT, P], F32R)
        w_lo = sb("w_lo", [P, 2, KT, P], F32R)
        gated = sb("gated", [P, KT, TT])
        xin = gated[:].rearrange("p a b -> p (a b)")[:, 0:NC * D].rearrange("p (c d) -> p c d", d=D)
        ident = sb("ident", [P, P])
        upper = sb("upper", [P, P])
        causal = sb("causal", [P, P])
        ones = sb("ones", [P, P])
        levels = sb("levels", [P, LEVELS, P], mybir.dt.bfloat16)
        arena = sb("arena", [P, 4096 + 2 * TT])
        lnmask = arena[:, 0:TP]
        probs = arena[:, TP:TP + 10 * P]
        probT = arena[:, TP + 10 * P:TP + 20 * P]
        ktok = arena[:, TP + 20 * P:TP + 24 * P].rearrange("p (c d) -> p c d", c=NC)
        vtok = arena[:, TP + 24 * P:TP + 28 * P].rearrange("p (c d) -> p c d", c=NC)
        rope = arena[0:ROT, 4096:4096 + 2 * TT].rearrange("p (a t) -> p a t", a=2)
        b_kb, b_kbT, b_kdec, b_vb, b_D, b_QK, b_U, b_T, b_Y, b_B0 = [
            arena[:, n * TP:(n + 1) * TP].rearrange("p (c d) -> p c d", c=NC) for n in range(10)]
        b_A = b_kb
        b_B = (b_B0, b_D)
        b_o = b_T
        xq = sb("xq", [P, 3 + TT])
        xk = sb("xk", [P, TT])
        xv = sb("xv", [P, TT])
        xz = sb("xz", [P, TT])
        cq = sb("cq", [P, TT])
        acc = sb("acc", [P, TT])
        ez = sb("ez", [P, TT])
        sz = sb("sz", [P, TT])
        small = sb("small", [P, 4 * P])
        S = small[:, 0:P]
        rr = small[:, P:2 * P]
        vn = small[:, 2 * P:3 * P]
        o1 = small[:, 3 * P:4 * P]
        gw = small[:, 0:160].rearrange("p (a c h) -> p a c h", a=4, c=NC + 1)
        gt = small[:, 160:240].rearrange("p (c a h) -> p c a h", a=2, c=NC + 1)
        kv = sb("kv", [P, 2, WA])
        S0 = sb("S0", [P, NB, P])
        rb = sb("rb", [11, 10 * P])
        rows = rb[:, 0:P]
        vexp = rb[0:NB, P:5 * P].rearrange("p (b e) -> p b e", e=P)
        pd = rb[0:NH, 5 * P:8 * P].rearrange("p (n t) -> p n t", n=3)
        kvr = rb[0:NB, 8 * P:10 * P].rearrange("p (n t) -> p n t", n=2)
        qkrow = rb[0:NB, 5 * P:7 * P].rearrange("p (n t) -> p n t", n=2)
        vrow = rb[0:NB, 7 * P:8 * P]
        dgs = rb[0:NB, 8 * P:9 * P].rearrange("p (a h b) -> p a h b", a=2, h=NH)
        stT = sb("stT", [P, 3 * NH, 28])
        cw = sb("cw", [P, 3, 28])
        vecT = sb("vecT", [P, KT + 1])
        ssum = sb("ssum", [P, 8])
        rstd = sb("rstd", [P, 8])
        adt = sb("adt", [P, 2, NH])
        G6 = sb("G6", [P, 6, NC, NH])
        hg = sb("hg", [P, 6, NC])
        gneg = sb("gneg", [P, NH])
        bgs = sb("bgs", [P, 2, NH, NB])
        sk = sb("sk", [P, 4, NC])
        lnss = sb("lnss", [P, 2, NC])
        lnrk = sb("lnrk", [P, NC])
        oq = sb("oq", [P, NC])
        on = sb("on", [P, 2, NC])
        stat = sb("stat", [P, 3, NC])
        qS = sb("qS", [P, NH, NB])
        kS = sb("kS", [P, NH, NB])
        vS = sb("vS", [P, NH, NB])
        zS = sb("zS", [P, NH, NB])
        qks = sb("qks", [P, NH, NB])
        snew = sb("snew", [NH, NB])
        sc = sb("sc", [P, 3, NH])
        ds = sb("ds", [NH, 8])
        dg = sb("dg", [NH, NH])
        pT = sb("pT", [P, 4, NH])
        da = sb("da", [P, NH])
        dd = sb("dd", [P, 13, NB])
        fin = sb("fin", [P, 8])
        rotm = sb("rotm", [ROT, 2 * ROT])
        s_in = xz[:, 0:P]
        xba = cq[0:16, :]
        scin = arena[0:28, 0:CONV_CH]
        xs_in = kv[0:NB].rearrange("p a b -> p (a b)")
        junk = arena[:, CONV_CH:CONV_CH + D]
        qb = sb("qb", [P, WA])
        g_bc = (S0[:].rearrange("p b e -> p (b e)"), qb[:])
        xres = [arena[:, 0:D], arena[:, D:2 * D], kv[:].rearrange("p a b -> p (a b)"),
                w_raw[:].rearrange("p a b c -> p (a b c)")]
        xs_res = (S0[0:NB].rearrange("p b e -> p (b e)"), qb[0:NB])
        K_TILE, V_TILE = (kv[:, 0], kv[:, 1], kv[:, 0]), (kv[:, 1], kv[:, 0], qb[:])

        PJ = ctx.enter_context(nc.psum_tensor("PJ", [P, 2, TP], F32))
        MX = ctx.enter_context(nc.psum_tensor("MX", [P, 4, TP], F32))
        MD = ctx.enter_context(nc.psum_tensor("MD", [P, 2, TP], F32))

        UTS = 3 * (LEVELS - 2) + 1
        def blocks(x, n, odd):
            return x.rearrange("p (k a s) -> p k a s", a=2, s=1 << n)[:, :, odd, :]

        def all_blocks(x, n, odd):
            return x.rearrange("p c (k a s) -> p (c k) a s", a=2, s=1 << n)[:, :, odd, :]

        def mx(n):
            return MX[:, n].rearrange("p (c d) -> p c d", c=NC)

        NAMES = """c_in g_in s_loaded adt_in x_sq x_scaled hT_ps hT_hi hT_lo vec_ps vec_sb st_ps st_sb consts w_hi_ok w_lo_dve
        w_lo_pool w_used proj_ps proj_sb        
           q_rot q_ok k_rot k_ok k_T ktok_ok k_out v_T vtok_ok v_out row_out qrow_out
        scores negmax expd probs_ok probT_ps probT_ok attn_ps z_sig z_ok gated_a stash_q stash_k stash_v stash_z
        act_chain dve_chain cw_ok crow_ps crow_ok crow_out conv_ok conv_sig kv_silu q_silu mix_T1 mix_ss
        mix_scal mix_lnrk mix_gb mix_gr mix_tok mix_kbT_ps mix_kbT mix_arg mix_D mix_kk mix_qk mix_A mix_QK mix_B
        mix_U0 mix_T_ps mix_T mix_Y_ps mix_Y mix_Z mix_UT ch_kS ch_r ch_v_ps ch_v ch_S_ps ch_o_ps ch_S ch_o1 ch_o
        o_sq o_n o_T gated_b z_sig_b z_ok_b S_out hg_ok snew_ps snew_ok qkp qb_in kb0_in kb1_in kb2_in prod red sc_T
        sc_max p_exp p_norm p_T pT_ok vb0_in vb1_in vb2_in pv_ps gated_ad dkq d_sum d_vec d_rows d_rows_ok d_vexp
        d_outer d_add S0_in S0_scaled S0_out gated_bd g_hi g_lo sq_y ss_y y_T y_out_ok y_out memset_ok
        zero_cols gates_pe gates_act gates_dve rstd_ok mix_rs on_rs d_rs d_rs2 fin_rs"""
        s = {n: sem(n) for n in NAMES.split()}
        x_in = [sem(f"x_in{c}") for c in range(NC + 1)]
        raw_in = [sem(f"w_raw_in{q}") for q in range(NQ)]

        def lo_sem(q):
            return s["w_lo_dve"] if q % 2 == 0 else s["w_lo_pool"]

        block = ctx.enter_context(nc.Block())

        @block.sync
        def _(sp):
            def wait_lo(T, q):
                sp.wait_ge(lo_sem(q), 2 * T + q // 2 + 1)

            def load_w(view, c0, T, q, n=P):
                sp.dma_start(w_raw[:, q, :, 0:n], view[:, 4 * q:4 * q + 4, bass.ds(c0, n)]).then_inc(raw_in[q], 16)

            sp.dma_start(xs_in, x_sample.rearrange("b t d -> (b t) d")).then_inc(x_in[NC], 16)
            sp.dma_start(xin[:, 0, :], x_prompt[0, 0:P, :]).then_inc(x_in[0], 16)
            sp.dma_start(ident[:], c_ident).then_inc(s["c_in"], 16)
            for n in range(2):
                sp.dma_start(g_bc[n], g_pre[0, n * WA:(n + 1) * WA].partition_broadcast(P)).then_inc(s["g_in"], 16)
            sp.dma_start(scin[0:24], state_conv[0].rearrange("b i c -> (b i) c")).then_inc(s["c_in"], 16)
            sp.dma_start(scin[24:28], conv_w[0]).then_inc(s["c_in"], 16)
            sp.dma_start(s_in[0:KT], g_post.rearrange("o (a p) -> (o a) p", p=P)).then_inc(s["c_in"], 16)
            sp.dma_start(s_in[KT:KT + 1], onorm_w).then_inc(s["c_in"], 16)
            for c in range(1, NC):
                sp.dma_start(xin[:, c, :], x_prompt[0, c * P:(c + 1) * P, :]).then_inc(x_in[c], 16)
            for q in range(NQ):
                load_w(w_in_v, 8 * WA, 0, q, 16)
            sp.dma_start(upper[:], c_upper).then_inc(s["consts"], 16)
            sp.dma_start(causal[:], c_causal).then_inc(s["consts"], 16)
            sp.dma_start(levels[:], c_levels).then_inc(s["consts"], 16)
            sp.dma_start(rotm[:], c_rot).then_inc(s["consts"], 16)
            sp.dma_start(adt[:, 0], a_log[0].partition_broadcast(P)).then_inc(s["adt_in"], 16)
            sp.dma_start(adt[:, 1], dt_bias[0].partition_broadcast(P)).then_inc(s["adt_in"], 16)
            sp.dma_start(cv_s[0, :, 0:2, :], state_conv[0, :, 1:3, :]).then_inc(s["S_out"], 16)
            for q in range(NQ):
                wait_lo(0, q)
                load_w(w_in_v, 0, 1, q)
            sp.wait_ge(s["x_sq"], NC + 1)
            sp.wait_ge(s["st_ps"], 24)
            sp.dma_start(lnmask, c_lnmask).then_inc(s["s_loaded"], 16)
            sp.dma_start(rope, c_rope).then_inc(s["s_loaded"], 16)

            def head_loads(h, T, nxt, work):
                for j in range(4):
                    for seg in range(SEGS):
                        if seg % 2 == 0 and nxt[j] is not None:
                            q = seg // 2
                            view, c0 = nxt[j]
                            wait_lo(T + j + 1, q)
                            load_w(view, c0, T + j + 2, q)
                        for g in work:
                            next(g, None)

            def cache_block(view, n):
                return (view[PAST - 128:PAST], view[PAST - 512:PAST:4], view[0:PAST:16])[n].rearrange(
                    "t h d -> t (h d)")

            def decode(b):
                vc = cache_v[0, b]
                yield from idle(8)
                sp.wait_ge(s["red"], 3 * b + 1)
                sp.dma_start(K_TILE[2], cache_block(cache_k[0, b], 2)).then_inc(s["kb2_in"], 16)
                yield from idle(4)
                sp.wait_ge(s["red"], 3 * b + 2)
                sp.dma_start(V_TILE[0], cache_block(vc, 0)).then_inc(s["vb0_in"], 16)
                yield
                sp.wait_ge(s["d_add"], 2 * b + 2)
                sp.dma_start(st_s[0, :, b].rearrange("b d e -> d b e"), S0[:]).then_inc(s["S0_out"], 16)
                yield from idle(2)
                sp.wait_ge(s["red"], 3 * b + 3)
                for n in (1, 2):
                    sp.dma_start(V_TILE[n], cache_block(vc, n)).then_inc(s[f"vb{n}_in"], 16)

            def prefetch(b):
                yield from idle(26)
                sp.wait_ge(s["qrow_out"], 16 * NH)
                if not isinstance(b, int) or b > 0:
                    sp.wait_ge(s["pv_ps"], b)
                    sp.wait_ge(s["S0_out"], 16 * b)
                kc = cache_k[0, b]
                sp.dma_start(qb[:], scratch_q[b].partition_broadcast(P)).then_inc(s["qb_in"], 16)
                for n in range(2):
                    sp.dma_start(K_TILE[n], cache_block(kc, n)).then_inc(s[f"kb{n}_in"], 16)
                sp.dma_start(S0[:], state_delta[0, :, b].rearrange("b d e -> d b e")).then_inc(s["S0_in"], 16)

            def mix_b(h):
                yield from idle(31)
                sp.wait_ge(s["ch_S"], 4 * h + 4)
                sp.dma_start(st_p[0, 0, h], S).then_inc(s["S_out"], 16)

            def loads_a(h, last=False):
                a = [(w_in_v, 2 * WA + h * HD), (w_in_v, 3 * WA + h * HD)]
                b = [(w_in_v, 5 * WA), (w_in_v, 6 * WA)] if last else \
                    [(w_in_v, (h + 1) * HD), (w_in_v, WA + (h + 1) * HD)]
                return a + b

            def loads_b(h, last=False):
                a = [(w_in_v, 4 * WA + h * HD), (w_in_v, 7 * WA + h * HD)]
                b = [(w_out_v, 0), (w_out_v, P)] if last else \
                    [(w_in_v, 5 * WA + (h + 1) * HD), (w_in_v, 6 * WA + (h + 1) * HD)]
                return a + b

            for q in range(NQ):
                wait_lo(1, q)
                load_w(w_in_v, WA, 2, q)
            with sp.Fori(0, NH - 1) as h:
                head_loads(h, 4 * h + T_A, loads_a(h), [])
            head_loads(NH - 1, T_A + 4 * (NH - 1), loads_a(NH - 1, True), [])
            head_loads(0, T_B, loads_b(0), [prefetch(0)])
            with sp.Fori(1, NH - 1) as h:
                head_loads(h, 4 * h + T_B, loads_b(h), [mix_b(h - 1), decode(h - 1), prefetch(h)])
            h = NH - 1
            head_loads(h, 4 * h + T_B, loads_b(h, True), [mix_b(h - 1), decode(h - 1), prefetch(h)])
            gens = [mix_b(h), decode(h)]
            for _ in range(40):
                for g in gens:
                    next(g, None)
            with sp.Fori(0, KT - 2) as j:
                for q in range(NQ):
                    wait_lo(j + (T_O + 1), q)
                    load_w(w_out_v, (j + 2) * P, j, q)
            sp.wait_ge(s["gated_b"], NH)
            sp.wait_ge(s["pv_ps"], NB)
            sp.wait_ge(s["S0_out"], 16 * NH)
            for i in range(2):
                sp.dma_start(xs_res[i], x_sample.rearrange("b t d -> (b t) d")[:, i * WA:(i + 1) * WA]).then_inc(
                    x_in[NC], 16)
            for c in range(NC):
                if c == 3:
                    for q in range(NQ):
                        wait_lo(T_O + KT - 1, q)
                sp.dma_start(xres[c], x_prompt[0, c * P:(c + 1) * P, :]).then_inc(x_in[c], 16)
            for c in range(NC):
                sp.wait_ge(s["y_out_ok"], 4 * (c + 1))
                sp.dma_start(y_p[0, c * P:(c + 1) * P, :], xres[c]).then_inc(s["y_out"], 16)
            sp.wait_ge(s["y_out_ok"], 4 * (NC + 1))
            for i in range(2):
                sp.dma_start(y_s.rearrange("b t d -> (b t) d")[:, i * WA:(i + 1) * WA], xs_res[i]).then_inc(
                    s["y_out"], 16)
            sp.wait_ge(s["y_out"], 16 * (NC + 2))
            sp.wait_ge(s["k_out"], 16 * NH)
            sp.wait_ge(s["row_out"], 16 * NH)
            sp.wait_ge(s["v_out"], 32 * NH)
            sp.wait_ge(s["crow_out"], 32 * 3 * NH)
            sp.wait_ge(s["S_out"], 16 * (NH + 1))
            sp.wait_ge(s["S0_out"], 16 * NH)

        @block.tensor
        def _(pe):
            def segment(T, par, half, q, first=False):
                if half == 0:
                    pe.wait_ge(lo_sem(q), 2 * T + q // 2 + 1)
                if q == 0 and not first:
                    pe.wait_ge(s["proj_sb"], 2 * T - 1 + half)
                tok = slice(half * HALF, (half + 1) * HALF)
                out = PJ[:, half, 0:HALF]
                for k in range(4 * q, 4 * q + 4):
                    wh, wl = w_hi[:, par, k, :], w_lo[:, par, k, :]
                    pe.matmul(out, wh, h_hi[:, k, tok], start=k == 0, stop=False)
                    pe.matmul(out, wh, h_lo[:, k, tok], start=False, stop=False)
                    last = pe.matmul(out, wl, h_hi[:, k, tok], start=False, stop=k == KT - 1)
                if q == NQ - 1:
                    last.then_inc(s["proj_ps"], 1)
                elif half == 1:
                    last.then_inc(s["w_used"], 1)

            def project(T, par, work, first=False):
                for half in range(2):
                    for q in range(NQ):
                        segment(T, par, half, q, first)
                        for g in work:
                            next(g, None)

            pe.wait_ge(s["c_in"], 80)
            pe.transpose(MD[:, 0, 0:KT + 1], s_in[0:KT + 1], ident[0:KT + 1, 0:KT + 1]).then_inc(s["vec_ps"], 1)
            for m in range(3 * NH):
                bank, o = m // 12, (m % 12) * 28
                pe.transpose(MX[:, 2 + bank, o:o + 28], scin[:, m * P:(m + 1) * P], ident[0:28, 0:28]).then_inc(
                    s["st_ps"], 1)
            pe.wait_ge(s["x_scaled"], 2)
            for k in range(KT):
                last = pe.transpose(MD[:, 1, k * NB:(k + 1) * NB], xs_in[:, k * P:(k + 1) * P], ident[0:NB, 0:NB])
            last.then_inc(s["hT_ps"], 1)
            for c in range(NC):
                for b in range(4):
                    if b % 2 == 0:
                        pe.wait_ge(s["x_scaled"], 2 * c + 2 + b // 2 + 1)
                    if c > 0:
                        pe.wait_ge(s["hT_lo"], 4 * (c - 1) + b + 2)
                    elif b == 2:
                        pe.wait_ge(s["st_sb"], 2)
                    for k in range(4):
                        last = pe.transpose(MX[:, b, k * P:(k + 1) * P], xin[:, c, (4 * b + k) * P:(4 * b + k + 1) * P],
                                            ident[:])
                    last.then_inc(s["hT_ps"], 1)
            pe.wait_ge(s["hT_lo"], 4 * NC + 1)

            def gates():
                yield from idle(8)
                pe.wait_ge(s["proj_sb"], 2)
                for c in range(NC):
                    pe.transpose(MD[:, 0, c * 16:(c + 1) * 16], xba[:, c * P:(c + 1) * P], ident[0:16, 0:16])
                pe.transpose(MD[0:NB, 0, 64:80], xba[:, TP:TT], ident[0:16, 0:16]).then_inc(s["gates_pe"], 1)
                yield from idle(5)
                pe.wait_ge(s["gates_dve"], 2)
                g = gw[:, 3, 0:NC, :].rearrange("p c h -> p (c h)")
                pe.matmul(MD[:, 1, 0:32], upper[:], g, start=True, stop=True)
                pe.matmul(MD[:, 1, 32:64], ones[:], g, start=True, stop=True).then_inc(s["gates_pe"], 1)
                yield from idle(3)
                pe.wait_ge(s["gates_dve"], 5)
                pe.matmul(MD[:, 0, 0:P], ones[0:NB, :], dgs.rearrange("p a h b -> p (a h b)"), start=True,
                          stop=True).then_inc(s["gates_pe"], 1)

            def own_a(h):
                yield from idle(9)
                pe.wait_ge(s["proj_sb"], 8 * h + 4)
                if not isinstance(h, int) or h > 0:
                    pe.wait_ge(s["gated_a"], h)
                for half in range(2):
                    last = pe.matmul(MX[0:2 * ROT, half, 0:HALF], rotm[:], xq[0:ROT, half * HALF:(half + 1) * HALF],
                                     start=True, stop=True)
                last.then_inc(s["q_rot"], 1)
                yield from idle(8)
                pe.wait_ge(s["proj_sb"], 8 * h + 6)
                pe.wait_ge(s["q_ok"], h + 1)
                for half in range(2):
                    last = pe.matmul(MX[0:2 * ROT, half, 0:HALF], rotm[:], xk[0:ROT, half * HALF:(half + 1) * HALF],
                                     start=True, stop=True)
                last.then_inc(s["k_rot"], 1)
                yield from idle(2)
                pe.wait_ge(s["k_ok"], h + 1)
                for c in range(NC):
                    pe.transpose(MX[:, 2, c * P:(c + 1) * P], xk[:, c * P:(c + 1) * P], ident[:])
                pe.transpose(MX[0:NB, 3, 0:P], xq[:, TP:TT], ident[:])
                pe.transpose(MX[0:NB, 3, P:2 * P], xk[:, TP:TT], ident[:]).then_inc(s["k_T"], 1)
                yield from idle(6)
                pe.wait_ge(s["proj_sb"], 8 * h + 8)
                pe.wait_ge(s["ktok_ok"], 2 * h + 2)
                for c in range(NC):
                    pe.transpose(MX[:, 2, c * P:(c + 1) * P], xv[:, c * P:(c + 1) * P], ident[:])
                pe.transpose(MX[0:NB, 3, 0:P], xv[:, TP:TT], ident[:]).then_inc(s["v_T"], 1)
                for i in range(NC):
                    if i != 1:
                        yield
                    if i == 2:
                        pe.wait_ge(s["vtok_ok"], 2 * h + 2)
                    pe.matmul(MX[:, i, 0:(i + 1) * P], xq[:, i * P:(i + 1) * P], xk[:, 0:(i + 1) * P], start=True,
                              stop=True).then_inc(s["scores"], 1)

            OFF = [0, 1, 3, 6]

            def tail_a(h):
                yield
                pe.wait_ge(s["probs_ok"], 4 * h + 4)
                for kt in range(NC):
                    bank, col = (kt, 0) if kt < 3 else (2, 2 * P)
                    for i in range(kt, NC):
                        o = (i * (i + 1) // 2 + kt) * P
                        last = pe.transpose(MX[:, bank, col + (i - kt) * P:col + (i - kt + 1) * P], probs[:, o:o + P],
                                            ident[:])
                    if kt != 2:
                        last.then_inc(s["probT_ps"], 1)
                        yield
                for kt in range(NC):
                    if kt < 3:
                        pe.wait_ge(s["probT_ok"], 3 * h + kt + 1)
                    o = sum(NC - n for n in range(kt)) * P
                    last = pe.matmul(MX[:, 3, kt * P:TP], vtok[:, kt, :], probT[:, o:o + (NC - kt) * P],
                                     start=kt == 0, stop=kt == NC - 1)
                    if kt == 1:
                        yield
                last.then_inc(s["attn_ps"], 1)

            def own_b(h):
                for j in range(3):
                    yield from idle((11, 7, 8)[j])
                    pe.wait_ge(s["proj_sb"], 8 * h + (2 * T_B + 2 * (j + 1)))
                    if j == 0 and (not isinstance(h, int) or h > 0):
                        pe.wait_ge(s["d_add"], 2 * h)
                        pe.wait_ge(s["crow_ok"], 3 * h)
                    elif j > 0:
                        pe.wait_ge(s["crow_ok"], 3 * h + j)
                    pe.transpose(MD[0:11, 1, 0:P], xq[:, 3 + TP - 3:3 + TT], ident[:]).then_inc(s["crow_ps"], 1)

            def mix_b(h):
                chunks = range(NC)
                yield
                pe.wait_ge(s["q_silu"], h + 1)
                pe.wait_ge(s["kv_silu"], 2 * h + 2)
                for c in chunks:
                    pe.transpose(mx(0)[:, c, :], xk[:, c * P:(c + 1) * P], ident[:])
                for c in chunks:
                    last = pe.transpose(mx(2)[:, c, :], cq[:, c * P:(c + 1) * P], ident[:])
                last.then_inc(s["mix_T1"], 1)
                for c in chunks:
                    last = pe.transpose(mx(1)[:, c, :], xv[:, c * P:(c + 1) * P], ident[:])
                last.then_inc(s["mix_T1"], 1)
                yield
                pe.wait_ge(s["mix_gr"], h + 1)
                pe.matmul(MX[:, 3, :], ones[:], b_B0.rearrange("p c d -> p (c d)"), start=True, stop=True).then_inc(
                    s["mix_gb"], 1)
                yield from idle(2)
                pe.wait_ge(s["mix_tok"], 3 * h + 3)
                for c in chunks:
                    last = pe.transpose(mx(0)[:, c, :], b_kb[:, c, :], ident[:])
                last.then_inc(s["mix_kbT_ps"], 1)
                yield
                pe.wait_ge(s["mix_kbT"], h + 1)
                for c in chunks:
                    last = pe.matmul(mx(1)[:, c, :], xk[:, c * P:(c + 1) * P], b_kbT[:, c, :], start=True, stop=True)
                last.then_inc(s["mix_kk"], 1)
                for c in chunks:
                    last = pe.matmul(mx(2)[:, c, :], xk[:, c * P:(c + 1) * P], cq[:, c * P:(c + 1) * P], start=True,
                                     stop=True)
                last.then_inc(s["mix_qk"], 1)
                yield from idle(2)
                pe.wait_ge(s["mix_U0"], h + 1)
                for c in chunks:
                    last = pe.transpose(mx(0)[:, c, :], b_U[:, c, :], ident[:])
                last.then_inc(s["mix_T_ps"], 1)
                for n in range(1, LEVELS):
                    yield
                    pe.wait_ge(s["mix_B"], LEVELS * h + n + 1)
                    if n == 1:
                        pe.wait_ge(s["mix_T"], h + 1)
                        pe.wait_ge(s["mix_A"], h + 1)
                    else:
                        pe.wait_ge(s["mix_UT"], UTS * h + 3 * (n - 1) - 1)
                    for c in chunks:
                        last = pe.matmul(blocks(mx(1)[:, c, :], n, 0), b_B[n % 2][:, c, :],
                                         blocks(b_T[:, c, :], n, 0), start=True, stop=True)
                    last.then_inc(s["mix_Y_ps"], 1)
                    yield
                    pe.wait_ge(s["mix_Y"], (LEVELS - 1) * h + n)
                    if n == 1:
                        pe.wait_ge(s["mix_QK"], h + 1)
                    else:
                        pe.wait_ge(s["mix_UT"], UTS * h + 3 * (n - 1))
                    for c in chunks:
                        last = pe.matmul(blocks(mx(2)[:, c, :], n, 1), b_Y[:, c, :], blocks(b_U[:, c, :], n, 1),
                                         start=True, stop=True)
                    last.then_inc(s["mix_Z"], 1)
                    if n < LEVELS - 1:
                        for c in chunks:
                            last = pe.matmul(blocks(mx(3)[:, c, :], n, 0), b_U[:, c, :],
                                             blocks(b_Y[:, c, :], n, 0), start=True, stop=True)
                        last.then_inc(s["mix_Z"], 1)
                for c in chunks:
                    if c > 0:
                        yield
                        pe.wait_ge(s["ch_S"], NC * h + c)
                        pe.matmul(MX[:, 0, 0:P], b_kbT[:, c, :], S, start=True, stop=True).then_inc(s["ch_kS"], 1)
                        if c > 1:
                            pe.wait_ge(s["ch_o1"], (NC - 1) * h + c - 1)
                        pe.matmul(MX[:, 1, 0:P], cq[:, c * P:(c + 1) * P], S, start=True, stop=True).then_inc(
                            s["ch_o_ps"], 1)
                    yield
                    if c == 0:
                        pe.wait_ge(s["mix_UT"], UTS * h + UTS)
                    pe.wait_ge(s["ch_r"], NC * h + c + 1)
                    pe.matmul(MX[:, 2, 0:P], b_U[:, c, :], rr, start=True, stop=True).then_inc(s["ch_v_ps"], 1)
                    yield
                    pe.wait_ge(s["ch_v"], NC * h + c + 1)
                    pe.matmul(MX[:, 0, 0:P], b_kdec[:, c, :], vn, start=True, stop=True).then_inc(s["ch_S_ps"], 1)
                    if c > 0:
                        pe.wait_ge(s["ch_o"], NC * h + c)
                    pe.matmul(MX[:, 3, 0:P], b_QK[:, c, :], vn, start=True, stop=True).then_inc(s["ch_o_ps"], 1)
                yield
                pe.wait_ge(s["o_n"], h + 1)
                for c in chunks:
                    last = pe.transpose(mx(0)[:, c, :], b_o[:, c, :], ident[:])
                last.then_inc(s["o_T"], 1)

            def new_scores():
                pe.wait_ge(s["qkp"], 1)
                pe.wait_ge(s["gates_act"], 5)
                for b in range(NB):
                    last = pe.matmul(MD[0:NH, 0, b:b + 1], qks[:, :, b], ones[:, 0:1], start=True, stop=True)
                last.then_inc(s["snew_ps"], 1)
                yield

            def delta_decode(h):
                yield from idle(2)
                pe.wait_ge(s["dkq"], h + 1)
                pe.wait_ge(s["S0_in"], 16 * h + 16)
                pe.wait_ge(s["crow_ok"], 3 * h + 3)
                pe.matmul(MD[:, 1, 0:24], ones[:], dd[:, 2:5, :].rearrange("p a b -> p (a b)"), start=True, stop=True)
                for b in range(NB):
                    last = pe.matmul(MD[:, 1, 32 + 2 * b:34 + 2 * b], S0[:, b, :], dd[:, 0:2, b], start=True,
                                     stop=True)
                last.then_inc(s["d_sum"], 1)
                yield from idle(3)
                pe.wait_ge(s["d_vec"], h + 1)
                pe.transpose(MD[0:NB, 1, 0:P], dd[:, 5, :], ident[:])
                pe.transpose(MD[0:NB, 1, P:2 * P], dd[:, 6, :], ident[:])
                pe.matmul(MD[:, 1, 2 * P:2 * P + NB], ones[:], dd[:, 8, :], start=True, stop=True).then_inc(
                    s["d_rows"], 1)
                yield from idle(2)
                for n in range(2):
                    yield
                    pe.wait_ge(s["d_vexp"], 2 * h + n + 1)
                    if n == 0:
                        pe.wait_ge(s["d_rows_ok"], h + 1)
                        pe.wait_ge(s["gated_bd"], h + 1)
                    else:
                        yield
                        pe.wait_ge(s["d_add"], 2 * h + 1)
                    pe.matmul(MD[:, 1, :], kvr[:, 0, :], vexp.rearrange("p b e -> p (b e)"), start=True,
                              stop=True).then_inc(s["d_outer"], 1)

            def attn_decode(b):
                yield from idle(17)
                pe.wait_ge(s["red"], 3 * b + 3)
                for n in range(3):
                    last = pe.transpose(MD[0:NH, 0, n * P:(n + 1) * P], sc[:, n, :], ident[:])
                last.then_inc(s["sc_T"], 1)
                yield from idle(4)
                pe.wait_ge(s["p_norm"], b + 1)
                pe.matmul(MD[:, 0, 3 * NH:4 * NH], ones[0:NH, :], dg[:], start=True, stop=True)
                for n in range(3):
                    last = pe.transpose(MD[:, 0, n * NH:(n + 1) * NH], pd[:, n, :], ident[0:NH, 0:NH])
                last.then_inc(s["p_T"], 1)
                yield
                pe.wait_ge(s["pT_ok"], b + 1)
                for n in range(3):
                    pe.wait_ge(s[f"vb{n}_in"], 16 * b + 16)
                for hh in range(NH):
                    if hh > 0 and hh % 2 == 0:
                        yield
                    for n in range(3):
                        v = V_TILE[n]
                        last = pe.matmul(MD[:, 0, 64 + hh:65 + hh], v[:, hh * HD:(hh + 1) * HD], pT[:, n, hh:hh + 1],
                                         start=n == 0, stop=n == 2)
                last.then_inc(s["pv_ps"], 1)

            pe.wait_ge(s["consts"], 64)
            pe.wait_ge(s["memset_ok"], 1)
            project(0, 0, [], first=True)
            ga = gates()
            first_a = own_a(0)
            for j in range(4):
                project(T_A + j, (1 + j) % 2, [ga, first_a])
            with pe.Fori(1, NH) as h:
                work = [tail_a(h - 1), own_a(h)]
                for j in range(4):
                    project(4 * h + (T_A + j), (1 + j) % 2, work)
            work = [tail_a(NH - 1), own_b(0), new_scores()]
            for j in range(4):
                project(T_B + j, (1 + j) % 2, work)
            pe.wait_ge(s["gated_a"], NH)
            pe.wait_ge(s["snew_ok"], 1)
            with pe.Fori(1, NH) as h:
                work = [mix_b(h - 1), delta_decode(h - 1), own_b(h), attn_decode(h - 1)]
                for j in range(4):
                    project(4 * h + (T_B + j), (1 + j) % 2, work)
            work = [mix_b(NH - 1), delta_decode(NH - 1), attn_decode(NH - 1)]
            for _ in range(40):
                for g in work:
                    next(g, None)
            pe.wait_ge(s["g_lo"], KT)
            with pe.Fori(0, KT // 2) as i:
                for n in range(2):
                    project(2 * i + (T_O + n), (1 + n) % 2, [])
            pe.wait_ge(s["sq_y"], 2 * KT)
            for c in range(NC + 1):
                n = P if c < NC else NB
                last = pe.matmul(MD[0:n, 0, c:c + 1], acc[:, c * P:c * P + n], ones[:, 0:1], start=True, stop=True)
            last.then_inc(s["ss_y"], 1)
            pe.wait_ge(s["proj_sb"], 2 * (T_O + KT))
            for c in range(NC + 1):
                n = P if c < NC else NB
                for b in range(4):
                    if c > 0:
                        pe.wait_ge(s["y_out_ok"], 4 * (c - 1) + b + 1)
                    for k in range(4):
                        last = pe.transpose(MX[0:n, b, k * P:(k + 1) * P], gated[:, 4 * b + k, c * P:c * P + n],
                                            ident[:])
                    last.then_inc(s["y_T"], 1)

        @block.scalar
        def _(act):
            ch = Chain(act, s["act_chain"])

            def hi(T, par, q, n=P, first=False):
                act.wait_ge(raw_in[q], 16 * T + 16)
                if not first:
                    if q < NQ - 1:
                        act.wait_ge(s["w_used"], 3 * T - 6 + q + 1)
                    else:
                        act.wait_ge(s["proj_ps"], 2 * T - 2)
                act.activation(w_hi[:, par, 4 * q:4 * q + 4, 0:n], w_raw[:, q, :, 0:n], ACT.Copy).then_inc(
                    s["w_hi_ok"], 1)

            def rsqrt(out, in_, scale, ok):
                ch.link(act.activation(out, in_, ACT.Ln, scale=scale, bias=EPS))
                act.activation(out, out, ACT.Exp, scale=-0.5).then_inc(ok, 1)

            def sigmoid(out, in_, ok):
                ch.link(act.activation(out, in_, ACT.Exp, scale=-1.0))
                ch.link(act.activation(out, out, ACT.Ln, bias=1.0))
                act.activation(out, out, ACT.Exp, scale=-1.0).then_inc(ok, 1)

            def copy_out(T, half, dst, off=0):
                act.wait_ge(s["proj_ps"], 2 * T + half + 1)
                o = off + half * HALF
                n = dst.shape[0]
                act.activation(dst[:, o:o + HALF], PJ[0:n, half, 0:HALF], ACT.Copy).then_inc(s["proj_sb"], 1)

            def head(T, dsts, before, work, guards):
                for j in range(4):
                    for seg in range(SEGS):
                        if seg == 0:
                            dst, off = before if j == 0 else dsts[j - 1]
                            if dst is not None:
                                copy_out(T + (j - 1), 1, dst, off)
                        if seg == 4:
                            guards(j)
                            copy_out(T + j, 0, dsts[j][0][:], dsts[j][1])
                        for g in work:
                            next(g, None)
                        if seg % 2 == 0:
                            hi(T + (j + 1), j % 2, seg // 2)

            A_DST = [(xq[:], 0), (xk[:], 0), (xv[:], 0), (xz[:], 0)]
            B_DST = [(xq[:], 3), (xq[:], 3), (xq[:], 3), (xz[:], 0)]

            def guards_a(h):
                def guard(j):
                    if isinstance(h, int) and h == 0:
                        return
                    if j == 0:
                        act.wait_ge(s["scores"], 4 * h)
                        act.wait_ge(s["stash_q"], h)
                        act.wait_ge(s["stash_k"], h)
                    if j == 2:
                        act.wait_ge(s["stash_v"], h)
                    if j == 3:
                        act.wait_ge(s["z_ok"], h)
                return guard

            def guards_b(h):
                def guard(j):
                    if isinstance(h, int) and h == 0 and j == 0:
                        act.wait_ge(s["scores"], 4 * NH)
                        act.wait_ge(s["stash_q"], NH)
                        act.wait_ge(s["zero_cols"], 1)
                    elif j == 0:
                        act.wait_ge(s["conv_ok"], 3 * h)
                        act.wait_ge(s["crow_ps"], 3 * h)
                    if j in (1, 2):
                        act.wait_ge(s["conv_ok"], 3 * h + j)
                        act.wait_ge(s["crow_ps"], 3 * h + j)
                    if j == 3:
                        if isinstance(h, int) and h == 0:
                            act.wait_ge(s["z_ok"], NH)
                        else:
                            act.wait_ge(s["z_ok_b"], h)
                return guard

            act.preload_act_table_set("natural_log_exp_and_others")
            def x_rstd(n, c):
                rows_ = P if c < NC else NB
                act.wait_ge(x_in[c], 16)
                if n > 0:
                    act.wait_ge(s["x_sq"], n)
                act.activation(junk[0:rows_], xin[:, c, :] if c < NC else xs_in, ACT.Square,
                               accum_out=ssum[0:rows_, c:c + 1]).then_inc(s["x_sq"], 1)
                act.wait_ge(s["x_sq"], n + 1)
                rsqrt(rstd[0:rows_, c:c + 1], ssum[0:rows_, c:c + 1], 1.0 / D, s["rstd_ok"])

            def x_hi(c):
                for b in range(4):
                    act.wait_ge(s["hT_ps"], 4 * c + b + 2)
                    act.activation(h_hi[:, 4 * b:4 * b + 4, c * P:(c + 1) * P],
                                   MX[:, b].rearrange("p (k t) -> p k t", k=4), ACT.Copy).then_inc(s["hT_hi"], 1)

            x_rstd(0, NC)
            x_rstd(1, 0)
            act.wait_ge(s["vec_ps"], 1)
            act.activation(vecT[:], MD[:, 0, 0:KT + 1], ACT.Copy).then_inc(s["vec_sb"], 1)
            for m in range(2):
                act.wait_ge(s["st_ps"], 12 * m + 12)
                act.activation(stT[:, 12 * m:12 * m + 12, :].rearrange("p m w -> p (m w)"), MX[:, 2 + m, 0:336],
                               ACT.Copy).then_inc(s["st_sb"], 1)
            act.wait_ge(s["hT_ps"], 1)
            act.activation(h_hi[:, :, TP:TT], MD[:, 1, 0:P].rearrange("p (k b) -> p k b", k=KT), ACT.Copy).then_inc(
                s["hT_hi"], 1)
            x_rstd(2, 1)
            x_hi(0)
            x_rstd(3, 2)
            x_hi(1)
            x_rstd(4, 3)
            x_hi(2)
            x_hi(3)
            act.wait_ge(s["memset_ok"], 1)
            for q in range(NQ):
                hi(0, 0, q, 16, first=True)

            def gates():
                yield from idle(8)
                act.wait_ge(s["gates_pe"], 1)
                act.activation(gt[:, 0:NC].rearrange("p c a h -> p (c a h)"), MD[:, 0, 0:64], ACT.Copy)
                act.activation(gt[0:NB, NC].rearrange("p a h -> p (a h)"), MD[0:NB, 0, 64:80], ACT.Copy).then_inc(
                    s["gates_act"], 1)
                yield from idle(1)
                act.wait_ge(s["gates_dve"], 1)
                ch.link(act.activation(gw[:, 0], gt[:, :, 0, :], ACT.Exp, scale=-1.0))
                ch.link(act.activation(gw[:, 2], gw[:, 1], ACT.Exp, scale=-1.0))
                act.activation(gw[:, 2], gw[:, 2], ACT.Ln, bias=1.0)
                act.wait_ge(s["adt_in"], 32)
                act.activation(gneg[:], adt[:, 0], ACT.Exp).then_inc(s["gates_act"], 1)
                yield from idle(3)
                act.wait_ge(s["gates_pe"], 2)
                cum = MD[:, 1, 0:32].rearrange("p (c h) -> p c h", c=NC)
                act.activation(G6[:, 1], cum, ACT.Copy)
                act.activation(G6[:, 3], cum, ACT.Exp)
                act.activation(G6[:, 5], MD[:, 1, 32:64].rearrange("p (c h) -> p c h", c=NC), ACT.Exp)
                act.activation(gw[0:NB, 0, NC, :], gw[0:NB, 3, NC, :], ACT.Exp).then_inc(s["gates_act"], 1)
                yield
                act.wait_ge(s["gates_dve"], 3)
                act.activation(G6[:, 4], G6[:, 4], ACT.Exp).then_inc(s["gates_act"], 1)
                yield from idle(2)
                act.wait_ge(s["gates_pe"], 3)
                act.activation(bgs[:].rearrange("p a h b -> p (a h b)"), MD[:, 0, 0:P], ACT.Copy).then_inc(
                    s["gates_act"], 1)

            def own_a(h):
                first = isinstance(h, int) and h == 0
                yield from idle(19)
                act.wait_ge(s["k_T"], h + 1)
                if not first:
                    act.wait_ge(s["k_out"], 16 * h)
                    act.wait_ge(s["row_out"], 16 * h)
                    act.wait_ge(s["qrow_out"], 16 * h)
                act.activation(ktok, mx(2), ACT.Copy).then_inc(s["ktok_ok"], 1)
                act.activation(qkrow.rearrange("p a d -> p (a d)"), MX[0:NB, 3, 0:2 * P], ACT.Copy).then_inc(
                    s["ktok_ok"], 1)
                yield
                act.wait_ge(s["ktok_ok"], 2 * h + 2)
                act.dma_start(kp_v[:, :, h, :], ktok).then_inc(s["k_out"], 16)
                act.dma_start(scratch_q[:, bass.ds(h * HD, HD)], qkrow[:, 0]).then_inc(s["qrow_out"], 16)
                act.dma_start(wk_s[0, :, 0, h, :], qkrow[:, 1]).then_inc(s["row_out"], 16)
                yield from idle(5)
                act.wait_ge(s["v_T"], h + 1)
                if not first:
                    act.wait_ge(s["v_out"], 32 * h)
                    act.wait_ge(s["attn_ps"], h)
                act.activation(vtok, mx(2), ACT.Copy).then_inc(s["vtok_ok"], 1)
                act.activation(vrow, MX[0:NB, 3, 0:P], ACT.Copy).then_inc(s["vtok_ok"], 1)
                yield
                act.wait_ge(s["vtok_ok"], 2 * h + 2)
                act.dma_start(vp_v[:, :, h, :], vtok).then_inc(s["v_out"], 16)
                act.dma_start(wv_s[0, :, 0, h, :], vrow).then_inc(s["v_out"], 16)
                yield from idle(3)
                act.wait_ge(s["negmax"], h + 1)
                for i in range(NC):
                    p = probs[:, i * (i + 1) // 2 * P:(i + 1) * (i + 2) // 2 * P]
                    act.activation(p, p, ACT.Exp, bias=stat[:, 0, i:i + 1], accum_out=stat[:, 1, i:i + 1]).then_inc(
                        s["expd"], 1)

            def tail_a(h):
                yield
                act.wait_ge(s["proj_sb"], 8 * h + 2 * T_A + 8)
                act.wait_ge(s["k_ok"], h + 1)
                sigmoid(ez[:], xz[:], s["z_sig"])
                for n, (o, w) in enumerate(((0, 4), (4, 3), (7, 3))):
                    act.wait_ge(s["probT_ps"], 3 * h + n + 1)
                    act.activation(probT[:, o * P:(o + w) * P], MX[:, n, 0:w * P], ACT.Copy).then_inc(
                        s["probT_ok"], 1)
                    yield

            def own_b(h):
                for j, m in enumerate((1, 2, 0)):
                    yield from idle((11, 6, 7)[j])
                    act.wait_ge(s["crow_ps"], 3 * h + j + 1)
                    if j > 0 or not isinstance(h, int) or h > 0:
                        act.wait_ge(s["crow_out"], 32 * (3 * h + j))
                    act.activation(rows, MD[0:11, 1, 0:P], ACT.Copy).then_inc(s["crow_ok"], 1)
                    yield
                    act.wait_ge(s["conv_ok"], 3 * h + j + 1)
                    if j == 0:
                        act.wait_ge(s["z_ok"], NH)
                        if not isinstance(h, int) or h > 0:
                            act.wait_ge(s["z_ok_b"], h)
                    else:
                        act.wait_ge(s["kv_silu"], 2 * h + j)
                    sigmoid(ez[:], acc[:], s["conv_sig"])
                    act.wait_ge(s["crow_ok"], 3 * h + j + 1)
                    act.dma_start(cv_p[0, 0, :, bass.ds((h + m * NH) * P, P)], rows[0:3]).then_inc(s["crow_out"], 16)
                    act.dma_start(cv_s[0, :, 2, bass.ds((h + m * NH) * P, P)], rows[3:11]).then_inc(
                        s["crow_out"], 16)

            def mix_b(h):
                yield
                act.wait_ge(s["q_silu"], h + 1)
                act.wait_ge(s["mix_T1"], 2 * h + 1)
                for n, x in enumerate((0, 2)):
                    for c in range(NC):
                        act.activation((b_o, b_Y)[n][:, c, :], mx(x)[:, c, :], ACT.Square,
                                       accum_out=sk[:, n, c:c + 1]).then_inc(s["mix_ss"], 1)
                yield
                act.wait_ge(s["mix_ss"], 2 * NC * h + 2 * NC)
                ch.link(act.activation(lnss[:], sk[:, 0:2, :], ACT.Ln, bias=EPS))
                act.activation(lnrk[:], lnss[:, 0, :], ACT.Copy, scale=-0.5).then_inc(s["mix_lnrk"], 1)
                act.activation(sk[:, 0:2, :], lnss[:], ACT.Exp, scale=-0.5).then_inc(s["mix_rs"], 1)
                yield
                act.wait_ge(s["mix_arg"], h + 1)
                act.wait_ge(s["mix_lnrk"], h + 1)
                for c in range(NC):
                    act.activation(b_D[:, c, :], b_D[:, c, :], ACT.Exp, bias=lnrk[:, c:c + 1]).then_inc(s["mix_D"], 1)
                yield
                act.wait_ge(s["mix_kbT_ps"], h + 1)
                act.activation(b_kbT, mx(0), ACT.Copy).then_inc(s["mix_kbT"], 1)
                yield
                act.wait_ge(s["proj_sb"], 8 * h + 2 * T_B + 8)
                sigmoid(ez[:], xz[:], s["z_sig_b"])
                yield from idle(2)
                act.wait_ge(s["mix_T_ps"], h + 1)
                act.activation(b_T, mx(0), ACT.Copy).then_inc(s["mix_T"], 1)
                for n in range(1, LEVELS):
                    yield
                    act.wait_ge(s["mix_Y_ps"], (LEVELS - 1) * h + n)
                    act.activation(all_blocks(b_Y, n, 0), all_blocks(mx(1), n, 0), ACT.Copy).then_inc(s["mix_Y"], 1)
                    yield
                for c in range(NC):
                    if c > 0:
                        yield
                        act.wait_ge(s["ch_o_ps"], (2 * NC - 1) * h + 2 * c)
                        act.wait_ge(s["o_sq"], NC * h + c)
                        act.activation(o1, MX[:, 1, 0:P], ACT.Copy, scale=oq[:, c:c + 1]).then_inc(s["ch_o1"], 1)
                    yield
                    act.wait_ge(s["ch_v_ps"], NC * h + c + 1)
                    act.activation(vn, MX[:, 2, 0:P], ACT.Copy).then_inc(s["ch_v"], 1)
                    yield
                    act.wait_ge(s["ch_o"], NC * h + c + 1)
                    act.activation(o1, b_o[:, c, :], ACT.Square, accum_out=on[:, 0, c:c + 1]).then_inc(
                        s["o_sq"], 1)
                act.wait_ge(s["o_sq"], NC * h + NC)
                rsqrt(on[:, 1, :], on[:, 0, :], 1.0 / HD, s["on_rs"])

            def delta_decode(h):
                yield from idle(2)
                act.wait_ge(s["d_sum"], h + 1)
                rsqrt(dd[:, 9:11, :], MD[:, 1, 0:2 * NB].rearrange("p (a b) -> p a b", a=2), 1.0, s["d_rs"])
                yield from idle(3)
                act.wait_ge(s["d_rows"], h + 1)
                rsqrt(dd[:, 10, :], MD[:, 1, 2 * P:2 * P + NB], 1.0 / HD, s["d_rs2"])
                act.activation(kvr.rearrange("p a d -> p (a d)"), MD[0:NB, 1, 0:2 * P], ACT.Copy).then_inc(
                    s["d_rows_ok"], 1)

            def attn_decode(b):
                yield from idle(18)
                act.wait_ge(s["sc_max"], b + 1)
                act.activation(pd.rearrange("p a t -> p (a t)"), MD[0:NH, 0, 0:3 * P], ACT.Exp, bias=ds[:, 1:2],
                               scale=SCALE, accum_out=ds[:, 3:4])
                act.activation(ds[:, 4:5], ds[:, 2:3], ACT.Exp).then_inc(s["p_exp"], 1)
                yield from idle(3)
                act.wait_ge(s["p_T"], b + 1)
                act.activation(pT[:].rearrange("p a h -> p (a h)"), MD[:, 0, 0:4 * NH], ACT.Copy).then_inc(
                    s["pT_ok"], 1)

            for seg in range(SEGS):
                if seg % 2 == 0:
                    hi(1, 1, seg // 2, first=True)
                if seg == 4:
                    copy_out(0, 0, xba)
            ga, first_a = gates(), own_a(0)
            head(T_A, A_DST, (xba, 0), [ga, first_a], guards_a(0))
            ch.end(1)
            with act.Fori(1, NH) as h:
                ch.at(h, 1, 2)
                head(4 * h + T_A, A_DST, A_DST[3], [tail_a(h - 1), own_a(h)], guards_a(h))
            ch.end(NH - 1)
            head(T_B, B_DST, A_DST[3], [tail_a(NH - 1), own_b(0)], guards_b(0))
            ch.end(1)
            act.wait_ge(s["gated_a"], NH)
            act.wait_ge(s["k_out"], 16 * NH)
            act.wait_ge(s["v_out"], 32 * NH)
            with act.Fori(1, NH) as h:
                ch.at(h, 1, 12)
                head(4 * h + T_B, B_DST, B_DST[3],
                     [mix_b(h - 1), own_b(h), delta_decode(h - 1), attn_decode(h - 1)], guards_b(h))
            ch.end(NH - 1)
            copy_out(T_O - 1, 1, xz[:])
            work = [mix_b(NH - 1), delta_decode(NH - 1), attn_decode(NH - 1)]
            for n in range(40):
                for g in work:
                    next(g, None)
            act.wait_ge(s["gated_a"], NH)
            act.wait_ge(s["gated_ad"], NB)
            act.wait_ge(s["gated_b"], NH)
            act.wait_ge(s["gated_bd"], NH)
            for k in range(KT):
                act.activation(h_hi[:, k, :], gated[:, k, :], ACT.Copy).then_inc(s["g_hi"], 1)
            act.wait_ge(s["g_lo"], KT)
            with act.Fori(0, KT // 2 - 1) as i:
                for n in range(2):
                    T = 2 * i + (T_O + n)
                    for seg in range(SEGS):
                        if seg % 2 == 0:
                            hi(T + 1, n, seg // 2)
            T = T_O + KT - 2
            for q in range(NQ):
                hi(T + 1, 0, q)
            ch.end(1)
            act.wait_ge(s["fin_rs"], 1)
            rsqrt(fin[:], fin[:], 1.0 / D, s["fin_rs"])

        @block.vector
        def _(dve):
            ch = Chain(dve, s["dve_chain"])
            link = ch.link

            def lo(T, par, q, n=P):
                dve.wait_ge(s["w_hi_ok"], 4 * T + q + 1)
                dve.tensor_tensor(w_lo[:, par, 4 * q:4 * q + 4, 0:n], w_raw[:, q, :, 0:n],
                                  w_hi[:, par, 4 * q:4 * q + 4, 0:n].bitcast(F32), ALU.subtract).then_inc(
                    s["w_lo_dve"], 1)

            def head(T, work):
                for j in range(4):
                    for seg in range(SEGS):
                        for g in work:
                            next(g, None)
                        if seg % 4 == 0:
                            lo(T + (j + 1), j % 2, seg // 2)

            dve.memset(gt, 0.0)
            dve.memset(ones[:], 1.0)
            dve.memset(w_hi[:, 0, :, :].bitcast(F32), 0.0)
            dve.memset(w_lo[:, 0, :, :].bitcast(F32), 0.0).then_inc(s["memset_ok"], 1)

            def x_scale(n, c):
                rows_ = P if c < NC else NB
                x = xin[:, c, :] if c < NC else xs_in
                dve.wait_ge(s["rstd_ok"], n + 1)
                dve.wait_ge(s["g_in"], 32)
                for i in range(2):
                    xh = x[:, i * WA:(i + 1) * WA]
                    dve.scalar_tensor_tensor(xh, xh, rstd[0:rows_, c:c + 1], g_bc[i][0:rows_], ALU.mult,
                                             ALU.mult).then_inc(s["x_scaled"], 1)

            def x_lo(c):
                for b in range(4):
                    dve.wait_ge(s["hT_hi"], 4 * c + b + 2)
                    part = (slice(None), slice(4 * b, 4 * b + 4), slice(c * P, (c + 1) * P))
                    dve.tensor_tensor(h_lo[part], MX[:, b].rearrange("p (k t) -> p k t", k=4),
                                      h_hi[part].bitcast(F32), ALU.subtract).then_inc(s["hT_lo"], 1)

            x_scale(0, NC)
            x_scale(1, 0)
            dve.wait_ge(s["hT_hi"], 1)
            dve.tensor_tensor(h_lo[:, :, TP:TT], MD[:, 1, 0:P].rearrange("p (k b) -> p k b", k=KT),
                              h_hi[:, :, TP:TT].bitcast(F32), ALU.subtract).then_inc(s["hT_lo"], 1)
            x_scale(2, 1)
            x_lo(0)
            x_scale(3, 2)
            x_lo(1)
            x_scale(4, 3)
            x_lo(2)
            x_lo(3)
            for q in (0, 2):
                lo(0, 0, q, 16)

            def gates():
                yield from idle(8)
                dve.wait_ge(s["gates_act"], 1)
                dve.wait_ge(s["adt_in"], 32)
                a = gt[:, :, 1, :]
                dtb = adt[:, 1].unsqueeze(1).to_broadcast((P, NC + 1, NH))
                link(dve.tensor_tensor(a, a, dtb, ALU.add))
                link(dve.tensor_scalar(gw[:, 1], a, -1.0, None, ALU.mult))
                dve.tensor_tensor(gw[:, 1], gw[:, 1], a, ALU.max).then_inc(s["gates_dve"], 1)
                yield
                yield
                dve.wait_ge(s["gates_act"], 2)
                link(dve.tensor_scalar(gw[:, 0], gw[:, 0], 1.0, None, ALU.add))
                link(dve.reciprocal(gw[:, 0], gw[:, 0]))
                link(dve.tensor_scalar(a, a, 0.0, None, ALU.max))
                link(dve.tensor_tensor(a, a, gw[:, 2], ALU.add))
                link(dve.tensor_scalar(gneg[:], gneg[:], -1.0, None, ALU.mult))
                dve.tensor_copy(G6[:, 0], gw[:, 0, 0:NC, :])
                ident8 = ident[0:NB, 0:NB].unsqueeze(1).to_broadcast((NB, NH, NB))
                link(dve.tensor_tensor(dgs[:, 0], gw[0:NB, 0, NC, :].unsqueeze(2).to_broadcast((NB, NH, NB)), ident8,
                                       ALU.mult))
                dve.tensor_tensor(gw[:, 3], a, gneg[:].unsqueeze(1).to_broadcast((P, NC + 1, NH)),
                                  ALU.mult).then_inc(s["gates_dve"], 1)
                yield from idle(3)
                dve.wait_ge(s["gates_act"], 3)
                tot = MD[:, 1, 32:64].rearrange("p (c h) -> p c h", c=NC)
                dve.tensor_tensor(G6[:, 4], tot, G6[:, 1], ALU.subtract).then_inc(s["gates_dve"], 1)
                dve.tensor_scalar(G6[:, 2], G6[:, 3], -1.0, None, ALU.mult).then_inc(s["gates_dve"], 1)
                dve.tensor_tensor(dgs[:, 1], gw[0:NB, 0, NC, :].unsqueeze(2).to_broadcast((NB, NH, NB)), ident8,
                                  ALU.mult).then_inc(s["gates_dve"], 1)

            def rope_on(x, ps_ready, n, ok):
                t1, t2 = acc[0:ROT, :], ez[0:ROT, :]
                dve.wait_ge(ps_ready, n)
                link(dve.tensor_tensor(t1, x[0:ROT, 0:TT], rope[:, 0, :], ALU.mult))
                link(dve.tensor_tensor(t2.rearrange("p (a t) -> p a t", a=2), MX[0:ROT, 0:2, 0:HALF],
                                       rope[:, 1, :].rearrange("p (a t) -> p a t", a=2), ALU.mult))
                dve.tensor_tensor(x[0:ROT, 0:TT], t1, t2, ALU.add).then_inc(ok, 1)

            def own_a(h):
                first = isinstance(h, int) and h == 0
                yield from idle(9)
                rope_on(xq, s["q_rot"], h + 1, s["q_ok"])
                yield from idle(8)
                rope_on(xk, s["k_rot"], h + 1, s["k_ok"])
                yield from idle(9)
                for i in range(NC):
                    if i >= 2:
                        yield
                    p = probs[:, i * (i + 1) // 2 * P:(i + 1) * (i + 2) // 2 * P]
                    dve.wait_ge(s["scores"], NC * h + i + 1)
                    if i == 0 and not first:
                        dve.wait_ge(s["probT_ps"], 3 * h)
                    link(dve.scalar_tensor_tensor(p, MX[:, i, 0:(i + 1) * P], SCALE, lnmask[:, (NC - 1 - i) * P:TP],
                                                  ALU.mult, ALU.add))
                    link(dve.tensor_reduce(stat[:, 0, i:i + 1], p, AX.X, ALU.max))
                dve.tensor_scalar(stat[:, 0, :], stat[:, 0, :], -1.0, None, ALU.mult).then_inc(s["negmax"], 1)
                yield
                yield
                dve.wait_ge(s["expd"], NC * h + NC)
                link(dve.reciprocal(stat[:, 2, :], stat[:, 1, :]))
                for i in range(NC):
                    p = probs[:, i * (i + 1) // 2 * P:(i + 1) * (i + 2) // 2 * P]
                    dve.tensor_scalar(p, p, stat[:, 2, i:i + 1], None, ALU.mult).then_inc(s["probs_ok"], 1)

            def tail_a(h):
                yield from idle(2)
                dve.wait_ge(s["z_sig"], h + 1)
                dve.wait_ge(s["stash_v"], h + 1)
                dve.tensor_tensor(sz[:], xz[:], ez[:], ALU.mult).then_inc(s["z_ok"], 1)
                yield from idle(3)
                dve.wait_ge(s["z_ok"], h + 1)
                dve.wait_ge(s["attn_ps"], h + 1)
                dve.tensor_tensor(gated[:, h, 0:TP], MX[:, 3, :], sz[:, 0:TP], ALU.mult).then_inc(s["gated_a"], 1)

            def own_b(h):
                first = isinstance(h, int) and h == 0
                for j, m in enumerate((1, 2, 0)):
                    yield from idle((10, 5, 6)[j])
                    dve.wait_ge(s["proj_sb"], 8 * h + (2 * T_B + 2 * (j + 1)))
                    if j == 0:
                        dve.wait_ge(s["cw_ok"], h + 1)
                        if not first:
                            dve.wait_ge(s["q_silu"], h)
                    else:
                        dve.wait_ge(s["kv_silu"], 2 * h + j)
                    w = cw[:, m, :]
                    link(dve.tensor_scalar(acc[:, 0:TP], xq[:, 0:TP], w[:, 24:25], None, ALU.mult))
                    for i in range(1, CW):
                        link(dve.scalar_tensor_tensor(acc[:, 0:TP], xq[:, i:i + TP], w[:, 24 + i:25 + i],
                                                      acc[:, 0:TP], ALU.mult, ALU.add))
                    st = w[:, 0:24].rearrange("p (b i) -> p b i", i=3)
                    link(dve.tensor_scalar(acc[:, TP:TT], st[:, :, 0], w[:, 24:25], None, ALU.mult))
                    for i in range(1, CW):
                        src = st[:, :, i] if i < 3 else xq[:, 3 + TP:3 + TT]
                        ins = dve.scalar_tensor_tensor(acc[:, TP:TT], src, w[:, 24 + i:25 + i], acc[:, TP:TT],
                                                       ALU.mult, ALU.add)
                        if i < 3:
                            link(ins)
                    ins.then_inc(s["conv_ok"], 1)
                    yield from idle(2)
                    if j < 2:
                        dve.wait_ge(s["conv_sig"], 3 * h + j + 1)
                    if j < 2:
                        if j == 0 and not first:
                            dve.wait_ge(s["mix_qk"], h)
                        if j == 0 and first:
                            dve.wait_ge(s["scores"], NC * NH)
                            dve.wait_ge(s["stash_k"], NH)
                        if j == 1 and not first:
                            dve.wait_ge(s["mix_T1"], 2 * h)
                        if j == 1 and first:
                            dve.wait_ge(s["v_T"], NH)
                            dve.wait_ge(s["stash_v"], NH)
                        dve.tensor_tensor((xk, xv)[j][:], acc[:], ez[:], ALU.mult).then_inc(s["kv_silu"], 1)

            def bc(col):
                return col.unsqueeze(2).to_broadcast((P, NC, P))

            def mix_b(h):
                dve.wait_ge(s["conv_sig"], 3 * h + 3)
                dve.tensor_tensor(cq[:], acc[:], ez[:], ALU.mult).then_inc(s["q_silu"], 1)
                yield
                yield
                dve.wait_ge(s["hg_ok"], h + 1)
                dve.wait_ge(s["mix_rs"], h + 1)
                link(dve.tensor_scalar(sk[:, 1, :], sk[:, 1, :], SCALE, None, ALU.mult))
                dve.tensor_tensor(sk[:, 3, :], sk[:, 0, :], hg[:, 4, :], ALU.mult).then_inc(s["mix_scal"], 1)
                dve.tensor_tensor(sk[:, 2, :], sk[:, 0, :], hg[:, 0, :], ALU.mult).then_inc(s["mix_scal"], 1)
                dve.tensor_tensor(oq[:], sk[:, 1, :], hg[:, 3, :], ALU.mult).then_inc(s["mix_scal"], 1)
                dve.wait_ge(s["mix_scal"], 3 * h + 3)
                yield
                dve.wait_ge(s["mix_T1"], 2 * h + 2)
                dve.tensor_tensor(b_kb, mx(0), bc(sk[:, 2, :]), ALU.mult).then_inc(s["mix_tok"], 1)
                dve.tensor_tensor(b_kdec, mx(0), bc(sk[:, 3, :]), ALU.mult).then_inc(s["mix_tok"], 1)
                dve.tensor_tensor(b_vb, mx(1), bc(hg[:, 0, :]), ALU.mult).then_inc(s["mix_tok"], 1)
                dve.wait_ge(s["mix_gb"], h + 1)
                link(dve.tensor_tensor(b_D, mx(3), bc(hg[:, 1, :]), ALU.subtract))
                dve.scalar_tensor_tensor(b_D, b_D, 0.0, causal[:].unsqueeze(1).to_broadcast((P, NC, P)), ALU.min,
                                         ALU.add).then_inc(s["mix_arg"], 1)
                yield
                yield
                dve.wait_ge(s["mix_D"], NC * h + NC)
                dve.wait_ge(s["mix_kk"], h + 1)
                dve.tensor_tensor(b_A, mx(1), b_D, ALU.mult).then_inc(s["mix_A"], 1)
                dve.memset(all_blocks(b_Y, 1, 1), 0.0)
                dve.wait_ge(s["mix_qk"], h + 1)
                dve.tensor_tensor(b_QK, mx(2), b_D, ALU.mult).then_inc(s["mix_QK"], 1)
                yield
                dve.wait_ge(s["z_sig_b"], h + 1)
                dve.tensor_tensor(sz[:], xz[:], ez[:], ALU.mult).then_inc(s["z_ok_b"], 1)
                yield
                for n in range(1, LEVELS):
                    yield
                    yield
                    z = (2 * LEVELS - 3) * h + 2 * (n - 1) + 1
                    dve.wait_ge(s["mix_Z"], z)
                    if n < LEVELS - 1:
                        dve.wait_ge(s["mix_Z"], z + 1)
                    u = all_blocks(b_U, n, 1)
                    dve.tensor_tensor(u, u, all_blocks(mx(2), n, 1), ALU.subtract).then_inc(s["mix_UT"], 1)
                    if n < LEVELS - 1:
                        t = all_blocks(b_T, n, 0)
                        dve.tensor_tensor(t, t, all_blocks(mx(3), n, 0), ALU.subtract).then_inc(s["mix_UT"], 1)
                        dve.memset(all_blocks(b_Y, n + 1, 1), 0.0).then_inc(s["mix_UT"], 1)
                for c in range(NC):
                    if c == 0:
                        dve.tensor_copy(rr, b_vb[:, 0, :]).then_inc(s["ch_r"], 1)
                    else:
                        yield
                        dve.wait_ge(s["ch_kS"], (NC - 1) * h + c)
                        dve.scalar_tensor_tensor(rr, MX[:, 0, 0:P], hg[:, 2, c:c + 1], b_vb[:, c, :], ALU.mult,
                                                 ALU.add).then_inc(s["ch_r"], 1)
                    yield
                    yield
                    dve.wait_ge(s["ch_S_ps"], NC * h + c + 1)
                    if c == 0:
                        dve.wait_ge(s["S_out"], 16 * h + 16)
                        dve.tensor_copy(S, MX[:, 0, 0:P]).then_inc(s["ch_S"], 1)
                    else:
                        dve.scalar_tensor_tensor(S, S, hg[:, 5, c:c + 1], MX[:, 0, 0:P], ALU.mult,
                                                 ALU.add).then_inc(s["ch_S"], 1)
                    dve.wait_ge(s["ch_o_ps"], (2 * NC - 1) * h + 2 * c + 1)
                    if c == 0:
                        dve.tensor_scalar(b_o[:, c, :], MX[:, 3, 0:P], sk[:, 1, c:c + 1], None, ALU.mult).then_inc(
                            s["ch_o"], 1)
                    else:
                        dve.wait_ge(s["ch_o1"], (NC - 1) * h + c)
                        dve.scalar_tensor_tensor(b_o[:, c, :], MX[:, 3, 0:P], sk[:, 1, c:c + 1], o1, ALU.mult,
                                                 ALU.add).then_inc(s["ch_o"], 1)
                dve.wait_ge(s["on_rs"], h + 1)
                dve.tensor_tensor(b_o, b_o, bc(on[:, 1, :]), ALU.mult).then_inc(s["o_n"], 1)
                yield
                dve.wait_ge(s["o_T"], h + 1)
                dve.wait_ge(s["z_ok_b"], h + 1)
                dve.scalar_tensor_tensor(gated[:, NH + h, 0:TP], MX[:, 0, :], vecT[:, KT:KT + 1], sz[:, 0:TP], ALU.mult,
                                         ALU.mult).then_inc(s["gated_b"], 1)

            def new_scores():
                dve.wait_ge(s["stash_k"], NH)
                dve.wait_ge(s["stash_q"], NH)
                dve.tensor_tensor(qks[:], qS[:], kS[:], ALU.mult).then_inc(s["qkp"], 1)
                yield
                dve.wait_ge(s["snew_ps"], 1)
                dve.tensor_scalar(snew[:], MD[0:NH, 0, 0:NB], SCALE, None, ALU.mult).then_inc(s["snew_ok"], 1)

            def delta_decode(h):
                kd, qd = xk[:, TP:TT], cq[:, TP:TT]
                yield
                dve.wait_ge(s["q_silu"], h + 1)
                dve.wait_ge(s["kv_silu"], 2 * h + 2)
                dve.tensor_copy(dd[:, 0, :], kd)
                dve.tensor_copy(dd[:, 1, :], qd)
                dve.tensor_tensor(dd[:, 2, :], kd, kd, ALU.mult)
                dve.tensor_tensor(dd[:, 3, :], qd, qd, ALU.mult)
                dve.tensor_copy(bt_s(0), bgs[:, 0, h, :])
                dve.tensor_copy(bt_s(1), bgs[:, 1, h, :])
                dve.tensor_tensor(dd[:, 4, :], kd, qd, ALU.mult).then_inc(s["dkq"], 1)
                yield
                yield
                dve.wait_ge(s["dkq"], h + 1)
                dve.wait_ge(s["d_sum"], h + 1)
                rk, rq = dd[:, 9, :], dd[:, 10, :]
                ks = MD[:, 1, 32:32 + 2 * NB].rearrange("p (b a) -> p a b", a=2)
                dve.wait_ge(s["d_rs"], h + 1)
                link(dve.tensor_scalar(rq, rq, SCALE, None, ALU.mult))
                dve.tensor_tensor(dd[:, 5, :], dd[:, 0, :], rk, ALU.mult)
                link(dve.tensor_tensor(dd[:, 6, :], ks[:, 0], rk, ALU.mult))
                link(dve.tensor_tensor(dd[:, 6, :], dd[:, 6, :], bt_s(1), ALU.mult))
                link(dve.tensor_tensor(dd[:, 6, :], xv[:, TP:TT], dd[:, 6, :], ALU.subtract))
                link(dve.tensor_tensor(dd[:, 6, :], dd[:, 6, :], bt_s(0), ALU.mult))
                link(dve.tensor_tensor(dd[:, 7, :], MD[:, 1, 2 * NB:3 * NB], rk, ALU.mult))
                link(dve.tensor_tensor(dd[:, 7, :], dd[:, 7, :], dd[:, 6, :], ALU.mult))
                link(dve.tensor_tensor(dd[:, 8, :], ks[:, 1], bt_s(1), ALU.mult))
                link(dve.tensor_tensor(dd[:, 7, :], dd[:, 7, :], dd[:, 8, :], ALU.add))
                link(dve.tensor_tensor(dd[:, 7, :], dd[:, 7, :], rq, ALU.mult))
                dve.tensor_tensor(dd[:, 8, :], dd[:, 7, :], dd[:, 7, :], ALU.mult).then_inc(s["d_vec"], 1)
                yield from idle(4)
                dve.wait_ge(s["d_rows"], h + 1)
                dve.wait_ge(s["z_ok_b"], h + 1)
                dve.wait_ge(s["d_rs2"], h + 1)
                link(dve.tensor_tensor(dd[:, 7, :], dd[:, 7, :], dd[:, 10, :], ALU.mult))
                dve.scalar_tensor_tensor(gated[:, NH + h, TP:TT], dd[:, 7, :], vecT[:, KT:KT + 1], sz[:, TP:TT], ALU.mult,
                                         ALU.mult).then_inc(s["gated_bd"], 1)
                for n in range(2):
                    yield from idle(n + 1)
                    dve.wait_ge(s["d_outer"], 2 * h + n + 1)
                    dve.wait_ge(s["S0_scaled"], h + 1)
                    st = S0[:, 4 * n:4 * n + 4, :]
                    dve.tensor_tensor(st, st, MD[:, 1, :].rearrange("p (b e) -> p b e", b=4), ALU.add).then_inc(
                        s["d_add"], 1)

            def bt_s(n):
                return dd[:, 12 - n, :]

            def attn_decode(b):
                for n in range(3):
                    yield from idle((8, 4, 3)[n])
                    dve.wait_ge(s["prod"], 3 * b + n + 1)
                    src = K_TILE[n]
                    dve.tensor_reduce(sc[:, n, :], src.rearrange("p (h d) -> p h d", h=NH), AX.X, ALU.add).then_inc(
                        s["red"], 1)
                yield
                yield
                dve.wait_ge(s["sc_T"], b + 1)
                link(dve.tensor_reduce(ds[:, 0:1], MD[0:NH, 0, 0:3 * P], AX.X, ALU.max))
                link(dve.tensor_copy(ds[:, 2:3], snew[:, bass.ds(b, 1)]))
                link(dve.scalar_tensor_tensor(ds[:, 0:1], ds[:, 0:1], SCALE, ds[:, 2:3], ALU.mult, ALU.max))
                link(dve.tensor_scalar(ds[:, 1:2], ds[:, 0:1], -1.0, None, ALU.mult))
                dve.tensor_tensor(ds[:, 2:3], ds[:, 2:3], ds[:, 0:1], ALU.subtract).then_inc(s["sc_max"], 1)
                yield from idle(3)
                dve.wait_ge(s["p_exp"], b + 1)
                link(dve.tensor_scalar(ds[:, 4:5], ds[:, 4:5], 3.0, None, ALU.mult))
                link(dve.tensor_tensor(ds[:, 5:6], ds[:, 3:4], ds[:, 4:5], ALU.add))
                link(dve.reciprocal(ds[:, 5:6], ds[:, 5:6]))
                link(dve.tensor_tensor(ds[:, 4:5], ds[:, 4:5], ds[:, 5:6], ALU.mult))
                dve.tensor_scalar(dg[:], ident[0:NH, 0:NH], ds[:, 4:5], None, ALU.mult)
                dve.tensor_scalar(pd, pd, ds[:, 5:6], None, ALU.mult).then_inc(s["p_norm"], 1)
                yield from idle(6)
                dve.wait_ge(s["pT_ok"], b + 1)
                link(dve.tensor_tensor(da[:], vS[:, :, b], pT[:, 3, :], ALU.mult))
                dve.wait_ge(s["pv_ps"], b + 1)
                link(dve.tensor_tensor(da[:], MD[:, 0, 64:64 + NH], da[:], ALU.add))
                dve.tensor_tensor(gated[:, 0:NH, TP + b], da[:], zS[:, :, b], ALU.mult).then_inc(s["gated_ad"], 1)

            for q in (0, 2):
                lo(1, 1, q)
            dve.wait_ge(s["s_loaded"], 32)
            ga, first_a = gates(), own_a(0)
            head(T_A, [ga, first_a])
            ch.end(1)
            with dve.Fori(1, NH) as h:
                ch.at(h, 1, 13)
                head(4 * h + T_A, [tail_a(h - 1), own_a(h)])
            ch.end(NH - 1)
            head(T_B, [tail_a(NH - 1), own_b(0), new_scores()])
            ch.end(1)
            dve.wait_ge(s["stash_z"], NH)
            with dve.Fori(1, NH) as h:
                ch.at(h, 1, 44)
                head(4 * h + T_B, [mix_b(h - 1), delta_decode(h - 1), attn_decode(h - 1), own_b(h)])
            ch.end(NH - 1)
            work = [mix_b(NH - 1), delta_decode(NH - 1), attn_decode(NH - 1)]
            for _ in range(40):
                for g in work:
                    next(g, None)
            for k in range(KT):
                dve.wait_ge(s["g_hi"], k + 1)
                dve.tensor_tensor(h_lo[:, k, :], gated[:, k, :], h_hi[:, k, :].bitcast(F32), ALU.subtract).then_inc(
                    s["g_lo"], 1)
            link(dve.memset(acc[:], 0.0))
            ch.end(1)

            def y_half(T, j, half):
                dve.wait_ge(s["proj_ps"], 2 * T + half + 1)
                tok = slice(half * HALF, (half + 1) * HALF)
                link(dve.tensor_copy(sz[:, tok], PJ[:, half, 0:HALF]))
                dve.tensor_scalar(gated[:, j, tok], sz[:, tok], fin[:, 0:1], None, ALU.mult).then_inc(s["proj_sb"], 1)
                link(dve.tensor_tensor(ez[:, tok], sz[:, tok], sz[:, tok], ALU.mult))
                dve.tensor_tensor(acc[:, tok], acc[:, tok], ez[:, tok], ALU.add).then_inc(s["sq_y"], 1)

            def y_tile(T, j, par, split=True):
                link(dve.tensor_copy(fin[:, 0:1], vecT[:, bass.ds(j, 1)]))
                if split:
                    lo(T + 1, par, 0)
                    lo(T + 1, par, 2)
                y_half(T, j, 0)
                y_half(T, j, 1)

            dve.wait_ge(s["proj_sb"], 2 * T_O)
            with dve.Fori(0, KT // 2 - 1) as i:
                ch.at(i, 0, 10)
                for n in range(2):
                    y_tile(2 * i + (T_O + n), 2 * i + n, n)
            ch.end(KT // 2 - 1)
            y_tile(T_O + KT - 2, KT - 2, 0)
            y_tile(T_O + KT - 1, KT - 1, 1, split=False)
            dve.wait_ge(s["sq_y"], 2 * KT)
            link(dve.memset(fin[:], 1.0))
            dve.wait_ge(s["ss_y"], 1)
            link(dve.tensor_copy(fin[:, 0:NC], MD[:, 0, 0:NC]))
            link(dve.tensor_copy(fin[0:NB, NC:NC + 1], MD[0:NB, 0, NC:NC + 1]))
            dve.tensor_copy(fin[:, 7:8], fin[:, 7:8]).then_inc(s["fin_rs"], 1)
            dve.wait_ge(s["fin_rs"], 2)
            for c in range(NC + 1):
                n = P if c < NC else NB
                dve.wait_ge(x_in[c], 32 if c < NC else 48)
                for b in range(4):
                    x = xres[c][:, b * TP:(b + 1) * TP] if c < NC else xs_res[b // 2][:, b % 2 * TP:(b % 2 + 1) * TP]
                    dve.wait_ge(s["y_T"], 4 * c + b + 1)
                    dve.scalar_tensor_tensor(x, MX[0:n, b, :], fin[0:n, c:c + 1], x, ALU.mult, ALU.add).then_inc(
                        s["y_out_ok"], 1)

        @block.gpsimd
        def _(pool):
            def lo(T, par, q, n=P):
                pool.wait_ge(s["w_hi_ok"], 4 * T + q + 1)
                pool.tensor_tensor(w_lo[:, par, 4 * q:4 * q + 4, 0:n], w_raw[:, q, :, 0:n],
                                   w_hi[:, par, 4 * q:4 * q + 4, 0:n].bitcast(F32), ALU.subtract).then_inc(
                    s["w_lo_pool"], 1)

            def head(T, work):
                for j in range(4):
                    for seg in range(SEGS):
                        for g in work:
                            next(g, None)
                        if seg % 4 == 2:
                            lo(T + (j + 1), j % 2, seg // 2)

            def own_a(h):
                yield from idle(10)
                pool.wait_ge(s["q_ok"], h + 1)
                pool.tensor_copy(qS[:, h, :], xq[:, TP:TT]).then_inc(s["stash_q"], 1)
                yield from idle(8)
                pool.wait_ge(s["k_ok"], h + 1)
                pool.tensor_copy(kS[:, h, :], xk[:, TP:TT]).then_inc(s["stash_k"], 1)
                yield from idle(8)
                pool.wait_ge(s["proj_sb"], 8 * h + 2 * T_A + 6)
                pool.tensor_copy(vS[:, h, :], xv[:, TP:TT]).then_inc(s["stash_v"], 1)

            def tail_a(h):
                yield from idle(3)
                pool.wait_ge(s["z_ok"], h + 1)
                pool.tensor_copy(zS[:, h, :], sz[:, TP:TT]).then_inc(s["stash_z"], 1)

            def own_b(h):
                if isinstance(h, int) and h == 0:
                    pool.wait_ge(s["st_sb"], 2)
                else:
                    pool.wait_ge(s["conv_ok"], 3 * h)
                pool.tensor_copy(cw[:], stT[:].rearrange("p (m h) w -> p m h w", m=3)[:, :, h, :]).then_inc(
                    s["cw_ok"], 1)
                yield

            def mix_b(h):
                pool.wait_ge(s["q_silu"], h + 1)
                pool.tensor_copy(hg[:], G6[:, :, :, h]).then_inc(s["hg_ok"], 1)
                pool.wait_ge(s["hg_ok"], h + 1)
                pool.tensor_tensor(b_B0, ident[:].unsqueeze(1).to_broadcast((P, NC, P)),
                                   hg[:, 1, :].unsqueeze(2).to_broadcast((P, NC, P)), ALU.mult).then_inc(
                    s["mix_gr"], 1)
                yield
                yield from idle(5)
                pool.wait_ge(s["mix_A"], h + 1)
                pool.wait_ge(s["mix_gb"], h + 1)
                for n in range(LEVELS):
                    if n == 1:
                        pool.wait_ge(s["mix_QK"], h + 1)
                    if n == 2:
                        pool.wait_ge(s["mix_U0"], h + 1)
                    if n >= 3:
                        pool.wait_ge(s["mix_Y_ps"], (LEVELS - 1) * h + n - 2)
                    ins = pool.tensor_tensor(b_B[n % 2], b_A, levels[:, n, :].unsqueeze(1).to_broadcast((P, NC, P)),
                                             ALU.mult)
                    ins.then_inc(s["mix_B"], 1)
                    if n == 0:
                        pool.wait_ge(s["mix_B"], LEVELS * h + 1)
                        pool.tensor_tensor(b_U, ident[:].unsqueeze(1).to_broadcast((P, NC, P)), b_B[0],
                                           ALU.subtract).then_inc(s["mix_U0"], 1)
                    if n == 1:
                        yield
                    if n >= 1:
                        yield
                        yield

            def delta_decode(h):
                yield from idle(3)
                pool.wait_ge(s["d_sum"], h + 1)
                pool.tensor_tensor(S0[:], S0[:], dd[:, 11, :].unsqueeze(2).to_broadcast((P, NB, P)),
                                   ALU.mult).then_inc(s["S0_scaled"], 1)
                yield from idle(3)
                for n in range(2):
                    pool.wait_ge(s["d_rows_ok"], h + 1)
                    if n == 1:
                        pool.wait_ge(s["d_outer"], 2 * h + 1)
                    pool.tensor_tensor(vexp, kvr[:, 1, :].unsqueeze(1).to_broadcast((NB, 4, P)),
                                       ident[0:NB, 4 * n:4 * n + 4].unsqueeze(2).to_broadcast((NB, 4, P)),
                                       ALU.mult).then_inc(s["d_vexp"], 1)
                    yield
                    yield
                    yield

            def attn_decode(b):
                yield from idle(5)
                pool.wait_ge(s["qb_in"], 16 * b + 16)
                for n in range(3):
                    yield from idle((1, 5, 2)[n])
                    pool.wait_ge(s[f"kb{n}_in"], 16 * b + 16)
                    t = K_TILE[n]
                    pool.tensor_tensor(t, t, qb[:], ALU.mult).then_inc(s["prod"], 1)

            for q in (1, 3):
                pool.wait_ge(s["memset_ok"], 1)
                lo(0, 0, q, 16)
            for q in (1, 3):
                lo(1, 1, q)
            head(T_A, [own_a(0)])
            with pool.Fori(1, NH) as h:
                head(4 * h + T_A, [tail_a(h - 1), own_a(h)])
            pool.wait_ge(s["scores"], 4 * NH)
            pool.memset(xq[:, 0:3], 0.0).then_inc(s["zero_cols"], 1)
            head(T_B, [tail_a(NH - 1), own_b(0)])
            pool.wait_ge(s["gates_dve"], 5)
            pool.wait_ge(s["gates_act"], 4)
            pool.wait_ge(s["gated_a"], NH)
            pool.wait_ge(s["k_out"], 16 * NH)
            pool.wait_ge(s["v_out"], 32 * NH)
            with pool.Fori(1, NH) as h:
                head(4 * h + T_B, [mix_b(h - 1), own_b(h), delta_decode(h - 1), attn_decode(h - 1)])
            work = [mix_b(NH - 1), delta_decode(NH - 1), attn_decode(NH - 1)]
            for _ in range(40):
                for g in work:
                    next(g, None)
            with pool.Fori(0, KT // 2 - 1) as i:
                for n in range(2):
                    for q in (1, 3):
                        lo(2 * i + (T_O + n + 1), n, q)
            for q in (1, 3):
                lo(T_O + KT - 1, 0, q)


_INS = ["x_prompt", "x_sample", "cache_win_k", "cache_win_v", "state_conv", "state_delta", "g_pre", "w_in", "conv_w",
        "a_log", "dt_bias", "onorm_w", "w_out", "g_post"]
_CONST = ["c_ident", "c_upper", "c_causal", "c_levels", "c_lnmask", "c_rope", "c_rot"]
_OUTS = [(1, TP, D), (NB, 1, D), (1, 1, TP, NH, HD), (1, 1, TP, NH, HD), (1, 1, CW - 1, CONV_CH), (1, 1, NH, HD, HD),
         (1, NB, 1, NH, HD), (1, NB, 1, NH, HD), (1, NB, CW - 1, CONV_CH), (1, NB, NH, HD, HD)]


def kernel(**inputs):
    import concourse.bacc as bacc
    from concourse.bass_utils import run_bass_kernel_spmd

    nc = bacc.Bacc("TRN2", target_bir_lowering=False, num_devices=1)
    arrays, args = {}, []
    consts = tables()
    for name in _INS + _CONST:
        a = np.ascontiguousarray(inputs[name] if name in inputs else consts[name])
        arrays[f"in_{name}"] = a
        args.append(nc.dram_tensor(f"in_{name}", a.shape, mybir.dt.from_np(a.dtype), kind="ExternalInput").ap())
    for i, shape in enumerate(_OUTS):
        args.append(nc.dram_tensor(f"out_{i}", shape, F32, kind="ExternalOutput").ap())
    build(nc, *args)
    r = run_bass_kernel_spmd(nc, [arrays], core_ids=[0])
    return tuple(r.results[0][f"out_{i}"] for i in range(len(_OUTS)))
```

```python
from contextlib import ExitStack
import numpy as np
import concourse.bass as bass
from concourse import mybir

F32 = mybir.dt.float32
F32R = mybir.dt.float32r
ALU = mybir.AluOpType
ACT = mybir.ActivationFunctionType
AX = mybir.AxisListType

P = 128
D = 2048
TP = 512
NB = 8
TT = TP + NB
HALF = TT // 2
KT = D // P
NQ = 4
NH = 8
HD = 128
NC = TP // P
WA = NH * HD
CONV_CH = 3 * WA
CW = 4
PAST = 2048
ROT = 32
EPS = 1e-6
SCALE = HD ** -0.5
LEVELS = 7
NEG = -1.0e30
X_LOW = -43.0
SEGS = 8
T_A, T_B, T_O = 1, 1 + 4 * NH, 1 + 8 * NH


def tables():
    f = np.float32
    i = np.arange(P)
    t = {"c_ident": np.eye(P, dtype=f), "c_upper": (i[:, None] <= i[None, :]).astype(f)}
    t["c_causal"] = np.where(i[:, None] <= i[None, :], 0.0, NEG).astype(f)
    lev = np.zeros((P, LEVELS, P), mybir.dt.np(mybir.dt.bfloat16))
    for n in range(LEVELS):
        s = 1 << n
        same = i[:, None] // (2 * s) == i[None, :] // (2 * s)
        lev[:, n] = same & ((i[:, None] // s) % 2 == 0) & ((i[None, :] // s) % 2 == 1)
    t["c_levels"] = lev
    kk = np.arange(TP)
    dist = P * (NC - 1 - kk // P)[None, :] + i[:, None] - (kk % P)[None, :]
    cnt = sum(((dist >= 0) & (dist <= w) & (dist % d == 0)).astype(int) for w, d in ((128, 1), (512, 4), (2048, 16)))
    t["c_lnmask"] = np.where(cnt > 0, np.log(np.maximum(cnt, 1)), NEG).astype(f)
    half = ROT // 2
    inv = f(500000.0) ** (-np.arange(half, dtype=f) / f(half))
    pos = np.concatenate([np.arange(TP), np.full(NB, PAST)]).astype(f)
    ang = (pos[:, None] * inv[None, :]).astype(f).T.astype(np.float64)
    t["c_rope"] = np.stack([np.tile(np.cos(ang), (2, 1)), np.tile(np.sin(ang), (2, 1))], 1).astype(f)
    rot = np.zeros((ROT, 2 * ROT), f)
    for m in range(half):
        rot[m + half, m] = -1.0
        rot[m, m + half] = 1.0
    t["c_rot"] = rot
    return t


class Chain:

    def __init__(self, eng, sem):
        self.eng, self.sem, self.base, self.off, self.n, self.per = eng, sem, 0, 0, 0, 0

    def at(self, h, first, per):
        self.off, self.n, self.per = (h - first) * per, 0, per

    def end(self, iterations):
        assert iterations == 1 or self.n == self.per, (self.n, self.per)
        self.base, self.off, self.n = self.base + iterations * self.n, 0, 0

    def link(self, ins):
        self.n += 1
        ins.then_inc(self.sem, 1)
        self.eng.wait_ge(self.sem, self.off + (self.base + self.n))


PARTS = 4
UNITS = 3 * PARTS + 3


def out_unit(slot, p):
    if slot < PARTS:
        u = 4 * slot + p
        return (u // 3, u % 3) if u < 3 * PARTS else (PARTS, u - 3 * PARTS)
    return (p, NQ - 1) if slot == PARTS else (slot, p)


def splits(n):
    return {0: range(8), 1: range(8, 12), 12: (12,), 14: (13,), 16: (14,)}.get(n, ())


def idle(n):
    for _ in range(n):
        yield


def build(nc, x_prompt, x_sample, cache_k, cache_v, state_conv, state_delta, g_pre, w_in, conv_w, a_log, dt_bias,
          onorm_w, w_out, g_post, c_ident, c_upper, c_causal, c_levels, c_lnmask, c_rope, c_rot,
          y_p, y_s, wk_p, wv_p, cv_p, st_p, wk_s, wv_s, cv_s, st_s):
    w_in_v = w_in[0].rearrange("(kt p) c -> p kt c", p=P)
    w_out_v = w_out[0].rearrange("(kt p) c -> p kt c", p=P)
    kp_v = wk_p[0, 0].rearrange("(c p) h d -> p c h d", p=P)
    vp_v = wv_p[0, 0].rearrange("(c p) h d -> p c h d", p=P)
    scratch_q = nc.dram_tensor("scratch_q", (NB, WA), F32, kind="Internal").ap()

    with ExitStack() as ctx:
        def sb(name, shape, dt=F32):
            return ctx.enter_context(nc.sbuf_tensor(name, shape, dt))

        def sem(name):
            return ctx.enter_context(nc.semaphore(name))

        h_hi = sb("h_hi", [P, KT, TT], F32R)
        h_lo = sb("h_lo", [P, KT, TT], F32R)
        w_raw = sb("w_raw", [P, NQ, 4, P])
        w_hi = sb("w_hi", [P, 2, KT, P], F32R)
        w_lo = sb("w_lo", [P, 2, KT, P], F32R)
        gated = sb("gated", [P, KT, TT])
        xin = gated[:].rearrange("p a b -> p (a b)")[:, 0:NC * D].rearrange("p (c d) -> p c d", d=D)
        ident = sb("ident", [P, P])
        upper = sb("upper", [P, P])
        causal = sb("causal", [P, P])
        ones = sb("ones", [P, P])
        levels = sb("levels", [P, LEVELS, P], mybir.dt.bfloat16)
        arena = sb("arena", [P, 4096 + 2 * TT])
        lnmask = arena[:, 0:TP]
        probs = arena[:, TP:TP + 10 * P]
        probT = arena[:, TP + 10 * P:TP + 20 * P]
        ktok = arena[:, TP + 20 * P:TP + 24 * P].rearrange("p (c d) -> p c d", c=NC)
        vtok = arena[:, TP + 24 * P:TP + 28 * P].rearrange("p (c d) -> p c d", c=NC)
        rope = arena[0:ROT, 4096:4096 + 2 * TT].rearrange("p (a t) -> p a t", a=2)
        b_kb, b_kbT, b_kdec, b_vb, b_D, b_QK, b_U, b_T, b_Y, b_B0 = [
            arena[:, n * TP:(n + 1) * TP].rearrange("p (c d) -> p c d", c=NC) for n in range(10)]
        b_A = b_kb
        b_B = (b_B0, b_D)
        b_o = b_T
        xq = sb("xq", [P, 3 + TT])
        xk = sb("xk", [P, TT])
        xv = sb("xv", [P, TT])
        xz = sb("xz", [P, TT])
        cq = sb("cq", [P, TT])
        acc = sb("acc", [P, TT])
        ez = sb("ez", [P, TT])
        sz = sb("sz", [P, TT])
        small = sb("small", [P, 4 * P])
        S = small[:, 0:P]
        rr = small[:, P:2 * P]
        vn = small[:, 2 * P:3 * P]
        o1 = small[:, 3 * P:4 * P]
        gw = small[:, 0:160].rearrange("p (a c h) -> p a c h", a=4, c=NC + 1)
        gt = small[:, 160:240].rearrange("p (c a h) -> p c a h", a=2, c=NC + 1)
        kv = sb("kv", [P, 2, WA])
        S0 = sb("S0", [P, NB, P])
        rb = sb("rb", [11, 10 * P])
        rows = rb[:, 0:P]
        vexp = rb[0:NB, P:5 * P].rearrange("p (b e) -> p b e", e=P)
        pd = rb[0:NH, 5 * P:8 * P].rearrange("p (n t) -> p n t", n=3)
        kvr = rb[0:NB, 8 * P:10 * P].rearrange("p (n t) -> p n t", n=2)
        qkrow = rb[0:NB, 5 * P:7 * P].rearrange("p (n t) -> p n t", n=2)
        vrow = rb[0:NB, 7 * P:8 * P]
        dgs = rb[0:NB, 8 * P:9 * P].rearrange("p (a h b) -> p a h b", a=2, h=NH)
        stT = sb("stT", [P, 3 * NH, 28])
        cw = sb("cw", [P, 3, 28])
        vecT = sb("vecT", [P, KT + 1])
        ssum = sb("ssum", [P, 8])
        rstd = sb("rstd", [P, 8])
        adt = sb("adt", [P, 2, NH])
        G6 = sb("G6", [P, 6, NC, NH])
        hg = sb("hg", [P, 6, NC])
        gneg = sb("gneg", [P, NH])
        bgs = sb("bgs", [P, 2, NH, NB])
        sk = sb("sk", [P, 4, NC])
        lnss = sb("lnss", [P, 2, NC])
        lnrk = sb("lnrk", [P, NC])
        oq = sb("oq", [P, NC])
        on = sb("on", [P, 2, NC])
        stat = sb("stat", [P, 3, NC])
        qS = sb("qS", [P, NH, NB])
        kS = sb("kS", [P, NH, NB])
        vS = sb("vS", [P, NH, NB])
        zS = sb("zS", [P, NH, NB])
        qks = sb("qks", [P, NH, NB])
        snew = sb("snew", [NH, NB])
        sc = sb("sc", [P, 3, NH])
        ds = sb("ds", [NH, 8])
        dg = sb("dg", [NH, NH])
        pT = sb("pT", [P, 4, NH])
        da = sb("da", [P, NH])
        dd = sb("dd", [P, 13, NB])
        fin = sb("fin", [P, 8])
        rotm = sb("rotm", [ROT, 2 * ROT])
        s_in = xz[:, 0:P]
        xba = cq[0:16, :]
        scin = arena[0:28, 0:CONV_CH]
        xs_in = kv[0:NB].rearrange("p a b -> p (a b)")
        junk = arena[:, CONV_CH:CONV_CH + D]
        qb = sb("qb", [P, WA])
        g_bc = (S0[:].rearrange("p b e -> p (b e)"), qb[:])
        xres = [arena[:, 0:D], arena[:, D:2 * D], kv[:].rearrange("p a b -> p (a b)"),
                w_raw[:].rearrange("p a b c -> p (a b c)")]
        xs_res = (S0[0:NB].rearrange("p b e -> p (b e)"), qb[0:NB])
        K_TILE, V_TILE = (kv[:, 0], kv[:, 1], kv[:, 0]), (kv[:, 1], kv[:, 0], qb[:])

        PJ = ctx.enter_context(nc.psum_tensor("PJ", [P, 2, TP], F32))
        MX = ctx.enter_context(nc.psum_tensor("MX", [P, 4, TP], F32))
        MD = ctx.enter_context(nc.psum_tensor("MD", [P, 2, TP], F32))

        UTS = 3 * (LEVELS - 2) + 1
        def blocks(x, n, odd):
            return x.rearrange("p (k a s) -> p k a s", a=2, s=1 << n)[:, :, odd, :]

        def all_blocks(x, n, odd):
            return x.rearrange("p c (k a s) -> p (c k) a s", a=2, s=1 << n)[:, :, odd, :]

        def mx(n):
            return MX[:, n].rearrange("p (c d) -> p c d", c=NC)

        NAMES = (
            "c_in g_in consts s_loaded x_sq rstd_ok x_scaled hT_ps hT_hi hT_lo vec_ps st_ps st_sb memset_ok "
            "w_hi_ok w_lo_dve w_lo_pool w_used proj_ps proj_sb "
            "gates_pe gates_act gates_dve "
            "q_rot q_ok k_rot k_ok k_T ktok_ok k_out v_T vtok_ok v_out row_out qrow_out scores negmax expd "
            "probs_ok probT_ps probT_ok attn_ps z_low z_sig z_ok gated_a stash_q stash_k stash_v stash_z "
            "act_chain dve_chain "
            "zero_cols cw_ok crow_ps crow_ok crow_out conv_ok conv_sig kv_silu q_silu "
            "hg_ok mix_T1 mix_ss mix_lnrk mix_rs mix_scal mix_gb mix_tok mix_kbT_ps mix_kbT mix_arg mix_D "
            "mix_kk mix_qk mix_A mix_QK mix_B mix_U0 mix_T_ps mix_T mix_Y_ps mix_Y mix_Z mix_UT ch_kS ch_r "
            "ch_v_ps ch_v ch_S_ps ch_o_ps ch_S ch_o1 ch_o o_sq on_rs o_n o_T z_sig_b z_ok_b gated_b S_out "
            "snew_ps snew_ok qkp qb_in kb0_in kb1_in kb2_in prod red sc_T sc_max p_exp p_norm p_T pT_ok vb0_in "
            "vb1_in vb2_in pv_sum pv_ps gated_ad "
            "dkq d_sum d_rs d_vec d_rows d_rows_ok d_rs2 d_vexp d_outer d_add S0_in S0_scaled S0_out gated_bd "
            "g_hi g_lo part_ps part_sb rest_ps sq_y ss_y fin_rs y_T y_out_ok y_out "
        )
        s = {n: sem(n) for n in NAMES.split()}
        x_in = [sem(f"x_in{c}") for c in range(NC + 1)]
        raw_in = [sem(f"w_raw_in{q}") for q in range(NQ)]

        def lo_sem(q):
            return s["w_lo_dve"] if q % 2 == 0 else s["w_lo_pool"]

        block = ctx.enter_context(nc.Block())

        @block.sync
        def _(sp):
            def wait_lo(T, q):
                sp.wait_ge(lo_sem(q), 2 * T + q // 2 + 1)

            def load_w(view, c0, q, n=P, src=None):
                k = 4 * (q if src is None else src)
                sp.dma_start(w_raw[:, q, :, 0:n], view[:, k:k + 4, bass.ds(c0, n)]).then_inc(raw_in[q], 16)

            def load_out(slot, p):
                j, q = out_unit(slot, p)
                load_w(w_out_v, j * P, p, src=q)

            sp.dma_start(xs_in, x_sample.rearrange("b t d -> (b t) d")).then_inc(x_in[NC], 16)
            sp.dma_start(xin[:, 0, :], x_prompt[0, 0:P, :]).then_inc(x_in[0], 16)
            for n in range(2):
                sp.dma_start(g_bc[n], g_pre[0, n * WA:(n + 1) * WA].partition_broadcast(P)).then_inc(s["g_in"], 16)
            sp.dma_start(ident[:], c_ident).then_inc(s["c_in"], 16)
            sp.dma_start(xin[:, 1, :], x_prompt[0, P:2 * P, :]).then_inc(x_in[1], 16)
            sp.dma_start(scin[0:24], state_conv[0].rearrange("b i c -> (b i) c")).then_inc(s["c_in"], 16)
            sp.dma_start(scin[24:28], conv_w[0]).then_inc(s["c_in"], 16)
            sp.dma_start(s_in[0:KT], g_post.rearrange("o (a p) -> (o a) p", p=P)).then_inc(s["c_in"], 16)
            sp.dma_start(s_in[KT:KT + 1], onorm_w).then_inc(s["c_in"], 16)
            for c in range(2, NC):
                sp.dma_start(xin[:, c, :], x_prompt[0, c * P:(c + 1) * P, :]).then_inc(x_in[c], 16)
            for q in range(NQ):
                load_w(w_in_v, 8 * WA, q, 16)
            sp.dma_start(upper[:], c_upper).then_inc(s["consts"], 16)
            sp.dma_start(causal[:], c_causal).then_inc(s["consts"], 16)
            sp.dma_start(levels[:], c_levels).then_inc(s["consts"], 16)
            sp.dma_start(rotm[:], c_rot).then_inc(s["consts"], 16)
            sp.dma_start(adt[:, 0], a_log[0].partition_broadcast(P)).then_inc(s["consts"], 16)
            sp.dma_start(adt[:, 1], dt_bias[0].partition_broadcast(P)).then_inc(s["consts"], 16)
            sp.dma_start(cv_s[0, :, 0:2, :], state_conv[0, :, 1:3, :]).then_inc(s["S_out"], 16)
            for q in range(NQ):
                wait_lo(0, q)
                load_w(w_in_v, 0, q)
            sp.wait_ge(s["x_sq"], NC + 1)
            sp.wait_ge(s["st_ps"], 24)
            sp.dma_start(lnmask, c_lnmask).then_inc(s["s_loaded"], 16)
            sp.dma_start(rope, c_rope).then_inc(s["s_loaded"], 16)

            def head_loads(T, nxt, work):
                for j in range(4):
                    for seg in range(SEGS):
                        if seg % 2 == 0 and nxt[j] is not None:
                            q = seg // 2
                            wait_lo(T + j + 1, q)
                            if nxt[j][0] is w_out_v:
                                load_out(nxt[j][1], q)
                            else:
                                load_w(*nxt[j], q)
                        for g in work:
                            next(g, None)

            def cache_block(view, n):
                return (view[PAST - 128:PAST], view[PAST - 512:PAST:4], view[0:PAST:16])[n].rearrange(
                    "t h d -> t (h d)")

            def attn_decode(b):
                vc = cache_v[0, b]
                yield from idle(8)
                sp.wait_ge(s["red"], 3 * b + 1)
                sp.dma_start(K_TILE[2], cache_block(cache_k[0, b], 2)).then_inc(s["kb2_in"], 16)
                yield from idle(4)
                sp.wait_ge(s["red"], 3 * b + 2)
                sp.dma_start(V_TILE[0], cache_block(vc, 0)).then_inc(s["vb0_in"], 16)
                yield from idle(3)
                sp.wait_ge(s["red"], 3 * b + 3)
                for n in (1, 2):
                    sp.dma_start(V_TILE[n], cache_block(vc, n)).then_inc(s[f"vb{n}_in"], 16)

            def attn_rows(b):
                yield from idle(30)
                sp.wait_ge(s["qrow_out"], 16 * NH)
                if not isinstance(b, int) or b > 0:
                    sp.wait_ge(s["pv_ps"], b)
                kc = cache_k[0, b]
                sp.dma_start(qb[:], scratch_q[b].partition_broadcast(P)).then_inc(s["qb_in"], 16)
                for n in range(2):
                    sp.dma_start(K_TILE[n], cache_block(kc, n)).then_inc(s[f"kb{n}_in"], 16)

            def delta_decode(h):
                yield from idle(13)
                sp.wait_ge(s["d_add"], 2 * h + 2)
                sp.dma_start(st_s[0, :, h].rearrange("b d e -> d b e"), S0[:]).then_inc(s["S0_out"], 16)

            def delta_states(h):
                yield from idle(28)
                if not isinstance(h, int) or h > 0:
                    sp.wait_ge(s["S0_out"], 16 * h)
                sp.dma_start(S0[:], state_delta[0, :, h].rearrange("b d e -> d b e")).then_inc(s["S0_in"], 16)

            def mix_b(h):
                yield from idle(31)
                sp.wait_ge(s["ch_S"], 4 * h + 4)
                sp.dma_start(st_p[0, 0, h], S).then_inc(s["S_out"], 16)

            def loads_a(h, last=False):
                a = [(w_in_v, 2 * WA + h * HD), (w_in_v, 3 * WA + h * HD)]
                b = [(w_in_v, 5 * WA), (w_in_v, 6 * WA)] if last else \
                    [(w_in_v, (h + 1) * HD), (w_in_v, WA + (h + 1) * HD)]
                return a + b

            def loads_b(h, last=False):
                a = [(w_in_v, 4 * WA + h * HD), (w_in_v, 7 * WA + h * HD)]
                b = [(w_out_v, 0), (w_out_v, 1)] if last else \
                    [(w_in_v, 5 * WA + (h + 1) * HD), (w_in_v, 6 * WA + (h + 1) * HD)]
                return a + b

            for q in range(NQ):
                wait_lo(1, q)
                load_w(w_in_v, WA, q)
            with sp.Fori(0, NH - 1) as h:
                head_loads(4 * h + T_A, loads_a(h), [])
            head_loads(T_A + 4 * (NH - 1), loads_a(NH - 1, True), [attn_rows(0)])
            head_loads(T_B, loads_b(0), [attn_decode(0), attn_rows(1), delta_states(0)])
            with sp.Fori(1, NH - 1) as h:
                head_loads(4 * h + T_B, loads_b(h),
                           [mix_b(h - 1), attn_decode(h), delta_decode(h - 1), attn_rows(h + 1), delta_states(h)])
            h = NH - 1
            head_loads(4 * h + T_B, loads_b(h, True),
                       [mix_b(h - 1), attn_decode(h), delta_decode(h - 1), delta_states(h)])
            gens = [mix_b(h), delta_decode(h)]
            for n in range(40):
                if n % 2 == 0 and n < 8 * PARTS:
                    slot, p = n // 8, n // 2 % 4
                    wait_lo(T_O + slot + 1, p)
                    load_out(slot + 2, p)
                for g in gens:
                    next(g, None)
            for p in range(NQ):
                wait_lo(T_O + PARTS + 1, p)
                load_out(PARTS + 2, p)
            with sp.Fori(PARTS + 1, KT - 2) as j:
                for q in range(NQ):
                    wait_lo(j + (T_O + 1), q)
                    load_w(w_out_v, (j + 2) * P, q)
            sp.wait_ge(s["gated_b"], NH)
            sp.wait_ge(s["pv_ps"], NB)
            sp.wait_ge(s["S0_out"], 16 * NH)
            for i in range(2):
                sp.dma_start(xs_res[i], x_sample.rearrange("b t d -> (b t) d")[:, i * WA:(i + 1) * WA]).then_inc(
                    x_in[NC], 16)
            for c in range(NC):
                if c == 3:
                    for q in range(NQ):
                        wait_lo(T_O + KT - 1, q)
                sp.dma_start(xres[c], x_prompt[0, c * P:(c + 1) * P, :]).then_inc(x_in[c], 16)
            for c in range(NC):
                sp.wait_ge(s["y_out_ok"], 4 * (c + 1))
                sp.dma_start(y_p[0, c * P:(c + 1) * P, :], xres[c]).then_inc(s["y_out"], 16)
            sp.wait_ge(s["y_out_ok"], 4 * (NC + 1))
            for i in range(2):
                sp.dma_start(y_s.rearrange("b t d -> (b t) d")[:, i * WA:(i + 1) * WA], xs_res[i]).then_inc(
                    s["y_out"], 16)
            sp.wait_ge(s["y_out"], 16 * (NC + 2))
            sp.wait_ge(s["k_out"], 16 * NH)
            sp.wait_ge(s["row_out"], 16 * NH)
            sp.wait_ge(s["v_out"], 32 * NH)
            sp.wait_ge(s["crow_out"], 32 * 3 * NH)
            sp.wait_ge(s["S_out"], 16 * (NH + 1))
            sp.wait_ge(s["S0_out"], 16 * NH)

        @block.tensor
        def _(pe):
            def segment(T, par, half, q, first=False):
                if half == 0:
                    pe.wait_ge(lo_sem(q), 2 * T + q // 2 + 1)
                if q == 0 and not first:
                    pe.wait_ge(s["proj_sb"], 2 * T - 1 + half)
                tok = slice(half * HALF, (half + 1) * HALF)
                out = PJ[:, half, 0:HALF]
                for k in range(4 * q, 4 * q + 4):
                    wh, wl = w_hi[:, par, k, :], w_lo[:, par, k, :]
                    pe.matmul(out, wh, h_hi[:, k, tok], start=k == 0, stop=False)
                    pe.matmul(out, wh, h_lo[:, k, tok], start=False, stop=False)
                    last = pe.matmul(out, wl, h_hi[:, k, tok], start=False, stop=k == KT - 1)
                if q == NQ - 1:
                    last.then_inc(s["proj_ps"], 1)
                elif half == 1:
                    last.then_inc(s["w_used"], 1)

            def project(T, par, work, first=False):
                for half in range(2):
                    for q in range(NQ):
                        segment(T, par, half, q, first)
                        for g in work:
                            next(g, None)

            pe.wait_ge(s["c_in"], 80)
            pe.transpose(MD[:, 0, 0:KT + 1], s_in[0:KT + 1], ident[0:KT + 1, 0:KT + 1]).then_inc(s["vec_ps"], 1)
            for m in range(3 * NH):
                bank, o = m // 12, (m % 12) * 28
                pe.transpose(MX[:, 2 + bank, o:o + 28], scin[:, m * P:(m + 1) * P], ident[0:28, 0:28]).then_inc(
                    s["st_ps"], 1)
            pe.wait_ge(s["x_scaled"], 2)
            for k in range(KT):
                last = pe.transpose(MD[:, 1, k * NB:(k + 1) * NB], xs_in[:, k * P:(k + 1) * P], ident[0:NB, 0:NB])
            last.then_inc(s["hT_ps"], 1)
            for c in range(NC):
                for b in range(4):
                    if b % 2 == 0:
                        pe.wait_ge(s["x_scaled"], 2 * c + 2 + b // 2 + 1)
                    if c > 0:
                        pe.wait_ge(s["hT_lo"], 4 * (c - 1) + b + 2)
                    elif b == 2:
                        pe.wait_ge(s["st_sb"], 2)
                    for k in range(4):
                        last = pe.transpose(MX[:, b, k * P:(k + 1) * P], xin[:, c, (4 * b + k) * P:(4 * b + k + 1) * P],
                                            ident[:])
                    last.then_inc(s["hT_ps"], 1)
            pe.wait_ge(s["hT_lo"], 4 * NC + 1)

            def gates():
                yield from idle(8)
                pe.wait_ge(s["proj_sb"], 2)
                for c in range(NC):
                    pe.transpose(MD[:, 0, c * 16:(c + 1) * 16], xba[:, c * P:(c + 1) * P], ident[0:16, 0:16])
                pe.transpose(MD[0:NB, 0, 64:80], xba[:, TP:TT], ident[0:16, 0:16]).then_inc(s["gates_pe"], 1)
                yield from idle(5)
                pe.wait_ge(s["gates_dve"], 2)
                g = gw[:, 3, 0:NC, :].rearrange("p c h -> p (c h)")
                pe.matmul(MD[:, 1, 0:32], upper[:], g, start=True, stop=True)
                pe.matmul(MD[:, 1, 32:64], ones[:], g, start=True, stop=True).then_inc(s["gates_pe"], 1)
                yield from idle(3)
                pe.wait_ge(s["gates_dve"], 5)
                pe.matmul(MD[:, 0, 0:P], ones[0:NB, :], dgs.rearrange("p a h b -> p (a h b)"), start=True,
                          stop=True).then_inc(s["gates_pe"], 1)

            def own_a(h):
                yield from idle(9)
                pe.wait_ge(s["proj_sb"], 8 * h + 4)
                if not isinstance(h, int) or h > 0:
                    pe.wait_ge(s["gated_a"], h)
                for half in range(2):
                    last = pe.matmul(MX[0:2 * ROT, half, 0:HALF], rotm[:], xq[0:ROT, half * HALF:(half + 1) * HALF],
                                     start=True, stop=True)
                last.then_inc(s["q_rot"], 1)
                yield from idle(8)
                pe.wait_ge(s["proj_sb"], 8 * h + 6)
                pe.wait_ge(s["q_ok"], h + 1)
                for half in range(2):
                    last = pe.matmul(MX[0:2 * ROT, half, 0:HALF], rotm[:], xk[0:ROT, half * HALF:(half + 1) * HALF],
                                     start=True, stop=True)
                last.then_inc(s["k_rot"], 1)
                yield from idle(2)
                pe.wait_ge(s["k_ok"], h + 1)
                for c in range(NC):
                    pe.transpose(MX[:, 2, c * P:(c + 1) * P], xk[:, c * P:(c + 1) * P], ident[:])
                pe.transpose(MX[0:NB, 3, 0:P], xq[:, TP:TT], ident[:])
                pe.transpose(MX[0:NB, 3, P:2 * P], xk[:, TP:TT], ident[:]).then_inc(s["k_T"], 1)
                yield from idle(6)
                pe.wait_ge(s["proj_sb"], 8 * h + 8)
                pe.wait_ge(s["ktok_ok"], 2 * h + 2)
                for c in range(NC):
                    pe.transpose(MX[:, 2, c * P:(c + 1) * P], xv[:, c * P:(c + 1) * P], ident[:])
                pe.transpose(MX[0:NB, 3, 0:P], xv[:, TP:TT], ident[:]).then_inc(s["v_T"], 1)
                for i in range(NC):
                    if i != 1:
                        yield
                    if i == 2:
                        pe.wait_ge(s["vtok_ok"], 2 * h + 2)
                    pe.matmul(MX[:, i, 0:(i + 1) * P], xq[:, i * P:(i + 1) * P], xk[:, 0:(i + 1) * P], start=True,
                              stop=True).then_inc(s["scores"], 1)

            def tail_a(h):
                yield
                pe.wait_ge(s["probs_ok"], 4 * h + 4)
                for kt in range(NC):
                    bank, col = (kt, 0) if kt < 3 else (2, 2 * P)
                    for i in range(kt, NC):
                        o = (i * (i + 1) // 2 + kt) * P
                        last = pe.transpose(MX[:, bank, col + (i - kt) * P:col + (i - kt + 1) * P], probs[:, o:o + P],
                                            ident[:])
                    if kt != 2:
                        last.then_inc(s["probT_ps"], 1)
                        yield
                for kt in range(NC):
                    if kt < 3:
                        pe.wait_ge(s["probT_ok"], 3 * h + kt + 1)
                    o = sum(NC - n for n in range(kt)) * P
                    last = pe.matmul(MX[:, 3, kt * P:TP], vtok[:, kt, :], probT[:, o:o + (NC - kt) * P],
                                     start=kt == 0, stop=kt == NC - 1)
                    if kt == 1:
                        yield
                last.then_inc(s["attn_ps"], 1)

            def own_b(h):
                for j in range(3):
                    yield from idle((11, 7, 8)[j])
                    pe.wait_ge(s["proj_sb"], 8 * h + (2 * T_B + 2 * (j + 1)))
                    if j == 0 and (not isinstance(h, int) or h > 0):
                        pe.wait_ge(s["d_add"], 2 * h)
                        pe.wait_ge(s["crow_ok"], 3 * h)
                    elif j > 0:
                        pe.wait_ge(s["crow_ok"], 3 * h + j)
                    pe.transpose(MD[0:11, 1, 0:P], xq[:, 3 + TP - 3:3 + TT], ident[:]).then_inc(s["crow_ps"], 1)

            def mix_b(h):
                chunks = range(NC)
                yield
                pe.wait_ge(s["q_silu"], h + 1)
                pe.wait_ge(s["kv_silu"], 2 * h + 2)
                for c in chunks:
                    pe.transpose(mx(0)[:, c, :], xk[:, c * P:(c + 1) * P], ident[:])
                for c in chunks:
                    last = pe.transpose(mx(2)[:, c, :], cq[:, c * P:(c + 1) * P], ident[:])
                last.then_inc(s["mix_T1"], 1)
                for c in chunks:
                    last = pe.transpose(mx(1)[:, c, :], xv[:, c * P:(c + 1) * P], ident[:])
                last.then_inc(s["mix_T1"], 1)
                yield
                pe.wait_ge(s["hg_ok"], h + 1)
                for c in chunks:
                    last = pe.transpose(mx(3)[:, c, :], hg[:, 1, c:c + 1].to_broadcast((P, P)), ident[:])
                last.then_inc(s["mix_gb"], 1)
                yield from idle(2)
                pe.wait_ge(s["mix_tok"], 3 * h + 3)
                for c in chunks:
                    last = pe.transpose(mx(0)[:, c, :], b_kb[:, c, :], ident[:])
                last.then_inc(s["mix_kbT_ps"], 1)
                yield
                pe.wait_ge(s["mix_kbT"], h + 1)
                for c in chunks:
                    last = pe.matmul(mx(1)[:, c, :], xk[:, c * P:(c + 1) * P], b_kbT[:, c, :], start=True, stop=True)
                last.then_inc(s["mix_kk"], 1)
                for c in chunks:
                    last = pe.matmul(mx(2)[:, c, :], xk[:, c * P:(c + 1) * P], cq[:, c * P:(c + 1) * P], start=True,
                                     stop=True)
                last.then_inc(s["mix_qk"], 1)
                yield from idle(2)
                pe.wait_ge(s["mix_U0"], h + 1)
                for c in chunks:
                    last = pe.transpose(mx(0)[:, c, :], b_U[:, c, :], ident[:])
                last.then_inc(s["mix_T_ps"], 1)
                for n in range(1, LEVELS):
                    yield
                    pe.wait_ge(s["mix_B"], LEVELS * h + n + 1)
                    if n == 1:
                        pe.wait_ge(s["mix_T"], h + 1)
                        pe.wait_ge(s["mix_A"], h + 1)
                    else:
                        pe.wait_ge(s["mix_UT"], UTS * h + 3 * (n - 1) - 1)
                    for c in chunks:
                        last = pe.matmul(blocks(mx(1)[:, c, :], n, 0), b_B[n % 2][:, c, :],
                                         blocks(b_T[:, c, :], n, 0), start=True, stop=True)
                    last.then_inc(s["mix_Y_ps"], 1)
                    yield
                    pe.wait_ge(s["mix_Y"], (LEVELS - 1) * h + n)
                    if n == 1:
                        pe.wait_ge(s["mix_QK"], h + 1)
                    else:
                        pe.wait_ge(s["mix_UT"], UTS * h + 3 * (n - 1))
                    for c in chunks:
                        last = pe.matmul(blocks(mx(2)[:, c, :], n, 1), b_Y[:, c, :], blocks(b_U[:, c, :], n, 1),
                                         start=True, stop=True)
                    last.then_inc(s["mix_Z"], 1)
                    if n < LEVELS - 1:
                        for c in chunks:
                            last = pe.matmul(blocks(mx(3)[:, c, :], n, 0), b_U[:, c, :],
                                             blocks(b_Y[:, c, :], n, 0), start=True, stop=True)
                        last.then_inc(s["mix_Z"], 1)
                for c in chunks:
                    if c > 0:
                        yield
                        pe.wait_ge(s["ch_S"], NC * h + c)
                        pe.matmul(MX[:, 0, 0:P], b_kbT[:, c, :], S, start=True, stop=True).then_inc(s["ch_kS"], 1)
                        if c > 1:
                            pe.wait_ge(s["ch_o1"], (NC - 1) * h + c - 1)
                        pe.matmul(MX[:, 1, 0:P], cq[:, c * P:(c + 1) * P], S, start=True, stop=True).then_inc(
                            s["ch_o_ps"], 1)
                    yield
                    if c == 0:
                        pe.wait_ge(s["mix_UT"], UTS * h + UTS)
                    pe.wait_ge(s["ch_r"], NC * h + c + 1)
                    pe.matmul(MX[:, 2, 0:P], b_U[:, c, :], rr, start=True, stop=True).then_inc(s["ch_v_ps"], 1)
                    yield
                    pe.wait_ge(s["ch_v"], NC * h + c + 1)
                    pe.matmul(MX[:, 0, 0:P], b_kdec[:, c, :], vn, start=True, stop=True).then_inc(s["ch_S_ps"], 1)
                    if c > 0:
                        pe.wait_ge(s["ch_o"], NC * h + c)
                    pe.matmul(MX[:, 3, 0:P], b_QK[:, c, :], vn, start=True, stop=True).then_inc(s["ch_o_ps"], 1)
                yield
                pe.wait_ge(s["o_n"], h + 1)
                for c in chunks:
                    last = pe.transpose(mx(0)[:, c, :], b_o[:, c, :], ident[:])
                last.then_inc(s["o_T"], 1)

            def new_scores():
                pe.wait_ge(s["qkp"], 1)
                pe.wait_ge(s["gates_act"], 5)
                for b in range(NB):
                    last = pe.matmul(MD[0:NH, 0, b:b + 1], qks[:, :, b], ones[:, 0:1], start=True, stop=True)
                last.then_inc(s["snew_ps"], 1)
                yield

            def delta_decode(h):
                yield from idle(2)
                pe.wait_ge(s["dkq"], h + 1)
                pe.wait_ge(s["S0_in"], 16 * h + 16)
                pe.wait_ge(s["crow_ok"], 3 * h + 3)
                pe.matmul(MD[:, 1, 0:24], ones[:], dd[:, 2:5, :].rearrange("p a b -> p (a b)"), start=True, stop=True)
                for b in range(NB):
                    last = pe.matmul(MD[:, 1, 32 + 2 * b:34 + 2 * b], S0[:, b, :], dd[:, 0:2, b], start=True,
                                     stop=True)
                last.then_inc(s["d_sum"], 1)
                yield from idle(3)
                pe.wait_ge(s["d_vec"], h + 1)
                pe.transpose(MD[0:NB, 1, 0:P], dd[:, 5, :], ident[:])
                pe.transpose(MD[0:NB, 1, P:2 * P], dd[:, 6, :], ident[:])
                pe.matmul(MD[:, 1, 2 * P:2 * P + NB], ones[:], dd[:, 8, :], start=True, stop=True).then_inc(
                    s["d_rows"], 1)
                yield from idle(2)
                for n in range(2):
                    yield from idle(n + 1)
                    pe.wait_ge(s["d_vexp"], 2 * h + n + 1)
                    if n == 0:
                        pe.wait_ge(s["d_rows_ok"], h + 1)
                        pe.wait_ge(s["gated_bd"], h + 1)
                    else:
                        pe.wait_ge(s["d_add"], 2 * h + 1)
                    pe.matmul(MD[:, 1, :], kvr[:, 0, :], vexp.rearrange("p b e -> p (b e)"), start=True,
                              stop=True).then_inc(s["d_outer"], 1)

            def attn_decode(b):
                yield from idle(17)
                pe.wait_ge(s["snew_ok"], 1)
                pe.wait_ge(s["red"], 3 * b + 3)
                for n in range(3):
                    last = pe.transpose(MD[0:NH, 0, n * P:(n + 1) * P], sc[:, n, :], ident[:])
                last.then_inc(s["sc_T"], 1)
                yield from idle(5)
                pe.wait_ge(s["p_norm"], b + 1)
                pe.matmul(MD[:, 0, 3 * NH:4 * NH], ones[0:NH, :], dg[:], start=True, stop=True)
                for n in range(3):
                    last = pe.transpose(MD[:, 0, n * NH:(n + 1) * NH], pd[:, n, :], ident[0:NH, 0:NH])
                last.then_inc(s["p_T"], 1)
                yield from idle(8)
                pe.wait_ge(s["pv_sum"], b + 1)
                for hh in range(NH):
                    last = pe.matmul(MD[:, 0, 64 + hh:65 + hh], V_TILE[0][:, hh * HD:(hh + 1) * HD], ones[:, 0:1],
                                     start=True, stop=True)
                last.then_inc(s["pv_ps"], 1)

            pe.wait_ge(s["consts"], 96)
            pe.wait_ge(s["memset_ok"], 1)
            project(0, 0, [], first=True)
            ga = gates()
            first_a = own_a(0)
            for j in range(4):
                project(T_A + j, (1 + j) % 2, [ga, first_a])
            with pe.Fori(1, NH) as h:
                work = [tail_a(h - 1), own_a(h)]
                for j in range(4):
                    project(4 * h + (T_A + j), (1 + j) % 2, work)
            work = [tail_a(NH - 1), own_b(0), new_scores(), attn_decode(0)]
            for j in range(4):
                project(T_B + j, (1 + j) % 2, work)
            pe.wait_ge(s["gated_a"], NH)
            with pe.Fori(1, NH) as h:
                work = [mix_b(h - 1), delta_decode(h - 1), own_b(h), attn_decode(h)]
                for j in range(4):
                    project(4 * h + (T_B + j), (1 + j) % 2, work)

            def unit(slot, p, half, start, stop):
                par, q = (T_O + slot) % 2, out_unit(slot, p)[1]
                tok = slice(half * HALF, (half + 1) * HALF)
                out = PJ[:, half, 0:HALF]
                if half == 0:
                    pe.wait_ge(lo_sem(p), 2 * (T_O + slot) + p // 2 + 1)
                for i in range(4):
                    wh, wl, k = w_hi[:, par, 4 * p + i, :], w_lo[:, par, 4 * p + i, :], 4 * q + i
                    if half == 0:
                        pe.wait_ge(s["g_lo"], k + 1)
                    pe.matmul(out, wh, h_hi[:, k, tok], start=start and i == 0, stop=False)
                    pe.matmul(out, wh, h_lo[:, k, tok], start=False, stop=False)
                    last = pe.matmul(out, wl, h_hi[:, k, tok], start=False, stop=stop and i == 3)
                return last

            work = [mix_b(NH - 1), delta_decode(NH - 1)]
            for n in range(40):
                if n < 2 * UNITS:
                    u, half = n // 2, n % 2
                    slot, p = u // 4, u % 4
                    j, q = out_unit(slot, p)
                    if q == 0 and j == 0:
                        pe.wait_ge(s["proj_sb"], 2 * T_O - 1 + half)
                    elif q == 0:
                        pe.wait_ge(s["part_sb"], 2 * (j - 1) + half + 1)
                    last = unit(slot, p, half, q == 0, q == 2 and j < PARTS)
                    if half == 1:
                        last.then_inc(s["w_used"], 1) if p < NQ - 1 else last.then_inc(s["proj_ps"], 2)
                    elif q == 2 and j < PARTS:
                        last.then_inc(s["part_ps"], 1)
                for g in work:
                    next(g, None)
            for half in range(2):
                unit(PARTS - 1, NQ - 1, half, False, True).then_inc(s["proj_ps"], 1)
            for p in range(NQ):
                for half in range(2):
                    pe.wait_ge(s["proj_sb"], 2 * T_O + 2 * p + half + 1)
                    last = unit(PARTS, p, half, True, True)
                    if half == 0:
                        last.then_inc(s["rest_ps"], 1)
                    else:
                        last.then_inc(s["w_used"], 1) if p < NQ - 1 else last.then_inc(s["proj_ps"], 2)
            with pe.Fori(0, (KT - PARTS - 1) // 2) as i:
                for n in range(2):
                    project(2 * i + (T_O + PARTS + 1 + n), n, [])
            project(T_O + KT - 1, 0, [])
            pe.wait_ge(s["sq_y"], 2 * KT)
            for c in range(NC + 1):
                n = P if c < NC else NB
                last = pe.matmul(MD[0:n, 0, c:c + 1], acc[:, c * P:c * P + n], ones[:, 0:1], start=True, stop=True)
            last.then_inc(s["ss_y"], 1)
            pe.wait_ge(s["proj_sb"], 2 * (T_O + KT))
            for c in range(NC + 1):
                n = P if c < NC else NB
                for b in range(4):
                    if c > 0:
                        pe.wait_ge(s["y_out_ok"], 4 * (c - 1) + b + 1)
                    for k in range(4):
                        last = pe.transpose(MX[0:n, b, k * P:(k + 1) * P], gated[:, 4 * b + k, c * P:c * P + n],
                                            ident[:])
                    last.then_inc(s["y_T"], 1)

        @block.scalar
        def _(act):
            ch = Chain(act, s["act_chain"])

            def hi(T, par, q, n=P, first=False):
                act.wait_ge(raw_in[q], 16 * T + 16)
                if not first:
                    if q < NQ - 1:
                        act.wait_ge(s["w_used"], 3 * T - 6 + q + 1)
                    else:
                        act.wait_ge(s["proj_ps"], 2 * T - 2)
                act.activation(w_hi[:, par, 4 * q:4 * q + 4, 0:n], w_raw[:, q, :, 0:n], ACT.Copy).then_inc(
                    s["w_hi_ok"], 1)

            def rsqrt(out, in_, scale, ok):
                ch.link(act.activation(out, in_, ACT.Ln, scale=scale, bias=EPS))
                act.activation(out, out, ACT.Exp, scale=-0.5).then_inc(ok, 1)

            def sigmoid(out, ok):
                ch.link(act.activation(out, out, ACT.Exp, scale=-1.0))
                ch.link(act.activation(out, out, ACT.Ln, bias=1.0))
                act.activation(out, out, ACT.Exp, scale=-1.0).then_inc(ok, 1)

            def sigmoid_steps(out, ok):
                ch.link(act.activation(out, out, ACT.Exp, scale=-1.0))
                yield
                ch.link(act.activation(out, out, ACT.Ln, bias=1.0))
                yield
                act.activation(out, out, ACT.Exp, scale=-1.0).then_inc(ok, 1)

            def copy_out(T, half, dst, off=0):
                act.wait_ge(s["proj_ps"], 2 * T + half + 1)
                o = off + half * HALF
                n = dst.shape[0]
                act.activation(dst[:, o:o + HALF], PJ[0:n, half, 0:HALF], ACT.Copy).then_inc(s["proj_sb"], 1)

            def head(T, dsts, before, work, guards):
                for j in range(4):
                    for seg in range(SEGS):
                        if seg == 0:
                            dst, off = before if j == 0 else dsts[j - 1]
                            if dst is not None:
                                copy_out(T + (j - 1), 1, dst, off)
                        for g in work:
                            next(g, None)
                        if seg == 4:
                            guards(j)
                            copy_out(T + j, 0, dsts[j][0][:], dsts[j][1])
                        if seg % 2 == 0:
                            hi(T + (j + 1), j % 2, seg // 2)

            A_DST = [(xq[:], 0), (xk[:], 0), (xv[:], 0), (xz[:], 0)]
            B_DST = [(xq[:], 3), (xq[:], 3), (xq[:], 3), (xz[:], 0)]

            def guards_a(h):
                def guard(j):
                    if isinstance(h, int) and h == 0:
                        return
                    if j == 0:
                        act.wait_ge(s["scores"], 4 * h)
                        act.wait_ge(s["stash_q"], h)
                        act.wait_ge(s["stash_k"], h)
                    if j == 2:
                        act.wait_ge(s["stash_v"], h)
                    if j == 3:
                        act.wait_ge(s["z_ok"], h)
                return guard

            def guards_b(h):
                def guard(j):
                    if isinstance(h, int) and h == 0 and j == 0:
                        act.wait_ge(s["scores"], 4 * NH)
                        act.wait_ge(s["stash_q"], NH)
                        act.wait_ge(s["zero_cols"], 1)
                    elif j == 0:
                        act.wait_ge(s["conv_ok"], 3 * h)
                        act.wait_ge(s["crow_ps"], 3 * h)
                    if j in (1, 2):
                        act.wait_ge(s["conv_ok"], 3 * h + j)
                        act.wait_ge(s["crow_ps"], 3 * h + j)
                    if j == 3:
                        if isinstance(h, int) and h == 0:
                            act.wait_ge(s["z_ok"], NH)
                        else:
                            act.wait_ge(s["z_ok_b"], h)
                return guard

            act.preload_act_table_set("natural_log_exp_and_others")
            def x_rstd(n, c):
                rows_ = P if c < NC else NB
                act.wait_ge(x_in[c], 16)
                if n > 0:
                    act.wait_ge(s["x_sq"], n)
                act.activation(junk[0:rows_], xin[:, c, :] if c < NC else xs_in, ACT.Square,
                               accum_out=ssum[0:rows_, c:c + 1]).then_inc(s["x_sq"], 1)
                act.wait_ge(s["x_sq"], n + 1)
                rsqrt(rstd[0:rows_, c:c + 1], ssum[0:rows_, c:c + 1], 1.0 / D, s["rstd_ok"])

            def x_hi(c):
                for b in range(4):
                    act.wait_ge(s["hT_ps"], 4 * c + b + 2)
                    act.activation(h_hi[:, 4 * b:4 * b + 4, c * P:(c + 1) * P],
                                   MX[:, b].rearrange("p (k t) -> p k t", k=4), ACT.Copy).then_inc(s["hT_hi"], 1)

            x_rstd(0, NC)
            for c in range(NC - 1):
                x_rstd(c + 1, c)
            act.wait_ge(s["vec_ps"], 1)
            act.activation(vecT[:], MD[:, 0, 0:KT + 1], ACT.Copy)
            for m in range(2):
                act.wait_ge(s["st_ps"], 12 * m + 12)
                act.activation(stT[:, 12 * m:12 * m + 12, :].rearrange("p m w -> p (m w)"), MX[:, 2 + m, 0:336],
                               ACT.Copy).then_inc(s["st_sb"], 1)
            act.wait_ge(s["hT_ps"], 1)
            act.activation(h_hi[:, :, TP:TT], MD[:, 1, 0:P].rearrange("p (k b) -> p k b", k=KT), ACT.Copy).then_inc(
                s["hT_hi"], 1)
            x_hi(0)
            x_rstd(NC, NC - 1)
            x_hi(1)
            x_hi(2)
            x_hi(3)
            act.wait_ge(s["memset_ok"], 1)
            for q in range(NQ):
                hi(0, 0, q, 16, first=True)

            def gates():
                yield from idle(8)
                act.wait_ge(s["gates_pe"], 1)
                act.activation(gt[:, 0:NC].rearrange("p c a h -> p (c a h)"), MD[:, 0, 0:64], ACT.Copy)
                act.activation(gt[0:NB, NC].rearrange("p a h -> p (a h)"), MD[0:NB, 0, 64:80], ACT.Copy).then_inc(
                    s["gates_act"], 1)
                yield from idle(1)
                act.wait_ge(s["gates_dve"], 1)
                ch.link(act.activation(gw[:, 0], gt[:, :, 0, :], ACT.Exp, scale=-1.0))
                ch.link(act.activation(gw[:, 2], gw[:, 1], ACT.Exp, scale=-1.0))
                act.activation(gw[:, 2], gw[:, 2], ACT.Ln, bias=1.0)
                act.wait_ge(s["consts"], 96)
                act.activation(gneg[:], adt[:, 0], ACT.Exp).then_inc(s["gates_act"], 1)
                yield from idle(3)
                act.wait_ge(s["gates_pe"], 2)
                cum = MD[:, 1, 0:32].rearrange("p (c h) -> p c h", c=NC)
                act.activation(G6[:, 1], cum, ACT.Copy)
                act.activation(G6[:, 3], cum, ACT.Exp)
                act.activation(G6[:, 5], MD[:, 1, 32:64].rearrange("p (c h) -> p c h", c=NC), ACT.Exp)
                act.activation(gw[0:NB, 0, NC, :], gw[0:NB, 3, NC, :], ACT.Exp).then_inc(s["gates_act"], 1)
                yield
                act.wait_ge(s["gates_dve"], 3)
                act.activation(G6[:, 4], G6[:, 4], ACT.Exp).then_inc(s["gates_act"], 1)
                yield from idle(2)
                act.wait_ge(s["gates_pe"], 3)
                act.activation(bgs[:].rearrange("p a h b -> p (a h b)"), MD[:, 0, 0:P], ACT.Copy).then_inc(
                    s["gates_act"], 1)

            def own_a(h):
                first = isinstance(h, int) and h == 0
                yield from idle(19)
                act.wait_ge(s["k_T"], h + 1)
                if not first:
                    act.wait_ge(s["k_out"], 16 * h)
                    act.wait_ge(s["row_out"], 16 * h)
                    act.wait_ge(s["qrow_out"], 16 * h)
                act.activation(ktok, mx(2), ACT.Copy).then_inc(s["ktok_ok"], 1)
                act.activation(qkrow.rearrange("p a d -> p (a d)"), MX[0:NB, 3, 0:2 * P], ACT.Copy).then_inc(
                    s["ktok_ok"], 1)
                yield
                act.wait_ge(s["ktok_ok"], 2 * h + 2)
                act.dma_start(kp_v[:, :, h, :], ktok).then_inc(s["k_out"], 16)
                act.dma_start(scratch_q[:, bass.ds(h * HD, HD)], qkrow[:, 0]).then_inc(s["qrow_out"], 16)
                act.dma_start(wk_s[0, :, 0, h, :], qkrow[:, 1]).then_inc(s["row_out"], 16)
                yield from idle(5)
                act.wait_ge(s["v_T"], h + 1)
                if not first:
                    act.wait_ge(s["v_out"], 32 * h)
                    act.wait_ge(s["attn_ps"], h)
                act.activation(vtok, mx(2), ACT.Copy).then_inc(s["vtok_ok"], 1)
                act.activation(vrow, MX[0:NB, 3, 0:P], ACT.Copy).then_inc(s["vtok_ok"], 1)
                yield
                act.wait_ge(s["vtok_ok"], 2 * h + 2)
                act.dma_start(vp_v[:, :, h, :], vtok).then_inc(s["v_out"], 16)
                act.dma_start(wv_s[0, :, 0, h, :], vrow).then_inc(s["v_out"], 16)
                yield from idle(3)
                act.wait_ge(s["negmax"], h + 1)
                for i in range(NC):
                    p = probs[:, i * (i + 1) // 2 * P:(i + 1) * (i + 2) // 2 * P]
                    act.activation(p, p, ACT.Exp, bias=stat[:, 0, i:i + 1], accum_out=stat[:, 1, i:i + 1]).then_inc(
                        s["expd"], 1)

            def tail_a(h):
                yield
                act.wait_ge(s["z_low"], h + 1)
                sigmoid(ez[:], s["z_sig"])
                for n, (o, w) in enumerate(((0, 4), (4, 3), (7, 3))):
                    act.wait_ge(s["probT_ps"], 3 * h + n + 1)
                    act.activation(probT[:, o * P:(o + w) * P], MX[:, n, 0:w * P], ACT.Copy).then_inc(
                        s["probT_ok"], 1)
                    yield

            def own_b(h):
                for j, m in enumerate((1, 2, 0)):
                    yield from idle((11, 4, 5)[j])
                    act.wait_ge(s["crow_ps"], 3 * h + j + 1)
                    if j > 0 or not isinstance(h, int) or h > 0:
                        act.wait_ge(s["crow_out"], 32 * (3 * h + j))
                    act.activation(rows, MD[0:11, 1, 0:P], ACT.Copy).then_inc(s["crow_ok"], 1)
                    yield
                    act.wait_ge(s["conv_ok"], 3 * h + j + 1)
                    if j == 0:
                        act.wait_ge(s["z_ok"], NH)
                        if not isinstance(h, int) or h > 0:
                            act.wait_ge(s["z_ok_b"], h)
                    else:
                        act.wait_ge(s["kv_silu"], 2 * h + j)
                    yield from sigmoid_steps(ez[:], s["conv_sig"])
                    act.wait_ge(s["crow_ok"], 3 * h + j + 1)
                    act.dma_start(cv_p[0, 0, :, bass.ds((h + m * NH) * P, P)], rows[0:3]).then_inc(s["crow_out"], 16)
                    act.dma_start(cv_s[0, :, 2, bass.ds((h + m * NH) * P, P)], rows[3:11]).then_inc(
                        s["crow_out"], 16)

            def mix_b(h):
                yield
                act.wait_ge(s["q_silu"], h + 1)
                act.wait_ge(s["mix_T1"], 2 * h + 1)
                for n, x in enumerate((0, 2)):
                    for c in range(NC):
                        act.activation((b_o, b_Y)[n][:, c, :], mx(x)[:, c, :], ACT.Square,
                                       accum_out=sk[:, n, c:c + 1]).then_inc(s["mix_ss"], 1)
                yield
                act.wait_ge(s["mix_ss"], 2 * NC * h + 2 * NC)
                ch.link(act.activation(lnss[:], sk[:, 0:2, :], ACT.Ln, bias=EPS))
                act.activation(lnrk[:], lnss[:, 0, :], ACT.Copy, scale=-0.5).then_inc(s["mix_lnrk"], 1)
                act.activation(sk[:, 0:2, :], lnss[:], ACT.Exp, scale=-0.5).then_inc(s["mix_rs"], 1)
                yield
                act.wait_ge(s["mix_arg"], h + 1)
                act.wait_ge(s["mix_lnrk"], h + 1)
                for c in range(NC):
                    act.activation(b_D[:, c, :], b_D[:, c, :], ACT.Exp, bias=lnrk[:, c:c + 1]).then_inc(s["mix_D"], 1)
                yield
                act.wait_ge(s["mix_kbT_ps"], h + 1)
                act.activation(b_kbT, mx(0), ACT.Copy).then_inc(s["mix_kbT"], 1)
                yield
                act.wait_ge(s["z_low"], NH + h + 1)
                sigmoid(ez[:], s["z_sig_b"])
                yield from idle(2)
                act.wait_ge(s["mix_T_ps"], h + 1)
                act.activation(b_T, mx(0), ACT.Copy).then_inc(s["mix_T"], 1)
                for n in range(1, LEVELS):
                    yield
                    act.wait_ge(s["mix_Y_ps"], (LEVELS - 1) * h + n)
                    act.activation(all_blocks(b_Y, n, 0), all_blocks(mx(1), n, 0), ACT.Copy).then_inc(s["mix_Y"], 1)
                    yield
                for c in range(NC):
                    if c > 0:
                        yield
                        act.wait_ge(s["ch_o_ps"], (2 * NC - 1) * h + 2 * c)
                        act.wait_ge(s["o_sq"], NC * h + c)
                        act.activation(o1, MX[:, 1, 0:P], ACT.Copy, scale=oq[:, c:c + 1]).then_inc(s["ch_o1"], 1)
                    yield
                    act.wait_ge(s["ch_v_ps"], NC * h + c + 1)
                    act.activation(vn, MX[:, 2, 0:P], ACT.Copy).then_inc(s["ch_v"], 1)
                    yield
                    act.wait_ge(s["ch_o"], NC * h + c + 1)
                    act.activation(o1, b_o[:, c, :], ACT.Square, accum_out=on[:, 0, c:c + 1]).then_inc(
                        s["o_sq"], 1)
                act.wait_ge(s["o_sq"], NC * h + NC)
                rsqrt(on[:, 1, :], on[:, 0, :], 1.0 / HD, s["on_rs"])

            def delta_decode(h):
                yield from idle(2)
                act.wait_ge(s["d_sum"], h + 1)
                rsqrt(dd[:, 9:11, :], MD[:, 1, 0:2 * NB].rearrange("p (a b) -> p a b", a=2), 1.0, s["d_rs"])
                yield from idle(3)
                act.wait_ge(s["d_rows"], h + 1)
                rsqrt(dd[:, 10, :], MD[:, 1, 2 * P:2 * P + NB], 1.0 / HD, s["d_rs2"])
                act.activation(kvr.rearrange("p a d -> p (a d)"), MD[0:NB, 1, 0:2 * P], ACT.Copy).then_inc(
                    s["d_rows_ok"], 1)

            def attn_decode(b):
                yield from idle(18)
                act.wait_ge(s["row_out"], 16 * NH)
                act.wait_ge(s["qrow_out"], 16 * NH)
                act.wait_ge(s["v_out"], 32 * NH)
                act.wait_ge(s["sc_max"], b + 1)
                act.activation(pd.rearrange("p a t -> p (a t)"), MD[0:NH, 0, 0:3 * P], ACT.Exp, bias=ds[:, 1:2],
                               scale=SCALE, accum_out=ds[:, 3:4])
                act.activation(ds[:, 4:5], ds[:, 2:3], ACT.Exp).then_inc(s["p_exp"], 1)
                yield from idle(4)
                act.wait_ge(s["p_T"], b + 1)
                act.activation(pT[:].rearrange("p a h -> p (a h)"), MD[:, 0, 0:4 * NH], ACT.Copy).then_inc(
                    s["pT_ok"], 1)

            for seg in range(SEGS):
                if seg % 2 == 0:
                    hi(1, 1, seg // 2, first=True)
                if seg == 4:
                    copy_out(0, 0, xba)
            ga, first_a = gates(), own_a(0)
            head(T_A, A_DST, (xba, 0), [ga, first_a], guards_a(0))
            ch.end(1)
            with act.Fori(1, NH) as h:
                ch.at(h, 1, 2)
                head(4 * h + T_A, A_DST, A_DST[3], [tail_a(h - 1), own_a(h)], guards_a(h))
            ch.end(NH - 1)
            head(T_B, B_DST, A_DST[3], [tail_a(NH - 1), own_b(0), attn_decode(0)], guards_b(0))
            ch.end(1)
            act.wait_ge(s["gated_a"], NH)
            act.wait_ge(s["k_out"], 16 * NH)
            act.wait_ge(s["v_out"], 32 * NH)
            with act.Fori(1, NH) as h:
                ch.at(h, 1, 12)
                head(4 * h + T_B, B_DST, B_DST[3],
                     [mix_b(h - 1), own_b(h), delta_decode(h - 1), attn_decode(h)], guards_b(h))
            ch.end(NH - 1)
            copy_out(T_O - 1, 1, xz[:])

            def done(eng, slot, p, half, ps, n):
                if half == 0:
                    eng.wait_ge(ps, n)
                elif p < NQ - 1:
                    eng.wait_ge(s["w_used"], 3 * (T_O + slot) + p + 1)
                else:
                    eng.wait_ge(s["proj_ps"], 2 * (T_O + slot) + 2)

            def g_hi(k):
                act.activation(h_hi[:, k, :], gated[:, k, :], ACT.Copy).then_inc(s["g_hi"], 1)

            act.wait_ge(s["proj_ps"], 2 * T_O)
            act.wait_ge(s["gated_a"], NH)
            act.wait_ge(s["gated_ad"], NB)
            act.wait_ge(s["gated_b"], NH - 1)
            act.wait_ge(s["gated_bd"], NH - 1)
            work = [mix_b(NH - 1), delta_decode(NH - 1)]
            for n in range(40):
                for k in splits(n):
                    g_hi(k)
                if n < 2 * UNITS:
                    u, half = n // 2, n % 2
                    j, q = out_unit(u // 4, u % 4)
                    if q == 2 and j < PARTS:
                        done(act, u // 4, u % 4, half, s["part_ps"], j + 1)
                        act.wait_ge(s["g_lo"], j + 1)
                        act.activation(gated[:, j, half * HALF:(half + 1) * HALF], PJ[:, half, 0:HALF],
                                       ACT.Copy).then_inc(s["part_sb"], 1)
                for g in work:
                    next(g, None)
                if n % 2 == 0 and n < 8 * PARTS:
                    slot = n // 8
                    hi(T_O + slot + 1, (T_O + slot + 1) % 2, n // 2 % 4)
            act.wait_ge(s["gated_b"], NH)
            act.wait_ge(s["gated_bd"], NH)
            g_hi(KT - 1)
            for q in range(NQ):
                hi(T_O + PARTS + 1, 0, q)
            with act.Fori(0, (KT - PARTS - 1) // 2) as i:
                for n in range(2):
                    for q in range(NQ):
                        hi(2 * i + (T_O + PARTS + 2 + n), 1 - n, q)
            ch.end(1)
            act.wait_ge(s["fin_rs"], 1)
            rsqrt(fin[:], fin[:], 1.0 / D, s["fin_rs"])

        @block.vector
        def _(dve):
            ch = Chain(dve, s["dve_chain"])
            link = ch.link

            def lo(T, par, q, n=P):
                dve.wait_ge(s["w_hi_ok"], 4 * T + q + 1)
                dve.tensor_tensor(w_lo[:, par, 4 * q:4 * q + 4, 0:n], w_raw[:, q, :, 0:n],
                                  w_hi[:, par, 4 * q:4 * q + 4, 0:n].bitcast(F32), ALU.subtract).then_inc(
                    s["w_lo_dve"], 1)

            def head(T, work):
                for j in range(4):
                    for seg in range(SEGS):
                        for g in work:
                            next(g, None)
                        if seg % 4 == 0:
                            lo(T + (j + 1), j % 2, seg // 2)

            dve.memset(gt, 0.0)
            dve.memset(ones[:], 1.0)
            dve.memset(w_hi[:, 0, :, :].bitcast(F32), 0.0)
            dve.memset(w_lo[:, 0, :, :].bitcast(F32), 0.0).then_inc(s["memset_ok"], 1)

            def x_scale(n, c):
                rows_ = P if c < NC else NB
                x = xin[:, c, :] if c < NC else xs_in
                dve.wait_ge(s["rstd_ok"], n + 1)
                dve.wait_ge(s["g_in"], 32)
                for i in range(2):
                    xh = x[:, i * WA:(i + 1) * WA]
                    dve.scalar_tensor_tensor(xh, xh, rstd[0:rows_, c:c + 1], g_bc[i][0:rows_], ALU.mult,
                                             ALU.mult).then_inc(s["x_scaled"], 1)

            def x_lo(c):
                for b in range(4):
                    dve.wait_ge(s["hT_hi"], 4 * c + b + 2)
                    part = (slice(None), slice(4 * b, 4 * b + 4), slice(c * P, (c + 1) * P))
                    dve.tensor_tensor(h_lo[part], MX[:, b].rearrange("p (k t) -> p k t", k=4),
                                      h_hi[part].bitcast(F32), ALU.subtract).then_inc(s["hT_lo"], 1)

            x_scale(0, NC)
            x_scale(1, 0)
            x_scale(2, 1)
            dve.wait_ge(s["hT_hi"], 1)
            dve.tensor_tensor(h_lo[:, :, TP:TT], MD[:, 1, 0:P].rearrange("p (k b) -> p k b", k=KT),
                              h_hi[:, :, TP:TT].bitcast(F32), ALU.subtract).then_inc(s["hT_lo"], 1)
            x_lo(0)
            x_scale(3, 2)
            x_lo(1)
            x_scale(4, 3)
            x_lo(2)
            x_lo(3)
            for q in (0, 2):
                lo(0, 0, q, 16)

            def gates():
                yield from idle(8)
                dve.wait_ge(s["gates_act"], 1)
                dve.wait_ge(s["consts"], 96)
                a = gt[:, :, 1, :]
                dtb = adt[:, 1].unsqueeze(1).to_broadcast((P, NC + 1, NH))
                link(dve.tensor_tensor(a, a, dtb, ALU.add))
                link(dve.tensor_scalar(gw[:, 1], a, -1.0, None, ALU.mult))
                dve.tensor_tensor(gw[:, 1], gw[:, 1], a, ALU.max).then_inc(s["gates_dve"], 1)
                yield
                yield
                dve.wait_ge(s["gates_act"], 2)
                link(dve.tensor_scalar(gw[:, 0], gw[:, 0], 1.0, None, ALU.add))
                link(dve.reciprocal(gw[:, 0], gw[:, 0]))
                link(dve.tensor_scalar(a, a, 0.0, None, ALU.max))
                link(dve.tensor_tensor(a, a, gw[:, 2], ALU.add))
                link(dve.tensor_scalar(gneg[:], gneg[:], -1.0, None, ALU.mult))
                dve.tensor_copy(G6[:, 0], gw[:, 0, 0:NC, :])
                ident8 = ident[0:NB, 0:NB].unsqueeze(1).to_broadcast((NB, NH, NB))
                link(dve.tensor_tensor(dgs[:, 0], gw[0:NB, 0, NC, :].unsqueeze(2).to_broadcast((NB, NH, NB)), ident8,
                                       ALU.mult))
                dve.tensor_tensor(gw[:, 3], a, gneg[:].unsqueeze(1).to_broadcast((P, NC + 1, NH)),
                                  ALU.mult).then_inc(s["gates_dve"], 1)
                yield from idle(3)
                dve.wait_ge(s["gates_act"], 3)
                tot = MD[:, 1, 32:64].rearrange("p (c h) -> p c h", c=NC)
                dve.tensor_tensor(G6[:, 4], tot, G6[:, 1], ALU.subtract).then_inc(s["gates_dve"], 1)
                dve.tensor_scalar(G6[:, 2], G6[:, 3], -1.0, None, ALU.mult).then_inc(s["gates_dve"], 1)
                dve.tensor_tensor(dgs[:, 1], gw[0:NB, 0, NC, :].unsqueeze(2).to_broadcast((NB, NH, NB)), ident8,
                                  ALU.mult).then_inc(s["gates_dve"], 1)

            def rope_on(x, ps_ready, n, ok):
                t1, t2 = acc[0:ROT, :], ez[0:ROT, :]
                dve.wait_ge(ps_ready, n)
                link(dve.tensor_tensor(t1, x[0:ROT, 0:TT], rope[:, 0, :], ALU.mult))
                link(dve.tensor_tensor(t2.rearrange("p (a t) -> p a t", a=2), MX[0:ROT, 0:2, 0:HALF],
                                       rope[:, 1, :].rearrange("p (a t) -> p a t", a=2), ALU.mult))
                dve.tensor_tensor(x[0:ROT, 0:TT], t1, t2, ALU.add).then_inc(ok, 1)

            def own_a(h):
                first = isinstance(h, int) and h == 0
                yield from idle(9)
                rope_on(xq, s["q_rot"], h + 1, s["q_ok"])
                yield from idle(8)
                rope_on(xk, s["k_rot"], h + 1, s["k_ok"])
                yield from idle(9)
                for i in range(NC):
                    if i >= 2:
                        yield
                    p = probs[:, i * (i + 1) // 2 * P:(i + 1) * (i + 2) // 2 * P]
                    dve.wait_ge(s["scores"], NC * h + i + 1)
                    if i == 0 and not first:
                        dve.wait_ge(s["probT_ps"], 3 * h)
                    link(dve.scalar_tensor_tensor(p, MX[:, i, 0:(i + 1) * P], SCALE, lnmask[:, (NC - 1 - i) * P:TP],
                                                  ALU.mult, ALU.add))
                    link(dve.tensor_reduce(stat[:, 0, i:i + 1], p, AX.X, ALU.max))
                dve.tensor_scalar(stat[:, 0, :], stat[:, 0, :], -1.0, None, ALU.mult).then_inc(s["negmax"], 1)
                yield
                yield
                dve.wait_ge(s["expd"], NC * h + NC)
                link(dve.reciprocal(stat[:, 2, :], stat[:, 1, :]))
                for i in range(NC):
                    p = probs[:, i * (i + 1) // 2 * P:(i + 1) * (i + 2) // 2 * P]
                    dve.tensor_scalar(p, p, stat[:, 2, i:i + 1], None, ALU.mult).then_inc(s["probs_ok"], 1)

            def z_low():
                dve.tensor_scalar(ez[:], xz[:], X_LOW, None, ALU.max).then_inc(s["z_low"], 1)

            def tail_a(h):
                dve.wait_ge(s["proj_sb"], 8 * h + 2 * T_A + 8)
                z_low()
                yield from idle(2)
                dve.wait_ge(s["z_sig"], h + 1)
                dve.wait_ge(s["stash_v"], h + 1)
                dve.tensor_tensor(sz[:], xz[:], ez[:], ALU.mult).then_inc(s["z_ok"], 1)
                yield from idle(3)
                dve.wait_ge(s["z_ok"], h + 1)
                dve.wait_ge(s["attn_ps"], h + 1)
                dve.tensor_tensor(gated[:, h, 0:TP], MX[:, 3, :], sz[:, 0:TP], ALU.mult).then_inc(s["gated_a"], 1)

            def own_b(h):
                first = isinstance(h, int) and h == 0
                for j, m in enumerate((1, 2, 0)):
                    yield from idle((10, 2, 2)[j])
                    dve.wait_ge(s["proj_sb"], 8 * h + (2 * T_B + 2 * (j + 1)))
                    if j == 0:
                        dve.wait_ge(s["cw_ok"], h + 1)
                        if not first:
                            dve.wait_ge(s["q_silu"], h)
                    else:
                        dve.wait_ge(s["kv_silu"], 2 * h + j)
                    w = cw[:, m, :]
                    link(dve.tensor_scalar(acc[:, 0:TP], xq[:, 0:TP], w[:, 24:25], None, ALU.mult))
                    for i in range(1, CW):
                        link(dve.scalar_tensor_tensor(acc[:, 0:TP], xq[:, i:i + TP], w[:, 24 + i:25 + i],
                                                      acc[:, 0:TP], ALU.mult, ALU.add))
                        if i == (2, 2, 1)[j]:
                            yield
                    st = w[:, 0:24].rearrange("p (b i) -> p b i", i=3)
                    link(dve.tensor_scalar(acc[:, TP:TT], st[:, :, 0], w[:, 24:25], None, ALU.mult))
                    for i in range(1, CW):
                        src = st[:, :, i] if i < 3 else xq[:, 3 + TP:3 + TT]
                        ins = dve.scalar_tensor_tensor(acc[:, TP:TT], src, w[:, 24 + i:25 + i], acc[:, TP:TT],
                                                       ALU.mult, ALU.add)
                        link(ins)
                    dve.tensor_scalar(ez[:], acc[:], X_LOW, None, ALU.max).then_inc(s["conv_ok"], 1)
                    yield from idle((3, 5, 3)[j])
                    if j < 2:
                        dve.wait_ge(s["conv_sig"], 3 * h + j + 1)
                    if j < 2:
                        if j == 0 and not first:
                            dve.wait_ge(s["mix_qk"], h)
                        if j == 0 and first:
                            dve.wait_ge(s["scores"], NC * NH)
                            dve.wait_ge(s["stash_k"], NH)
                        if j == 1 and not first:
                            dve.wait_ge(s["mix_T1"], 2 * h)
                        if j == 1 and first:
                            dve.wait_ge(s["v_T"], NH)
                            dve.wait_ge(s["stash_v"], NH)
                        dve.tensor_tensor((xk, xv)[j][:], acc[:], ez[:], ALU.mult).then_inc(s["kv_silu"], 1)

            def bc(col):
                return col.unsqueeze(2).to_broadcast((P, NC, P))

            def mix_b(h):
                dve.wait_ge(s["conv_sig"], 3 * h + 3)
                dve.tensor_tensor(cq[:], acc[:], ez[:], ALU.mult).then_inc(s["q_silu"], 1)
                yield
                yield
                dve.wait_ge(s["hg_ok"], h + 1)
                dve.wait_ge(s["mix_rs"], h + 1)
                link(dve.tensor_scalar(sk[:, 1, :], sk[:, 1, :], SCALE, None, ALU.mult))
                dve.tensor_tensor(sk[:, 3, :], sk[:, 0, :], hg[:, 4, :], ALU.mult).then_inc(s["mix_scal"], 1)
                dve.tensor_tensor(sk[:, 2, :], sk[:, 0, :], hg[:, 0, :], ALU.mult).then_inc(s["mix_scal"], 1)
                dve.tensor_tensor(oq[:], sk[:, 1, :], hg[:, 3, :], ALU.mult).then_inc(s["mix_scal"], 1)
                dve.wait_ge(s["mix_scal"], 3 * h + 3)
                yield
                dve.wait_ge(s["mix_T1"], 2 * h + 2)
                dve.tensor_tensor(b_kb, mx(0), bc(sk[:, 2, :]), ALU.mult).then_inc(s["mix_tok"], 1)
                dve.tensor_tensor(b_kdec, mx(0), bc(sk[:, 3, :]), ALU.mult).then_inc(s["mix_tok"], 1)
                dve.tensor_tensor(b_vb, mx(1), bc(hg[:, 0, :]), ALU.mult).then_inc(s["mix_tok"], 1)
                dve.wait_ge(s["mix_gb"], h + 1)
                link(dve.tensor_tensor(b_D, mx(3), bc(hg[:, 1, :]), ALU.subtract))
                dve.scalar_tensor_tensor(b_D, b_D, 0.0, causal[:].unsqueeze(1).to_broadcast((P, NC, P)), ALU.min,
                                         ALU.add).then_inc(s["mix_arg"], 1)
                dve.wait_ge(s["proj_sb"], 8 * h + 2 * T_B + 8)
                z_low()
                yield
                yield
                dve.wait_ge(s["mix_D"], NC * h + NC)
                dve.wait_ge(s["mix_kk"], h + 1)
                dve.tensor_tensor(b_A, mx(1), b_D, ALU.mult).then_inc(s["mix_A"], 1)
                dve.memset(all_blocks(b_Y, 1, 1), 0.0)
                dve.wait_ge(s["mix_qk"], h + 1)
                dve.tensor_tensor(b_QK, mx(2), b_D, ALU.mult).then_inc(s["mix_QK"], 1)
                yield
                dve.wait_ge(s["z_sig_b"], h + 1)
                dve.tensor_tensor(sz[:], xz[:], ez[:], ALU.mult).then_inc(s["z_ok_b"], 1)
                yield
                for n in range(1, LEVELS):
                    yield
                    yield
                    z = (2 * LEVELS - 3) * h + 2 * (n - 1) + 1
                    dve.wait_ge(s["mix_Z"], z)
                    if n < LEVELS - 1:
                        dve.wait_ge(s["mix_Z"], z + 1)
                    u = all_blocks(b_U, n, 1)
                    dve.tensor_tensor(u, u, all_blocks(mx(2), n, 1), ALU.subtract).then_inc(s["mix_UT"], 1)
                    if n < LEVELS - 1:
                        t = all_blocks(b_T, n, 0)
                        dve.tensor_tensor(t, t, all_blocks(mx(3), n, 0), ALU.subtract).then_inc(s["mix_UT"], 1)
                        dve.memset(all_blocks(b_Y, n + 1, 1), 0.0).then_inc(s["mix_UT"], 1)
                for c in range(NC):
                    if c == 0:
                        dve.tensor_copy(rr, b_vb[:, 0, :]).then_inc(s["ch_r"], 1)
                    else:
                        yield
                        dve.wait_ge(s["ch_kS"], (NC - 1) * h + c)
                        dve.scalar_tensor_tensor(rr, MX[:, 0, 0:P], hg[:, 2, c:c + 1], b_vb[:, c, :], ALU.mult,
                                                 ALU.add).then_inc(s["ch_r"], 1)
                    yield
                    yield
                    dve.wait_ge(s["ch_S_ps"], NC * h + c + 1)
                    if c == 0:
                        dve.wait_ge(s["S_out"], 16 * h + 16)
                        dve.tensor_copy(S, MX[:, 0, 0:P]).then_inc(s["ch_S"], 1)
                    else:
                        dve.scalar_tensor_tensor(S, S, hg[:, 5, c:c + 1], MX[:, 0, 0:P], ALU.mult,
                                                 ALU.add).then_inc(s["ch_S"], 1)
                    dve.wait_ge(s["ch_o_ps"], (2 * NC - 1) * h + 2 * c + 1)
                    if c == 0:
                        dve.tensor_scalar(b_o[:, c, :], MX[:, 3, 0:P], sk[:, 1, c:c + 1], None, ALU.mult).then_inc(
                            s["ch_o"], 1)
                    else:
                        dve.wait_ge(s["ch_o1"], (NC - 1) * h + c)
                        dve.scalar_tensor_tensor(b_o[:, c, :], MX[:, 3, 0:P], sk[:, 1, c:c + 1], o1, ALU.mult,
                                                 ALU.add).then_inc(s["ch_o"], 1)
                dve.wait_ge(s["on_rs"], h + 1)
                dve.tensor_tensor(b_o, b_o, bc(on[:, 1, :]), ALU.mult).then_inc(s["o_n"], 1)
                yield
                dve.wait_ge(s["o_T"], h + 1)
                dve.wait_ge(s["z_ok_b"], h + 1)
                dve.scalar_tensor_tensor(gated[:, NH + h, 0:TP], MX[:, 0, :], vecT[:, KT:KT + 1], sz[:, 0:TP], ALU.mult,
                                         ALU.mult).then_inc(s["gated_b"], 1)

            def new_scores():
                dve.wait_ge(s["stash_k"], NH)
                dve.wait_ge(s["stash_q"], NH)
                dve.tensor_tensor(qks[:], qS[:], kS[:], ALU.mult).then_inc(s["qkp"], 1)
                yield
                dve.wait_ge(s["snew_ps"], 1)
                dve.tensor_scalar(snew[:], MD[0:NH, 0, 0:NB], SCALE, None, ALU.mult).then_inc(s["snew_ok"], 1)

            def delta_decode(h):
                kd, qd = xk[:, TP:TT], cq[:, TP:TT]
                yield
                dve.wait_ge(s["q_silu"], h + 1)
                dve.wait_ge(s["kv_silu"], 2 * h + 2)
                dve.tensor_copy(dd[:, 0, :], kd)
                dve.tensor_copy(dd[:, 1, :], qd)
                dve.tensor_tensor(dd[:, 2, :], kd, kd, ALU.mult)
                dve.tensor_tensor(dd[:, 3, :], qd, qd, ALU.mult)
                dve.tensor_copy(bt_s(0), bgs[:, 0, h, :])
                dve.tensor_copy(bt_s(1), bgs[:, 1, h, :])
                dve.tensor_tensor(dd[:, 4, :], kd, qd, ALU.mult).then_inc(s["dkq"], 1)
                yield
                yield
                dve.wait_ge(s["dkq"], h + 1)
                dve.wait_ge(s["d_sum"], h + 1)
                rk, rq = dd[:, 9, :], dd[:, 10, :]
                ks = MD[:, 1, 32:32 + 2 * NB].rearrange("p (b a) -> p a b", a=2)
                dve.wait_ge(s["d_rs"], h + 1)
                link(dve.tensor_scalar(rq, rq, SCALE, None, ALU.mult))
                dve.tensor_tensor(dd[:, 5, :], dd[:, 0, :], rk, ALU.mult)
                link(dve.tensor_tensor(dd[:, 6, :], ks[:, 0], rk, ALU.mult))
                link(dve.tensor_tensor(dd[:, 6, :], dd[:, 6, :], bt_s(1), ALU.mult))
                link(dve.tensor_tensor(dd[:, 6, :], xv[:, TP:TT], dd[:, 6, :], ALU.subtract))
                link(dve.tensor_tensor(dd[:, 6, :], dd[:, 6, :], bt_s(0), ALU.mult))
                link(dve.tensor_tensor(dd[:, 7, :], MD[:, 1, 2 * NB:3 * NB], rk, ALU.mult))
                link(dve.tensor_tensor(dd[:, 7, :], dd[:, 7, :], dd[:, 6, :], ALU.mult))
                link(dve.tensor_tensor(dd[:, 8, :], ks[:, 1], bt_s(1), ALU.mult))
                link(dve.tensor_tensor(dd[:, 7, :], dd[:, 7, :], dd[:, 8, :], ALU.add))
                link(dve.tensor_tensor(dd[:, 7, :], dd[:, 7, :], rq, ALU.mult))
                dve.tensor_tensor(dd[:, 8, :], dd[:, 7, :], dd[:, 7, :], ALU.mult).then_inc(s["d_vec"], 1)
                yield from idle(4)
                dve.wait_ge(s["d_rows"], h + 1)
                dve.wait_ge(s["z_ok_b"], h + 1)
                dve.wait_ge(s["d_rs2"], h + 1)
                link(dve.tensor_tensor(dd[:, 7, :], dd[:, 7, :], dd[:, 10, :], ALU.mult))
                dve.scalar_tensor_tensor(gated[:, NH + h, TP:TT], dd[:, 7, :], vecT[:, KT:KT + 1], sz[:, TP:TT], ALU.mult,
                                         ALU.mult).then_inc(s["gated_bd"], 1)
                for n in range(2):
                    yield from idle(n + 1)
                    dve.wait_ge(s["d_outer"], 2 * h + n + 1)
                    dve.wait_ge(s["S0_scaled"], h + 1)
                    st = S0[:, 4 * n:4 * n + 4, :]
                    dve.tensor_tensor(st, st, MD[:, 1, :].rearrange("p (b e) -> p b e", b=4), ALU.add).then_inc(
                        s["d_add"], 1)

            def bt_s(n):
                return dd[:, 12 - n, :]

            def attn_decode(b):
                for n in range(3):
                    yield from idle((8, 4, 3)[n])
                    dve.wait_ge(s["prod"], 6 * b + n + 1)
                    src = K_TILE[n]
                    dve.tensor_reduce(sc[:, n, :], src.rearrange("p (h d) -> p h d", h=NH), AX.X, ALU.add).then_inc(
                        s["red"], 1)
                yield
                yield
                dve.wait_ge(s["sc_T"], b + 1)
                link(dve.tensor_reduce(ds[:, 0:1], MD[0:NH, 0, 0:3 * P], AX.X, ALU.max))
                link(dve.tensor_copy(ds[:, 2:3], snew[:, bass.ds(b, 1)]))
                link(dve.scalar_tensor_tensor(ds[:, 0:1], ds[:, 0:1], SCALE, ds[:, 2:3], ALU.mult, ALU.max))
                link(dve.tensor_scalar(ds[:, 1:2], ds[:, 0:1], -1.0, None, ALU.mult))
                dve.tensor_tensor(ds[:, 2:3], ds[:, 2:3], ds[:, 0:1], ALU.subtract).then_inc(s["sc_max"], 1)
                yield from idle(3)
                dve.wait_ge(s["p_exp"], b + 1)
                link(dve.tensor_scalar(ds[:, 4:5], ds[:, 4:5], 3.0, None, ALU.mult))
                link(dve.tensor_tensor(ds[:, 5:6], ds[:, 3:4], ds[:, 4:5], ALU.add))
                link(dve.reciprocal(ds[:, 5:6], ds[:, 5:6]))
                link(dve.tensor_tensor(ds[:, 4:5], ds[:, 4:5], ds[:, 5:6], ALU.mult))
                dve.tensor_scalar(dg[:], ident[0:NH, 0:NH], ds[:, 4:5], None, ALU.mult)
                dve.tensor_scalar(pd, pd, ds[:, 5:6], None, ALU.mult).then_inc(s["p_norm"], 1)
                yield from idle(7)
                dve.wait_ge(s["prod"], 6 * b + 5)
                link(dve.tensor_tensor(V_TILE[0], V_TILE[0], V_TILE[1], ALU.add))
                yield from idle(1)
                dve.wait_ge(s["prod"], 6 * b + 6)
                dve.tensor_tensor(V_TILE[0], V_TILE[0], V_TILE[2], ALU.add).then_inc(s["pv_sum"], 1)
                yield from idle(2)
                dve.wait_ge(s["pT_ok"], b + 1)
                link(dve.tensor_tensor(da[:], vS[:, :, b], pT[:, 3, :], ALU.mult))
                dve.wait_ge(s["pv_ps"], b + 1)
                dve.wait_ge(s["stash_z"], NH)
                link(dve.tensor_tensor(da[:], MD[:, 0, 64:64 + NH], da[:], ALU.add))
                dve.tensor_tensor(gated[:, 0:NH, TP + b], da[:], zS[:, :, b], ALU.mult).then_inc(s["gated_ad"], 1)

            for q in (0, 2):
                lo(1, 1, q)
            dve.wait_ge(s["s_loaded"], 32)
            ga, first_a = gates(), own_a(0)
            head(T_A, [ga, first_a])
            ch.end(1)
            with dve.Fori(1, NH) as h:
                ch.at(h, 1, 13)
                head(4 * h + T_A, [tail_a(h - 1), own_a(h)])
            ch.end(NH - 1)
            head(T_B, [tail_a(NH - 1), new_scores(), attn_decode(0), own_b(0)])
            ch.end(1)
            with dve.Fori(1, NH) as h:
                ch.at(h, 1, 48)
                head(4 * h + T_B, [mix_b(h - 1), delta_decode(h - 1), attn_decode(h), own_b(h)])
            ch.end(NH - 1)

            def g_lo(k):
                dve.wait_ge(s["g_hi"], k + 1)
                dve.tensor_tensor(h_lo[:, k, :], gated[:, k, :], h_hi[:, k, :].bitcast(F32), ALU.subtract).then_inc(
                    s["g_lo"], 1)

            work = [mix_b(NH - 1), delta_decode(NH - 1)]
            for n in range(40):
                for g in work:
                    next(g, None)
                for k in splits(n):
                    g_lo(k)
                if n % 4 == 0 and n < 8 * PARTS:
                    slot = n // 8
                    lo(T_O + slot + 1, (T_O + slot + 1) % 2, n // 2 % 4)
            g_lo(KT - 1)
            link(dve.memset(acc[:], 0.0))
            ch.end(1)

            def y_half(j, half, part=False):
                tok = slice(half * HALF, (half + 1) * HALF)
                if part:
                    link(dve.tensor_tensor(sz[:, tok], PJ[:, half, 0:HALF], gated[:, j, tok], ALU.add))
                else:
                    link(dve.tensor_copy(sz[:, tok], PJ[:, half, 0:HALF]))
                dve.tensor_scalar(gated[:, j, tok], sz[:, tok], fin[:, 0:1], None, ALU.mult).then_inc(s["proj_sb"], 1)
                link(dve.tensor_tensor(ez[:, tok], sz[:, tok], sz[:, tok], ALU.mult))
                dve.tensor_tensor(acc[:, tok], acc[:, tok], ez[:, tok], ALU.add).then_inc(s["sq_y"], 1)

            def y_tile(T, j, par, split=True):
                link(dve.tensor_copy(fin[:, 0:1], vecT[:, bass.ds(j, 1)]))
                if split:
                    lo(T + 1, par, 0)
                    lo(T + 1, par, 2)
                for half in range(2):
                    dve.wait_ge(s["proj_ps"], 2 * T + half + 1)
                    y_half(j, half)

            dve.wait_ge(s["proj_sb"], 2 * T_O)
            y_tile(T_O + PARTS - 1, PARTS, 0, split=False)
            lo(T_O + PARTS + 1, 0, 0)
            lo(T_O + PARTS + 1, 0, 2)
            for j in range(PARTS):
                link(dve.tensor_copy(fin[:, 0:1], vecT[:, j:j + 1]))
                for half in range(2):
                    dve.wait_ge(s["part_sb"], 2 * j + half + 1)
                    if half == 0:
                        dve.wait_ge(s["rest_ps"], j + 1)
                    elif j < NQ - 1:
                        dve.wait_ge(s["w_used"], 3 * (T_O + PARTS) + j + 1)
                    else:
                        dve.wait_ge(s["proj_ps"], 2 * (T_O + PARTS) + 2)
                    y_half(j, half, part=True)
            ch.end(1)
            with dve.Fori(0, (KT - PARTS - 1) // 2) as i:
                ch.at(i, 0, 10)
                for n in range(2):
                    y_tile(2 * i + (T_O + PARTS + 1 + n), 2 * i + (PARTS + 1 + n), 1 - n)
            ch.end((KT - PARTS - 1) // 2)
            y_tile(T_O + KT - 1, KT - 1, 1, split=False)
            dve.wait_ge(s["sq_y"], 2 * KT)
            link(dve.memset(fin[:], 1.0))
            dve.wait_ge(s["ss_y"], 1)
            link(dve.tensor_copy(fin[:, 0:NC], MD[:, 0, 0:NC]))
            dve.tensor_copy(fin[0:NB, NC:NC + 1], MD[0:NB, 0, NC:NC + 1]).then_inc(s["fin_rs"], 1)
            dve.wait_ge(s["fin_rs"], 2)
            for c in range(NC + 1):
                n = P if c < NC else NB
                dve.wait_ge(x_in[c], 32 if c < NC else 48)
                for b in range(4):
                    x = xres[c][:, b * TP:(b + 1) * TP] if c < NC else xs_res[b // 2][:, b % 2 * TP:(b % 2 + 1) * TP]
                    dve.wait_ge(s["y_T"], 4 * c + b + 1)
                    dve.scalar_tensor_tensor(x, MX[0:n, b, :], fin[0:n, c:c + 1], x, ALU.mult, ALU.add).then_inc(
                        s["y_out_ok"], 1)

        @block.gpsimd
        def _(pool):
            def lo(T, par, q, n=P):
                pool.wait_ge(s["w_hi_ok"], 4 * T + q + 1)
                pool.tensor_tensor(w_lo[:, par, 4 * q:4 * q + 4, 0:n], w_raw[:, q, :, 0:n],
                                   w_hi[:, par, 4 * q:4 * q + 4, 0:n].bitcast(F32), ALU.subtract).then_inc(
                    s["w_lo_pool"], 1)

            def head(T, work):
                for j in range(4):
                    for seg in range(SEGS):
                        for g in work:
                            next(g, None)
                        if seg % 4 == 2:
                            lo(T + (j + 1), j % 2, seg // 2)

            def own_a(h):
                yield from idle(10)
                pool.wait_ge(s["q_ok"], h + 1)
                pool.tensor_copy(qS[:, h, :], xq[:, TP:TT]).then_inc(s["stash_q"], 1)
                yield from idle(8)
                pool.wait_ge(s["k_ok"], h + 1)
                pool.tensor_copy(kS[:, h, :], xk[:, TP:TT]).then_inc(s["stash_k"], 1)
                yield from idle(8)
                pool.wait_ge(s["proj_sb"], 8 * h + 2 * T_A + 6)
                pool.tensor_copy(vS[:, h, :], xv[:, TP:TT]).then_inc(s["stash_v"], 1)

            def tail_a(h):
                yield from idle(3)
                pool.wait_ge(s["z_ok"], h + 1)
                pool.tensor_copy(zS[:, h, :], sz[:, TP:TT]).then_inc(s["stash_z"], 1)

            def own_b(h):
                if isinstance(h, int) and h == 0:
                    pool.wait_ge(s["st_sb"], 2)
                else:
                    pool.wait_ge(s["conv_ok"], 3 * h)
                pool.tensor_copy(cw[:], stT[:].rearrange("p (m h) w -> p m h w", m=3)[:, :, h, :]).then_inc(
                    s["cw_ok"], 1)
                yield

            def mix_b(h):
                pool.wait_ge(s["q_silu"], h + 1)
                pool.tensor_copy(hg[:], G6[:, :, :, h]).then_inc(s["hg_ok"], 1)
                yield
                yield from idle(5)
                pool.wait_ge(s["mix_A"], h + 1)
                for n in range(LEVELS):
                    if n == 1:
                        pool.wait_ge(s["mix_QK"], h + 1)
                    if n == 2:
                        pool.wait_ge(s["mix_U0"], h + 1)
                    if n >= 3:
                        pool.wait_ge(s["mix_Y_ps"], (LEVELS - 1) * h + n - 2)
                    ins = pool.tensor_tensor(b_B[n % 2], b_A, levels[:, n, :].unsqueeze(1).to_broadcast((P, NC, P)),
                                             ALU.mult)
                    ins.then_inc(s["mix_B"], 1)
                    if n == 0:
                        pool.wait_ge(s["mix_B"], LEVELS * h + 1)
                        pool.tensor_tensor(b_U, ident[:].unsqueeze(1).to_broadcast((P, NC, P)), b_B[0],
                                           ALU.subtract).then_inc(s["mix_U0"], 1)
                    if n == 1:
                        yield
                    if n >= 1:
                        yield
                        yield

            def delta_decode(h):
                yield from idle(3)
                pool.wait_ge(s["d_sum"], h + 1)
                pool.tensor_tensor(S0[:], S0[:], dd[:, 11, :].unsqueeze(2).to_broadcast((P, NB, P)),
                                   ALU.mult).then_inc(s["S0_scaled"], 1)
                yield from idle(3)
                for n in range(2):
                    pool.wait_ge(s["d_rows_ok"], h + 1)
                    if n == 1:
                        pool.wait_ge(s["d_outer"], 2 * h + 1)
                    pool.tensor_tensor(vexp, kvr[:, 1, :].unsqueeze(1).to_broadcast((NB, 4, P)),
                                       ident[0:NB, 4 * n:4 * n + 4].unsqueeze(2).to_broadcast((NB, 4, P)),
                                       ALU.mult).then_inc(s["d_vexp"], 1)
                    yield
                    yield
                    yield

            def attn_decode(b):
                yield from idle(5)
                pool.wait_ge(s["qb_in"], 16 * b + 16)
                for n in range(3):
                    yield from idle((1, 5, 2)[n])
                    pool.wait_ge(s[f"kb{n}_in"], 16 * b + 16)
                    t = K_TILE[n]
                    pool.tensor_tensor(t, t, qb[:], ALU.mult).then_inc(s["prod"], 1)
                for n in range(3):
                    yield from idle((10, 1, 1)[n])
                    if n == 0:
                        pool.wait_ge(s["pT_ok"], b + 1)
                    pool.wait_ge(s[f"vb{n}_in"], 16 * b + 16)
                    v = V_TILE[n].rearrange("p (h d) -> p h d", h=NH)
                    pool.tensor_tensor(v, v, pT[:, n, :].unsqueeze(2).to_broadcast((P, NH, HD)), ALU.mult).then_inc(
                        s["prod"], 1)

            for q in (1, 3):
                pool.wait_ge(s["memset_ok"], 1)
                lo(0, 0, q, 16)
            for q in (1, 3):
                lo(1, 1, q)
            head(T_A, [own_a(0)])
            with pool.Fori(1, NH) as h:
                head(4 * h + T_A, [tail_a(h - 1), own_a(h)])
            pool.wait_ge(s["scores"], 4 * NH)
            pool.memset(xq[:, 0:3], 0.0).then_inc(s["zero_cols"], 1)
            head(T_B, [tail_a(NH - 1), own_b(0), attn_decode(0)])
            pool.wait_ge(s["gates_dve"], 5)
            pool.wait_ge(s["gates_act"], 4)
            pool.wait_ge(s["gated_a"], NH)
            pool.wait_ge(s["k_out"], 16 * NH)
            pool.wait_ge(s["v_out"], 32 * NH)
            with pool.Fori(1, NH) as h:
                head(4 * h + T_B, [mix_b(h - 1), own_b(h), delta_decode(h - 1), attn_decode(h)])
            work = [mix_b(NH - 1), delta_decode(NH - 1)]
            for n in range(40):
                for g in work:
                    next(g, None)
                if n % 4 == 2 and n < 8 * PARTS:
                    slot = n // 8
                    lo(T_O + slot + 1, (T_O + slot + 1) % 2, n // 2 % 4)
            for q in (1, 3):
                lo(T_O + PARTS + 1, 0, q)
            with pool.Fori(0, (KT - PARTS - 1) // 2) as i:
                for n in range(2):
                    for q in (1, 3):
                        lo(2 * i + (T_O + PARTS + 2 + n), 1 - n, q)


_INS = ["x_prompt", "x_sample", "cache_win_k", "cache_win_v", "state_conv", "state_delta", "g_pre", "w_in", "conv_w",
        "a_log", "dt_bias", "onorm_w", "w_out", "g_post"]
_CONST = ["c_ident", "c_upper", "c_causal", "c_levels", "c_lnmask", "c_rope", "c_rot"]
_OUTS = [(1, TP, D), (NB, 1, D), (1, 1, TP, NH, HD), (1, 1, TP, NH, HD), (1, 1, CW - 1, CONV_CH), (1, 1, NH, HD, HD),
         (1, NB, 1, NH, HD), (1, NB, 1, NH, HD), (1, NB, CW - 1, CONV_CH), (1, NB, NH, HD, HD)]


def kernel(**inputs):
    import concourse.bacc as bacc
    from concourse.bass_utils import run_bass_kernel_spmd

    nc = bacc.Bacc("TRN2", target_bir_lowering=False, num_devices=1)
    arrays, args = {}, []
    consts = tables()
    for name in _INS + _CONST:
        a = np.ascontiguousarray(inputs[name] if name in inputs else consts[name])
        arrays[f"in_{name}"] = a
        args.append(nc.dram_tensor(f"in_{name}", a.shape, mybir.dt.from_np(a.dtype), kind="ExternalInput").ap())
    for i, shape in enumerate(_OUTS):
        args.append(nc.dram_tensor(f"out_{i}", shape, F32, kind="ExternalOutput").ap())
    build(nc, *args)
    r = run_bass_kernel_spmd(nc, [arrays], core_ids=[0])
    return tuple(r.results[0][f"out_{i}"] for i in range(len(_OUTS)))
```
